# Optimizing a Trainium2 kernel written in Bass

```python
import jax, jax.numpy as jnp
from jax import lax
import numpy as np

D_MODEL = 1024
BATCH = 1
SEQ = 1024
DEPTH = 1

N_HEADS_ATTN = 8
N_KV_HEADS = 2
GQA_GROUP = N_HEADS_ATTN // N_KV_HEADS
HEAD_DIM = 64
D_ATTN = N_HEADS_ATTN * HEAD_DIM
D_KV = N_KV_HEADS * HEAD_DIM
N_CONV_GROUPS = 8
D_CONV = D_MODEL - D_ATTN
CONV_WIDTH = 3
CMP_BLOCK = 32
CMP_STRIDE = 16
CMP_HIDDEN = 2 * HEAD_DIM
SEL_BLOCK = 64
SEL_TOPK = 16
WINDOW = 512
Q_CHUNK = 64
D_FF = 2816
FFN_CONV_WIDTH = 3
EPS = 1e-6
NEG = -1e30
BIG = 1e30
PROJ_WIDTHS = [D_ATTN] + [D_KV] * 6 + [3 * N_HEADS_ATTN] + [D_CONV] * 3
W_IN_COLS = sum(PROJ_WIDTHS)

kernel_name = "hymba_nsa_shortconv_convffn"

def rmsnorm(x, g):
    xf = x.astype(jnp.float32)
    y = xf * lax.rsqrt(jnp.mean(xf * xf, axis=-1, keepdims=True) + EPS)
    return (y * g.astype(jnp.float32)).astype(x.dtype)

def causal_dwconv(u, w):
    T = u.shape[1]
    W = w.shape[0]
    up = jnp.pad(u, ((0, 0), (W - 1, 0), (0, 0)))
    y = w[0] * up[:, 0:T]
    for k in range(1, W):
        y = y + w[k] * up[:, k:k + T]
    return y

def alibi_slopes(n):
    return jnp.exp2(-8.0 * jnp.arange(1, n + 1, dtype=jnp.float32) / n)

def masked_softmax(s, mask):
    s = jnp.where(mask, s, NEG)
    p = jax.nn.softmax(s, axis=-1)
    return jnp.where(mask, p, 0.0)

def compress_blocks(k, pos, w1, w2):
    B, T, H, dk = k.shape
    n_cmp = (T - CMP_BLOCK) // CMP_STRIDE + 1
    idx = np.arange(n_cmp)[:, None] * CMP_STRIDE + np.arange(CMP_BLOCK)[None, :]
    blk = k[:, idx] + pos[None, None, :, None, :]
    blk = blk.transpose(0, 3, 1, 2, 4).reshape(B, H, n_cmp, CMP_BLOCK * dk)
    return jax.nn.gelu(blk @ w1) @ w2

def cmp_to_sel_map(T):
    n_cmp = (T - CMP_BLOCK) // CMP_STRIDE + 1
    n_sel = T // SEL_BLOCK
    cs = np.arange(n_cmp)[:, None] * CMP_STRIDE
    ss = np.arange(n_sel)[None, :] * SEL_BLOCK
    ov = np.maximum(0, np.minimum(cs + CMP_BLOCK, ss + SEL_BLOCK) - np.maximum(cs, ss))
    return jnp.asarray((ov / CMP_BLOCK).astype(np.float32))

def nsa_attention(q, k_cmp, v_cmp, k_slc, v_slc, k_win, v_win, gates):
    B, H, G, T, dk = q.shape
    n_cmp = k_cmp.shape[2]
    n_sel = T // SEL_BLOCK
    topk = min(SEL_TOPK, n_sel)
    scale = dk ** -0.5
    slopes5 = alibi_slopes(N_HEADS_ATTN).reshape(1, H, G, 1, 1)
    slopes6 = slopes5[..., None]
    cmp_end = jnp.arange(n_cmp) * CMP_STRIDE + (CMP_BLOCK - 1)
    m_sel = cmp_to_sel_map(T)
    k_blocks = k_slc.reshape(B, H, n_sel, SEL_BLOCK, dk)
    v_blocks = v_slc.reshape(B, H, n_sel, SEL_BLOCK, dk)
    k_win_p = jnp.pad(k_win, ((0, 0), (0, 0), (WINDOW, 0), (0, 0)))
    v_win_p = jnp.pad(v_win, ((0, 0), (0, 0), (WINDOW, 0), (0, 0)))
    b_idx = jnp.arange(B)[:, None, None, None]
    h_idx = jnp.arange(H)[None, :, None, None]
    sel_j = jnp.arange(n_sel)

    def chunk(q0):
        t = q0 + jnp.arange(Q_CHUNK)
        qc = lax.dynamic_slice_in_dim(q, q0, Q_CHUNK, axis=3) * scale
        gc = lax.dynamic_slice_in_dim(gates, q0, Q_CHUNK, axis=3)
        d_c = (t[:, None] - cmp_end[None, :]).astype(jnp.float32)
        s_c = jnp.einsum('bkgqd,bknd->bkgqn', qc, k_cmp).astype(jnp.float32) - slopes5 * d_c
        p_c = masked_softmax(s_c, d_c >= 0)
        o_c = jnp.einsum('bkgqn,bknd->bkgqd', p_c.astype(v_cmp.dtype), v_cmp)
        imp = jnp.einsum('bkgqn,nj->bkqj', p_c, m_sel)
        jt = t // SEL_BLOCK
        forced = (sel_j[None, :] == 0) | (sel_j[None, :] == jt[:, None]) | (sel_j[None, :] == jt[:, None] - 1)
        imp = jnp.where(forced, BIG, imp)
        imp = jnp.where(sel_j[None, :] > jt[:, None], NEG, imp)
        _, idx = lax.top_k(imp, topk)
        ks = k_blocks[b_idx, h_idx, idx]
        vs = v_blocks[b_idx, h_idx, idx]
        s_pos = idx[..., None] * SEL_BLOCK + jnp.arange(SEL_BLOCK)
        d_s = (t[None, None, :, None, None] - s_pos).astype(jnp.float32)[:, :, None]
        s_s = jnp.einsum('bkgqd,bkqnsd->bkgqns', qc, ks).astype(jnp.float32) - slopes6 * d_s
        n_tok = topk * SEL_BLOCK
        s_s = s_s.reshape(B, H, G, Q_CHUNK, n_tok)
        p_s = masked_softmax(s_s, (d_s >= 0).reshape(B, H, 1, Q_CHUNK, n_tok))
        o_s = jnp.einsum('bkgqm,bkqmd->bkgqd', p_s.astype(vs.dtype), vs.reshape(B, H, Q_CHUNK, n_tok, dk))
        kw = lax.dynamic_slice_in_dim(k_win_p, q0, Q_CHUNK + WINDOW, axis=2)
        vw = lax.dynamic_slice_in_dim(v_win_p, q0, Q_CHUNK + WINDOW, axis=2)
        w_pos = q0 - WINDOW + jnp.arange(Q_CHUNK + WINDOW)
        d_w = t[:, None] - w_pos[None, :]
        m_w = (d_w >= 0) & (d_w < WINDOW) & (w_pos[None, :] >= 0)
        s_w = jnp.einsum('bkgqd,bkmd->bkgqm', qc, kw).astype(jnp.float32) - slopes5 * d_w.astype(jnp.float32)
        p_w = masked_softmax(s_w, m_w)
        o_w = jnp.einsum('bkgqm,bkmd->bkgqd', p_w.astype(vw.dtype), vw)
        return gc[..., 0:1] * o_c + gc[..., 1:2] * o_s + gc[..., 2:3] * o_w

    starts = jnp.arange(T // Q_CHUNK) * Q_CHUNK
    outs = lax.map(chunk, starts)
    return outs.transpose(1, 0, 4, 2, 3, 5).reshape(B, T, H * G * dk)

def setup_inputs(seed: int = 0) -> dict:
    key = jax.random.key(seed)
    ks = jax.random.split(key, 24)
    nrm = lambda k, shape, s: jax.random.normal(k, shape, jnp.float32) * s
    gain = lambda k, shape: 1.0 + 0.02 * jax.random.normal(k, shape, jnp.float32)
    L = DEPTH
    return {
        "x": nrm(ks[0], (BATCH, SEQ, D_MODEL), 1.0),
        "norm_mix_g": gain(ks[1], (L, D_MODEL)),
        "w_in": nrm(ks[2], (L, D_MODEL, W_IN_COLS), D_MODEL ** -0.5),
        "pos_ck": nrm(ks[3], (L, CMP_BLOCK, HEAD_DIM), 0.1),
        "w_ck1": nrm(ks[4], (L, CMP_BLOCK * HEAD_DIM, CMP_HIDDEN), (CMP_BLOCK * HEAD_DIM) ** -0.5),
        "w_ck2": nrm(ks[5], (L, CMP_HIDDEN, HEAD_DIM), CMP_HIDDEN ** -0.5),
        "pos_cv": nrm(ks[6], (L, CMP_BLOCK, HEAD_DIM), 0.1),
        "w_cv1": nrm(ks[7], (L, CMP_BLOCK * HEAD_DIM, CMP_HIDDEN), (CMP_BLOCK * HEAD_DIM) ** -0.5),
        "w_cv2": nrm(ks[8], (L, CMP_HIDDEN, HEAD_DIM), CMP_HIDDEN ** -0.5),
        "conv_mix_w": nrm(ks[9], (L, CONV_WIDTH, D_CONV), CONV_WIDTH ** -0.5),
        "norm_out_attn_g": gain(ks[10], (L, D_ATTN)),
        "norm_out_conv_g": gain(ks[11], (L, D_CONV)),
        "w_out": nrm(ks[12], (L, D_ATTN + D_CONV, D_MODEL), (D_ATTN + D_CONV) ** -0.5),
        "norm_ffn_g": gain(ks[13], (L, D_MODEL)),
        "w_gate": nrm(ks[14], (L, D_MODEL, D_FF), D_MODEL ** -0.5),
        "w_up": nrm(ks[15], (L, D_MODEL, D_FF), D_MODEL ** -0.5),
        "ffn_conv_w": nrm(ks[16], (L, FFN_CONV_WIDTH, D_FF), FFN_CONV_WIDTH ** -0.5),
        "ffn_conv_b": nrm(ks[17], (L, D_FF), 0.01),
        "w_down": nrm(ks[18], (L, D_FF, D_MODEL), D_FF ** -0.5),
        "norm_final_g": gain(ks[19], (D_MODEL,)),
    }

def reference(x, norm_mix_g, w_in, pos_ck, w_ck1, w_ck2, pos_cv, w_cv1, w_cv2, conv_mix_w,
              norm_out_attn_g, norm_out_conv_g, w_out, norm_ffn_g, w_gate, w_up,
              ffn_conv_w, ffn_conv_b, w_down, norm_final_g):
    B, T, _ = x.shape
    split_at = [int(v) for v in np.cumsum(PROJ_WIDTHS)[:-1]]
    H, G, dk = N_KV_HEADS, GQA_GROUP, HEAD_DIM
    for l in range(DEPTH):
        h = rmsnorm(x, norm_mix_g[l])
        proj = h @ w_in[l]
        q, k_c, v_c, k_s, v_s, k_w, v_w, g_lin, b_g, c_g, u = jnp.split(proj, split_at, axis=-1)
        q = q.reshape(B, T, H, G, dk).transpose(0, 2, 3, 1, 4)
        kv_heads = lambda a: a.reshape(B, T, H, dk)
        k_cmp = compress_blocks(kv_heads(k_c), pos_ck[l], w_ck1[l], w_ck2[l])
        v_cmp = compress_blocks(kv_heads(v_c), pos_cv[l], w_cv1[l], w_cv2[l])
        to_bhtd = lambda a: kv_heads(a).transpose(0, 2, 1, 3)
        gates = jax.nn.sigmoid(g_lin).reshape(B, T, H, G, 3).transpose(0, 2, 3, 1, 4)
        o_attn = nsa_attention(q, k_cmp, v_cmp, to_bhtd(k_s), to_bhtd(v_s),
                               to_bhtd(k_w), to_bhtd(v_w), gates)
        o_conv = b_g * causal_dwconv(c_g * u, conv_mix_w[l])
        mixed = jnp.concatenate([rmsnorm(o_attn, norm_out_attn_g[l]),
                                 rmsnorm(o_conv, norm_out_conv_g[l])], axis=-1)
        x = x + mixed @ w_out[l]
        h2 = rmsnorm(x, norm_ffn_g[l])
        gate = causal_dwconv(h2 @ w_gate[l], ffn_conv_w[l]) + ffn_conv_b[l]
        x = x + (jax.nn.silu(gate) * (h2 @ w_up[l])) @ w_down[l]
    return rmsnorm(x, norm_final_g)


_drawn_inputs = setup_inputs


def setup_inputs(seed=0):
    import zlib

    import numpy as np

    out = dict(_drawn_inputs(seed))
    spreads = {}
    factors = {'pos_ck': 8.0,
     'norm_out_attn_g': 14.555,
     'norm_out_conv_g': 14.884,
     'norm_ffn_g': 4.824,
     'ffn_conv_b': 28.11,
     'norm_final_g': 8.034}
    for name, (base, spread) in spreads.items():
        noise = np.random.default_rng([zlib.crc32(name.encode()), seed]).standard_normal(out[name].shape)
        drawn = base * np.exp(spread * noise) if base else spread * noise
        out[name] = __import__('jax').numpy.asarray(drawn.astype(out[name].dtype))
    for name, factor in factors.items():
        out[name] = (out[name] * factor).astype(out[name].dtype)
    return out
```

```python
import numpy as np
import concourse.bass as bass
from concourse import mybir
from contextlib import ExitStack

F32 = mybir.dt.float32
F32R = mybir.dt.float32r
BF16 = mybir.dt.bfloat16
ALU = mybir.AluOpType
ACT = mybir.ActivationFunctionType
AX = mybir.AxisListType

P = 128
D = 1024
T = 1024
KT = D // P
TT = T // P
BANK = 512
HALVES = T // BANK
HEADS, KV, DH = 8, 2, 64
GROUP = HEADS // KV
DFF = 2816
FT = DFF // P
CMP_BLOCK, CMP_STRIDE = 32, 16
NCMP = (T - CMP_BLOCK) // CMP_STRIDE + 1
CW = 64
WINDOW = 512
WT = WINDOW // P
SEL_BLOCK, SEL_TOPK = 64, 16
assert T // SEL_BLOCK <= SEL_TOPK
CONV_T = 4
EPS = 1e-6
NEG = -1e30
AR = 10

N_CONV = 3 * CONV_T
N_QKV = HEADS * DH // P + 3 * KV + 1
N_IN = N_CONV + N_QKV
N_OUT = D // P
OUT0 = N_IN
FFN0 = OUT0 + N_OUT
N_UNITS = FFN0 + 3 * FT
RING = 3

P_GMIX, P_GOUT, P_GFFN, P_GFIN = 0, 8, 16, 24
P_CONV = 32
P_FCW = P_CONV + 3 * CONV_T
P_FCB = P_FCW + 3 * FT
P_POSK = P_FCB + FT
P_POSV = P_POSK + CMP_BLOCK // 2
NPAR = P_POSV + CMP_BLOCK // 2
C_ID, C_ONE, C_VALID = 0, P, 2 * P
NCON = 2 * P + TT
M_ID, M_DIAG, M_EDGE, M_CMP = 0, P, 2 * P, 3 * P
NMASK = 3 * P + TT * CW


class Steps:

    def __init__(self, eng, sem):
        self.eng, self.sem, self.base, self.local, self.stack = eng, sem, 0, 0, []

    def add(self, ins):
        ins.then_inc(self.sem, 1)
        self.local += 1

    def settle(self):
        self.eng.wait_ge(self.sem, self.base + self.local)

    def enter(self, i, trips, per):
        start = self.base + self.local
        self.stack.append((start, trips, per))
        self.base, self.local = start + per * i, 0

    def leave(self):
        start, trips, per = self.stack.pop()
        assert self.local == per, (self.local, per)
        self.base, self.local = start, per * trips


def tiles_of_block(i):
    sel = [("sel", j, j * P) for j in range(i + 1)]
    win = [("win", j, (j - max(0, i - WT)) * P) for j in range(max(0, i - WT), i + 1)]
    near = win + [("cmp", 0, (WT + 1) * P)]
    cut = lambda x: [x[c:c + 4] for c in range(0, len(x), 4)]
    return cut(sel), cut(near)


def hybrid_layer(nc, xT, w_units, w_cmp1, w_cmp2, params_d, consts_d, masks_d, alibi_q, alibi_k, outT):
    with ExitStack() as ctx:
        def sb(name, shape, dt=F32):
            return ctx.enter_context(nc.sbuf_tensor(name, shape, dt))

        def sem(name):
            return ctx.enter_context(nc.semaphore(name))

        params = sb("params", [P, NPAR])
        consts = sb("consts", [P, NCON])
        masks = sb("masks", [P, NMASK], BF16)
        w2c = sb("w2c", [P, 2, DH])
        raw = sb("raw", [P, RING, 1024])
        wh = sb("wh", [P, RING, 1024], F32R)
        wl = sb("wl", [P, RING, 1024], F32R)
        F1 = sb("F1", [P, 15, 1024])
        R1 = sb("R1", [P, 16, 1024], F32R)
        R2 = sb("R2", [P, 8, 1024], F32R)
        PBm = sb("PBm", [P, 2, 768])
        small = sb("small", [P, 64])
        gates = sb("gates", [P, TT, 3 * HEADS])
        rsum = sb("rsum", [P, 2, 4])
        nmax = sb("nmax", [P, 2, 4])
        coef = sb("coef", [P, 2, 8])
        hidc = sb("hidc", [P, 2, CW])
        posb = sb("posb", [P, 2])
        otmp = sb("otmp", [P, 2, DH])
        PS = ctx.enter_context(nc.psum_tensor("PS", [P, 8, BANK], F32))

        def par(c, n=1):
            return params[:, c:c + n] if isinstance(c, int) else params[:, bass.ds(c, n)]

        ident = consts[:, C_ID:C_ID + P]
        ones = consts[:, C_ONE:C_ONE + P]

        def pair(p):
            return PS[:, 2 * p:2 * p + 2, :].rearrange("p a b -> p (a b)")

        Q0, GATE, KV0, Y0, X1 = 0, 4, 5, 11, 5
        U_S, CU_S, CT_S, SQ_S, ACCY = 5, 6, 7, 8, 9
        QA = [R1[:, 0, :], R1[:, 1, :]]
        QB = [R1[:, 2, :], R1[:, 3, :]]
        NK = 2 * T + CW
        KA = R1[:, 4:7, :].rearrange("p a b -> p (a b)")[:, 0:NK]
        KB = R1[:, 7:10, :].rearrange("p a b -> p (a b)")[:, 0:NK]
        VH, VL = R1[:, 10, :], R1[:, 11, :]
        VHC, VLC = R1[:, 6, 128:192], R1[:, 6, 192:256]
        PTH = [R1[:, 12, 0:512], R1[:, 12, 512:1024]]
        PTL = [R1[:, 13, 0:512], R1[:, 13, 512:1024]]
        PA = [raw[:, 1, :], raw[:, 2, :]]
        PB = [PBm[:, 0, :], PBm[:, 1, :]]
        RB = PBm[:, :, :].rearrange("p a b -> p (a b)")[:, 0:1024]
        CK, CV = raw[:, 1, :], raw[:, 2, :]
        W1C = F1[:, Y0:Y0 + 4, :].rearrange("p a b -> p (a b)").rearrange("p (k l h) -> p k l h", k=2, l=16)

        def f32(ap):
            return ap.bitcast(F32)

        consts_in, late_in, w1_in, ak_in = sem("consts_in"), sem("late_in"), sem("w1_in"), sem("ak_in")
        masks_in = sem("masks_in")
        x_in, aq_in = [sem(f"x_in{k}") for k in range(KT)], [sem(f"aq_in{e}") for e in range(2)]
        x1_in, out_done = sem("x1_in"), sem("out_done")
        unit_in = [sem(f"unit_in{s}") for s in range(RING)]
        unit_hi, unit_lo, unit_done = sem("unit_hi"), sem("unit_lo"), sem("unit_done")
        dve_step = sem("dve_step")
        sq_ready, acc_ready = sem("sq_ready"), sem("acc_ready")
        ss_ready, ss_read, rt_ready, diag_ready, rb_ready = (sem("ss_ready"), sem("ss_read"), sem("rt_ready"),
                                                             sem("diag_ready"), sem("rb_ready"))
        h_ready, h_hi_ready, h_lo_ready = sem("h_ready"), sem("h_hi_ready"), sem("h_lo_ready")
        v_copied, pad_ready, clear_ready, acc_clear = sem("v_copied"), sem("pad_ready"), sem("clear_ready"), sem("acc_clear")
        u_ready, cu_ready, tap_ready, y_ready, ysq_ready, accy_ready = (
            sem("u_ready"), sem("cu_ready"), sem("tap_ready"), sem("y_ready"), sem("ysq_ready"), sem("accy_ready"))
        yn_ready, mc_hi, mc_lo = sem("yn_ready"), sem("mc_hi"), sem("mc_lo")
        qkv_ready = sem("qkv_ready")
        gt_ready, gexp_ready, gates_ready = sem("gt_ready"), sem("gexp_ready"), sem("gates_ready")
        pos_ready, posb_ready = sem("pos_ready"), sem("posb_ready")
        ck_ready, hid_ready, gelu_ready, kvc_ready = sem("ck_ready"), sem("hid_ready"), sem("gelu_ready"), sem("kvc_ready")
        vt_ready, v_hi, v_lo, k_hi, k_lo, kc_hi, kc_lo = (sem("vt_ready"), sem("v_hi"), sem("v_lo"), sem("k_hi"),
                                                        sem("k_lo"), sem("kc_hi"), sem("kc_lo"))
        q_hi, q_lo = sem("q_hi"), sem("q_lo")
        sa_ready, sb_ready, max_a, max_b, pa_ready, pb_ready = (sem("sa_ready"), sem("sb_ready"), sem("max_a"),
                                                                sem("max_b"), sem("pa_ready"), sem("pb_ready"))
        tp_ready, pt_hi, pt_lo, pv_done, o_used = (sem("tp_ready"), sem("pt_hi"), sem("pt_lo"), sem("pv_done"),
                                                   sem("o_used"))
        osq_ready, on_ready, ot_ready, ma_hi, ma_lo = (sem("osq_ready"), sem("on_ready"), sem("ot_ready"),
                                                       sem("ma_hi"), sem("ma_lo"))
        x1_ready, x1sq_ready, acc1_ready = sem("x1_ready"), sem("x1sq_ready"), sem("acc1_ready")
        g_tap, taps_ready, silu_ready, a_ready, a_hi, a_lo = (sem("g_tap"), sem("taps_ready"), sem("silu_ready"),
                                                              sem("a_ready"), sem("a_hi"), sem("a_lo"))
        down_done, down_added = sem("down_done"), sem("down_added")
        x2sq_ready, acc2_ready, og_ready, out_ready = (sem("x2sq_ready"), sem("acc2_ready"), sem("og_ready"),
                                                       sem("out_ready"))

        def at(base, coef, i, k):
            return (base + k) % RING, (base + k) // RING + (coef // RING) * i + 1, base + k + coef * i

        def norm_sums(acc):
            for t in range(TT):
                last = nc.tensor.matmul(PS[:, 6, t:t + 1], acc[:, t * P:(t + 1) * P], ones[:, 0:1],
                                        start=True, stop=True)
            last.then_inc(ss_ready, 1)

        def norm_spread(pe, m):
            pe.wait_ge(diag_ready, m + 1)
            for h in range(HALVES):
                last = nc.tensor.matmul(PS[:, 6 + h, :], ones, RB[:, h * BANK:(h + 1) * BANK],
                                        start=True, stop=True)
            last.then_inc(rb_ready, 1)

        def norm_act(act, m):
            act.wait_ge(ss_read, m + 1 + (m > 1))
            nc.scalar.activation(small[:, 8:16], small[:, 0:8], ACT.Sqrt).then_inc(rt_ready, 1)

        def norm_dve(dve, steps, m, width):
            dve.wait_ge(ss_ready, m + 1)
            nc.vector.tensor_scalar(small[:, 0:8], PS[:, 6, 0:8], 1.0 / width, EPS, ALU.mult, ALU.add)\
                .then_inc(ss_read, 1)
            dve.wait_ge(rt_ready, m + 1 + (m > 1))
            newton(steps)
            nc.vector.tensor_tensor(RB.rearrange("p (t q) -> p t q", t=TT),
                                    ident.rearrange("p (o q) -> p o q", o=1).broadcast_to([P, TT, P]),
                                    small[:, 24:32].rearrange("p (t o) -> p t o", o=1).broadcast_to([P, TT, P]),
                                    ALU.mult).then_inc(diag_ready, 1)

        def newton(steps):
            v, root, r, rr, vrr, f, out = (small[:, c:c + 8] for c in (0, 8, 16, 32, 40, 48, 24))
            for ins in (lambda: nc.vector.reciprocal(r, root),
                        lambda: nc.vector.tensor_tensor(rr, r, r, ALU.mult),
                        lambda: nc.vector.tensor_tensor(vrr, rr, v, ALU.mult),
                        lambda: nc.vector.tensor_scalar(f, vrr, -0.5, 1.5, ALU.mult, ALU.add),
                        lambda: nc.vector.tensor_tensor(out, f, r, ALU.mult)):
                steps.add(ins())
                steps.settle()

        def load(sp, base, coef, i, k):
            slot, held, n = at(base, coef, i, k)
            sp.wait_ge(unit_lo, n - RING + 1)
            src = w_units[n] if isinstance(n, int) else w_units[bass.ds(n, 1), :, :].rearrange("o p n -> (o p) n")
            sp.dma_start(raw[:, slot, :], src).then_inc(unit_in[slot], 16)

        def split_hi(act, base, coef, i, k, free=False):
            slot, held, n = at(base, coef, i, k)
            act.wait_ge(unit_in[slot], 16 * held)
            if not free and (not isinstance(n, int) or n >= RING):
                act.wait_ge(unit_done, n - RING + 1)
            nc.scalar.activation(wh[:, slot, :], raw[:, slot, :], ACT.Copy).then_inc(unit_hi, 1)

        def split_lo(dve, base, coef, i, k, free=False):
            slot, held, n = at(base, coef, i, k)
            dve.wait_ge(unit_hi, n + 1)
            if not free and (not isinstance(n, int) or n >= RING):
                dve.wait_ge(unit_done, n - RING + 1)
            nc.vector.tensor_tensor(wl[:, slot, :], raw[:, slot, :], f32(wh[:, slot, :]), ALU.subtract)\
                .then_inc(unit_lo, 1)

        def unit_matmuls(pe, base, coef, i, k, p, hi, lo, order=range(KT), arrives=None):
            slot, held, n = at(base, coef, i, k)
            pe.wait_ge(unit_lo, n + 1)
            for kt in order:
                if arrives:
                    arrives(kt)
                w_h, w_l = wh[:, slot, kt * P:(kt + 1) * P], wl[:, slot, kt * P:(kt + 1) * P]
                first, end = kt == order[0], kt == order[-1]
                for h in range(HALVES):
                    out, cols = PS[:, 2 * p + h, :], slice(h * BANK, (h + 1) * BANK)
                    nc.tensor.matmul(out, w_h, hi(kt)[:, cols], start=first, stop=False)
                    nc.tensor.matmul(out, w_h, lo(kt)[:, cols], start=False, stop=False)
                for h in range(HALVES):
                    out, cols = PS[:, 2 * p + h, :], slice(h * BANK, (h + 1) * BANK)
                    last = nc.tensor.matmul(out, w_l, hi(kt)[:, cols], start=False, stop=end)
            last.then_inc(unit_done, 1)

        h_hi, h_lo = (lambda k: R1[:, k, :]), (lambda k: R1[:, 8 + k, :])
        m_hi = lambda k: R1[:, k, :] if k < 4 else R2[:, k - 4, :]
        m_lo = lambda k: R1[:, 4 + k, :] if k < 4 else R2[:, k, :]

        BLOCKS = [(e, i) for e in range(2) for i in range(TT)]
        NB = len(BLOCKS)
        CHUNKS = []
        for b, (e, i) in enumerate(BLOCKS):
            for u, cs in enumerate(tiles_of_block(i)):
                CHUNKS += [(b, u, c) for c in cs]
        NC = len(CHUNKS)
        assert NC % 2 == 0

        LAST = [max(c for c in range(NC) if CHUNKS[c][0] == b and CHUNKS[c][1] == u) + 1
                for b in range(NB) for u in range(2)]

        def act_at(par, e, part):
            return R2[:, 4 * par + 2 * e + part, :]

        T1 = [F1[:, 0, :], F1[:, 1, :]]
        SA = [F1[:, 2, :], F1[:, 3, :]]
        ACC = F1[:, 4, :]
        SQ = [F1[:, 13, :], F1[:, 14, :]]
        DOWN_PAIRS = [0, 1, 0, 1, 2, 3, 2, 3]

        block = ctx.enter_context(nc.Block())

        @block.sync
        def _(sp):
            sp.dma_start(F1[:, 0, :], xT[0]).then_inc(x_in[0], 16)
            sp.dma_start(consts[:, :], consts_d).then_inc(consts_in, 16)
            sp.dma_start(params[:, :], params_d).then_inc(consts_in, 16)
            for k in range(1, KT):
                sp.dma_start(F1[:, k, :], xT[k]).then_inc(x_in[k], 16)
            for n in range(RING):
                sp.dma_start(raw[:, n, :], w_units[n]).then_inc(unit_in[n], 16)
            sp.dma_start(w2c[:, :, :], w_cmp2).then_inc(late_in, 16)
            with sp.Fori(0, 4) as i:
                for k in range(3):
                    load(sp, 3, 3, i, k)
            with sp.Fori(0, 3) as i:
                for k in range(3):
                    load(sp, 15, 3, i, k)
            sp.wait_ge(mc_lo, CONV_T)
            sp.dma_start(F1[:, Y0:Y0 + 4, :], w_cmp1).then_inc(w1_in, 16)
            load(sp, 24, 0, 0, 0)
            sp.wait_ge(k_hi, 4 * KV)
            sp.wait_ge(k_lo, 2 * KV)
            sp.wait_ge(v_copied, KV)
            sp.wait_ge(ck_ready, 4 * KV)
            sp.wait_ge(hid_ready, 2 * KV)
            for k in range(KT):
                sp.dma_start(F1[:, X1 + k, :], xT[k]).then_inc(x1_in, 16)
            sp.wait_ge(tp_ready, 4 * NC)
            load(sp, 25, 0, 0, 0)
            load(sp, 26, 0, 0, 0)
            with sp.Fori(0, (N_UNITS - 28) // 3) as i:
                for k in range(3):
                    load(sp, 27, 3, i, k)
            load(sp, N_UNITS - 1, 0, 0, 0)
            for k in range(KT):
                sp.wait_ge(out_ready, k + 1)
                sp.dma_start(outT[k], F1[:, X1 + k, :]).then_inc(out_done, 16)
            sp.wait_ge(out_done, 16 * KT)

        @block.gpsimd
        def _(pool):
            pool.dma_start(masks[:, :], masks_d).then_inc(masks_in, 16)
            for k in range(KT):
                pool.wait_ge(h_hi_ready, k + 1)
                nc.gpsimd.tensor_tensor(h_lo(k), F1[:, k, :], f32(h_hi(k)), ALU.subtract).then_inc(h_lo_ready, 1)
            pool.wait_ge(ss_ready, 1)
            nc.gpsimd.memset(F1[:, ACCY, :], 0.0).then_inc(acc_clear, 1)
            pool.wait_ge(unit_done, N_IN)
            for pad in (KA[:, 2 * T:], KB[0:DH, 2 * T:], VHC, VLC):
                nc.gpsimd.memset(f32(pad), 0.0).then_inc(clear_ready, 1)
            pool.dma_start(KB[DH:DH + AR, :], alibi_k).then_inc(ak_in, 16)
            pool.wait_ge(qkv_ready, N_QKV)
            pool.wait_ge(unit_lo, N_IN + 2)
            pool.wait_ge(rb_ready, 2)
            with pool.Fori(0, KV) as g:
                slot = lambda what: bass.ds(KV0 + 3 * g + what, 1)
                nc.gpsimd.tensor_copy(RB, F1[:, slot(1), :].rearrange("p o t -> p (o t)")).then_inc(v_copied, 1)
                pool.wait_ge(v_copied, g + 1)
                for half, dst in ((0, CK), (1, CV)):
                    src = F1[half * DH:(half + 1) * DH, slot(2), :].rearrange("p o t -> p (o t)")
                    nc.gpsimd.tensor_copy(dst[0:DH, :], src).then_inc(ck_ready, 1)
                    pool.wait_ge(ck_ready, 4 * g + 2 * half + 1)
                    nc.gpsimd.tensor_copy(dst[DH:P, 0:T - 1], src[:, 1:T]).then_inc(ck_ready, 1)
                    if half == 0:
                        pool.wait_ge(ck_ready, 4 * g + 2)
                with pool.Fori(0, 2) as jj:
                    q = 2 * g + jj
                    pool.wait_ge(ck_ready, 4 * g + 4)
                    for e in range(2):
                        pool.dma_start(QB[e][DH:DH + AR, :], alibi_q[bass.ds(2 * q + e, 1)]
                                       .rearrange("o p n -> (o p) n")).then_inc(aq_in[e], 16)
                    pool.wait_ge(sb_ready, NB * q + NB)
                    pool.wait_ge(tp_ready, NC * q + NC)
            pool.wait_ge(gt_ready, 1)
            nc.gpsimd.memset(ACC, 0.0).then_inc(acc_clear, 1)
            for k in range(KT):
                pool.wait_ge(h_hi_ready, KT + k + 1)
                nc.gpsimd.tensor_tensor(h_lo(k), F1[:, k % 2, :], f32(h_hi(k)), ALU.subtract).then_inc(h_lo_ready, 1)
            nc.gpsimd.memset(ACC, 0.0).then_inc(acc_clear, 1)

        @block.scalar
        def _(act):
            for k in range(KT):
                act.wait_ge(x_in[k], 16)
                if k > 2:
                    act.wait_ge(acc_ready, k - 2)
                dst = F1[:, 10, :] if k == 0 else F1[:, 8 + k % 2, :]
                nc.scalar.activation(dst, F1[:, k, :], ACT.Square).then_inc(sq_ready, 1)
            norm_act(act, 0)
            split_hi(act, 0, 0, 0, 0)
            for k in range(KT):
                act.wait_ge(h_ready, k + 1)
                nc.scalar.activation(h_hi(k), F1[:, k, :], ACT.Copy).then_inc(h_hi_ready, 1)
            split_hi(act, 1, 0, 0, 0)
            act.wait_ge(h_lo_ready, KT)
            with act.Fori(0, CONV_T) as i:
                split_hi(act, 2, 3, i, 0, free=True)
                act.wait_ge(unit_done, 3 * i + 1)
                nc.scalar.activation(F1[:, U_S, :], pair(0), ACT.Copy).then_inc(u_ready, 1)
                split_hi(act, 3, 3, i, 0)
                act.wait_ge(cu_ready, i + 1)
                nc.scalar.activation(F1[:, CT_S, :], F1[:, CU_S, :], ACT.Copy, scale=par(P_CONV + 3 * i + 2))\
                    .then_inc(tap_ready, 1)
                split_hi(act, 4, 3, i, 0)
                act.wait_ge(y_ready, i + 1)
                nc.scalar.activation(F1[:, SQ_S, :], F1[:, bass.ds(Y0 + i, 1), :].rearrange("p o t -> p (o t)"),
                                     ACT.Square).then_inc(ysq_ready, 1)

            def evac(base, coef, i, k, slot):
                _, _, n = at(base, coef, i, k)
                act.wait_ge(unit_done, n + 1)
                nc.scalar.activation(slot, pair(n_pair(base + k)), ACT.Copy).then_inc(qkv_ready, 1)

            n_pair = lambda n: n % 3
            split_hi(act, 14, 0, 0, 0)
            evac(12, 0, 0, 0, F1[:, 0, :])
            norm_act(act, 1)
            split_hi(act, 15, 0, 0, 0)
            evac(13, 0, 0, 0, F1[:, 1, :])
            for k in range(CONV_T):
                act.wait_ge(yn_ready, k + 1)
                nc.scalar.activation(R2[:, k, :], F1[:, Y0 + k, :], ACT.Copy).then_inc(mc_hi, 1)
            with act.Fori(0, 3) as i:
                for k in range(3):
                    split_hi(act, 16, 3, i, k)
                    evac(14, 3, i, k, F1[:, bass.ds(3 * i + k + 2, 1), :].rearrange("p o t -> p (o t)"))
            act.wait_ge(gt_ready, 1)
            nc.scalar.activation(gates[:, :, :], PS[:, 4:6, :].rearrange("p a (b c) -> p (a b) c", c=P)[:, :, 0:3 * HEADS],
                                 ACT.Exp, scale=-1.0).then_inc(gexp_ready, 1)
            act.wait_ge(pos_ready, 1)
            nc.scalar.activation(posb[:, :], PS[:, 6, 0:2], ACT.Copy).then_inc(posb_ready, 1)
            act.wait_ge(clear_ready, 4)
            act.wait_ge(posb_ready, 1)
            with act.Fori(0, KV) as g:
                for half in range(2):
                    src = F1[half * DH:(half + 1) * DH, bass.ds(KV0 + 3 * g, 1), :].rearrange("p o t -> p (o t)")
                    for rows in (slice(0, DH), slice(DH, P)):
                        nc.scalar.activation(KA[rows, half * T:(half + 1) * T], src, ACT.Copy).then_inc(k_hi, 1)
                act.wait_ge(vt_ready, g + 1)
                nc.scalar.activation(VH, pair(2), ACT.Copy).then_inc(v_hi, 1)
                for kv in range(2):
                    act.wait_ge(hid_ready, 2 * g + kv + 1)
                    nc.scalar.activation(hidc[:, kv, 0:NCMP], PS[:, 6 + kv, 0:NCMP], ACT.Gelu_apprx_tanh,
                                         bias=posb[:, kv:kv + 1]).then_inc(gelu_ready, 1)
                act.wait_ge(kvc_ready, 2 * g + 1)
                for rows in (slice(0, DH), slice(DH, P)):
                    nc.scalar.activation(KA[rows, 2 * T:2 * T + NCMP], PS[0:DH, 6, P:P + NCMP], ACT.Copy)\
                        .then_inc(kc_hi, 1)
                act.wait_ge(kvc_ready, 2 * g + 2)
                nc.scalar.activation(VHC[0:NCMP, :], PS[0:NCMP, 7, P:P + DH], ACT.Copy).then_inc(kc_hi, 1)
                with act.Fori(0, 2) as jj:
                    q = 2 * g + jj
                    for e in range(2):
                        rows = slice(e * DH, (e + 1) * DH)
                        src = F1[rows, bass.ds(Q0 + q, 1), :].rearrange("p o t -> p (o t)")
                        nc.scalar.activation(QA[e][rows, :], src, ACT.Copy, scale=DH ** -0.5).then_inc(q_hi, 1)
                        nc.scalar.activation(QB[e][0:DH, :], src, ACT.Copy, scale=DH ** -0.5).then_inc(q_hi, 1)

                    def probs_a(b):
                        nk = P * (BLOCKS[b][1] + 1)
                        act.wait_ge(max_a, NB * q + b + 1)
                        if b > 1:
                            act.wait_ge(tp_ready, NC * q + LAST[2 * (b - 2)])
                        nc.scalar.activation(PA[b % 2][:, 0:nk], pair(0)[:, 0:nk], ACT.Exp, bias=nmax[:, b % 2, 0:1],
                                             accum_out=rsum[:, b % 2, 0:1]).then_inc(pa_ready, 1)

                    def probs_b(b):
                        nk = P * min(BLOCKS[b][1] + 1, WT + 1)
                        c0 = (WT + 1) * P
                        act.wait_ge(max_b, 2 * (NB * q + b) + 2)
                        if b > 1:
                            act.wait_ge(tp_ready, NC * q + LAST[2 * (b - 2) + 1])
                        nc.scalar.activation(PB[b % 2][:, 0:nk], pair(1)[:, 0:nk], ACT.Exp, bias=nmax[:, b % 2, 1:2],
                                             accum_out=rsum[:, b % 2, 1:2])
                        nc.scalar.activation(PB[b % 2][:, c0:c0 + CW], pair(1)[:, c0:c0 + CW], ACT.Exp,
                                             bias=nmax[:, b % 2, 2:3], accum_out=rsum[:, b % 2, 2:3]).then_inc(pb_ready, 1)

                    def turned(c):
                        w = P * len(CHUNKS[c][2])
                        act.wait_ge(tp_ready, NC * q + c + 1)
                        nc.scalar.activation(PTH[c % 2][:, 0:w], PS[:, 4 + c % 2, 0:w], ACT.Copy).then_inc(pt_hi, 1)

                    probs_a(0)
                    probs_b(0)
                    for b in range(NB):
                        for u, probs in ((0, probs_a), (1, probs_b)):
                            for c in range(NC):
                                if CHUNKS[c][0] == b and CHUNKS[c][1] == u:
                                    turned(c)
                            if b + 1 < NB:
                                probs(b + 1)
            act.wait_ge(o_used, 4 * NB)
            for t in range(TT):
                nc.scalar.activation(PS[:, t, :].rearrange("p (a b) -> p a b", a=4), F1[:, 0:4, t * P:(t + 1) * P],
                                     ACT.Square, accum_out=small[:, 56 + t:57 + t]).then_inc(osq_ready, 1)
            act.wait_ge(ss_read, 3)
            nc.scalar.activation(small[:, 8:16], small[:, 0:8], ACT.Sqrt).then_inc(rt_ready, 1)
            for k in range(4):
                act.wait_ge(ot_ready, k + 1)
                nc.scalar.activation(m_hi(k), pair(k), ACT.Copy, scale=par(P_GOUT + k)).then_inc(ma_hi, 1)

            def residual_square(base, coef, i, k):
                split_hi(act, base + 2, coef, i, k)
                _, _, n = at(base, coef, i, k)
                d = n - OUT0
                act.wait_ge(x1_ready, d + 1)
                if not isinstance(d, int) or d:
                    act.wait_ge(acc1_ready, d)
                nc.scalar.activation(SQ[0], F1[:, bass.ds(X1 + d, 1), :].rearrange("p o t -> p (o t)"), ACT.Square)\
                    .then_inc(x1sq_ready, 1)

            residual_square(OUT0, 0, 0, 0)
            residual_square(OUT0 + 1, 0, 0, 0)
            with act.Fori(0, 2) as i:
                for k in range(3):
                    residual_square(OUT0 + 2, 3, i, k)
            norm_act(act, 2)
            for k in range(KT):
                act.wait_ge(h_ready, KT + k + 1)
                nc.scalar.activation(h_hi(k), F1[:, k % 2, :], ACT.Copy).then_inc(h_hi_ready, 1)

            def gated(base, coef, i, k, e, f, par_pair, down):
                _, _, n = at(base, coef, i, k)
                split_hi(act, base + 2, coef, i, k)
                act.wait_ge(unit_done, n + 1)
                nc.scalar.activation(T1[e], pair(2 * e), ACT.Identity, scale=par(P_FCW + 3 * f + 2), bias=par(P_FCB + f))\
                    .then_inc(g_tap, 1)
                split_hi(act, base + 2, coef, i, k + 1)
                act.wait_ge(taps_ready, f + 1)
                if not isinstance(f, int) or f > 1:
                    act.wait_ge(a_lo, f - 1)
                nc.scalar.activation(SA[e], T1[e], ACT.Silu).then_inc(silu_ready, 1)
                act.wait_ge(a_ready, f + 1)
                if down is not None:
                    act.wait_ge(unit_done, down)
                nc.scalar.activation(act_at(par_pair, e, 0), SA[e], ACT.Copy).then_inc(a_hi, 1)

            for e in range(2):
                gated(FFN0, 0, 0, 2 * e, e, e, 0, None)
            with act.Fori(0, 5) as i:
                for s in range(2):
                    base = FFN0 + 4 + 6 * s
                    for e in range(2):
                        gated(base, 12, i, 2 * e, e, 4 * i + 2 * s + 2 + e, (s + 1) % 2, base + 12 * i)
                    split_hi(act, base + 2, 12, i, 4)
                    split_hi(act, base + 2, 12, i, 5)
            for k in range(KT):
                act.wait_ge(down_added, 10 * KT + k + 1)
                if k > 1:
                    act.wait_ge(acc2_ready, k - 1)
                nc.scalar.activation(SQ[k % 2], F1[:, X1 + k, :], ACT.Square).then_inc(x2sq_ready, 1)
            norm_act(act, 3)

        @block.vector
        def _(dve):
            steps = Steps(dve, dve_step)
            for k in range(1, KT):
                dve.wait_ge(sq_ready, k + 1)
                if k > 1:
                    dve.wait_ge(acc_ready, k - 1)
                nc.vector.tensor_tensor(F1[:, 10, :], F1[:, 10, :], F1[:, 8 + k % 2, :], ALU.add).then_inc(acc_ready, 1)
            dve.wait_ge(consts_in, 32)
            norm_dve(dve, steps, 0, D)
            split_lo(dve, 0, 0, 0, 0)
            dve.wait_ge(rb_ready, 1)
            for k in range(KT):
                nc.vector.scalar_tensor_tensor(F1[:, k, :], F1[:, k, :], par(P_GMIX + k), pair(3), ALU.mult, ALU.mult)\
                    .then_inc(h_ready, 1)
            split_lo(dve, 1, 0, 0, 0)
            dve.wait_ge(acc_clear, 1)
            with dve.Fori(0, CONV_T) as i:
                steps.enter(i, CONV_T, 2)
                y = F1[:, bass.ds(Y0 + i, 1), :].rearrange("p o t -> p (o t)")
                cu, tap = F1[:, CU_S, :], F1[:, CT_S, :]
                split_lo(dve, 2, 3, i, 0, free=True)
                dve.wait_ge(u_ready, i + 1)
                dve.wait_ge(unit_done, 3 * i + 2)
                nc.vector.tensor_tensor(cu, pair(1), F1[:, U_S, :], ALU.mult).then_inc(cu_ready, 1)
                split_lo(dve, 3, 3, i, 0)
                dve.wait_ge(tap_ready, i + 1)
                dve.wait_ge(cu_ready, i + 1)
                for lag in (1, 2):
                    steps.add(nc.vector.scalar_tensor_tensor(tap[:, lag:], cu[:, 0:T - lag], par(P_CONV + 3 * i + 2 - lag),
                                                             tap[:, lag:], ALU.mult, ALU.add))
                    steps.settle()
                split_lo(dve, 4, 3, i, 0)
                dve.wait_ge(unit_done, 3 * i + 3)
                nc.vector.tensor_tensor(y, pair(2), tap, ALU.mult).then_inc(y_ready, 1)
                dve.wait_ge(ysq_ready, i + 1)
                nc.vector.tensor_tensor(F1[:, ACCY, :], F1[:, ACCY, :], F1[:, SQ_S, :], ALU.add).then_inc(accy_ready, 1)
                steps.leave()
            split_lo(dve, 14, 0, 0, 0)
            norm_dve(dve, steps, 1, CONV_T * P)
            split_lo(dve, 15, 0, 0, 0)
            dve.wait_ge(rb_ready, 2)
            for k in range(CONV_T):
                nc.vector.scalar_tensor_tensor(F1[:, Y0 + k, :], F1[:, Y0 + k, :], par(P_GOUT + 4 + k), pair(3),
                                               ALU.mult, ALU.mult).then_inc(yn_ready, 1)
            for k in range(CONV_T):
                dve.wait_ge(mc_hi, k + 1)
                nc.vector.tensor_tensor(R2[:, 4 + k, :], F1[:, Y0 + k, :], f32(R2[:, k, :]), ALU.subtract)\
                    .then_inc(mc_lo, 1)
            with dve.Fori(0, 3) as i:
                for k in range(3):
                    split_lo(dve, 16, 3, i, k)
            dve.wait_ge(gexp_ready, 1)
            steps.add(nc.vector.tensor_scalar_add(gates[:, :, :], gates[:, :, :], 1.0))
            steps.settle()
            steps.add(nc.vector.reciprocal(gates[:, :, :], gates[:, :, :]))
            steps.settle()
            g3 = gates[:, :, :].rearrange("p t (h b) -> p t h b", b=3)[:, :, :, 2]
            steps.add(nc.vector.tensor_tensor(g3, g3, consts[:, C_VALID:C_VALID + TT].rearrange("p (t o) -> p t o", o=1)
                                              .broadcast_to([P, TT, HEADS]), ALU.mult))
            steps.settle()
            with dve.Fori(0, KV) as g:
                steps.enter(g, KV, 2 * 4 * NB)
                for half in range(2):
                    rows = slice(half * DH, (half + 1) * DH)
                    dve.wait_ge(k_hi, 4 * g + 2 * half + 2)
                    nc.vector.tensor_tensor(KB[0:DH, half * T:(half + 1) * T],
                                            F1[rows, bass.ds(KV0 + 3 * g, 1), :].rearrange("p o t -> p (o t)"),
                                            f32(KA[rows, half * T:(half + 1) * T]), ALU.subtract).then_inc(k_lo, 1)
                dve.wait_ge(v_hi, g + 1)
                nc.vector.tensor_tensor(VL, pair(2), f32(VH), ALU.subtract).then_inc(v_lo, 1)
                for buf in PB:
                    nc.vector.memset(buf[:, (WT + 1) * P + CW:], 0.0).then_inc(pad_ready, 1)
                dve.wait_ge(kc_hi, 3 * g + 2)
                nc.vector.tensor_tensor(KB[0:DH, 2 * T:2 * T + NCMP], PS[0:DH, 6, P:P + NCMP],
                                        f32(KA[0:DH, 2 * T:2 * T + NCMP]), ALU.subtract).then_inc(kc_lo, 1)
                dve.wait_ge(kc_hi, 3 * g + 3)
                nc.vector.tensor_tensor(VLC[0:NCMP, :], PS[0:NCMP, 7, P:P + DH], f32(VHC[0:NCMP, :]), ALU.subtract)\
                    .then_inc(kc_lo, 1)
                with dve.Fori(0, 2) as jj:
                    steps.enter(jj, 2, 4 * NB)
                    q = 2 * g + jj
                    for e in range(2):
                        rows, other = slice(e * DH, (e + 1) * DH), slice((1 - e) * DH, (2 - e) * DH)
                        dve.wait_ge(q_hi, 4 * q + 2 * e + 1)
                        nc.vector.scalar_tensor_tensor(QA[e][other, :],
                                                       F1[rows, bass.ds(Q0 + q, 1), :].rearrange("p o t -> p (o t)"),
                                                       DH ** -0.5, f32(QA[e][rows, :]), ALU.mult, ALU.subtract)\
                            .then_inc(q_lo, 1)

                    def max_of(b, col, unit, cols, count, signal):
                        nc.vector.tensor_reduce(nmax[:, b % 2, col:col + 1], pair(unit)[:, cols:cols + count], AX.X,
                                                ALU.max, negate=True).then_inc(signal, 1)

                    def maxes_a(b):
                        dve.wait_ge(sa_ready, NB * q + b + 1)
                        max_of(b, 0, 0, 0, P * (BLOCKS[b][1] + 1), max_a)

                    def maxes_b(b):
                        dve.wait_ge(sb_ready, NB * q + b + 1)
                        max_of(b, 1, 1, 0, P * min(BLOCKS[b][1] + 1, WT + 1), max_b)
                        max_of(b, 2, 1, (WT + 1) * P, CW, max_b)

                    def turned_low(c):
                        w = P * len(CHUNKS[c][2])
                        dve.wait_ge(pt_hi, NC * q + c + 1)
                        nc.vector.tensor_tensor(PTL[c % 2][:, 0:w], PS[:, 4 + c % 2, 0:w], f32(PTH[c % 2][:, 0:w]),
                                                ALU.subtract).then_inc(pt_lo, 1)

                    def combine(b):
                        e, i = BLOCKS[b]
                        k = coef[:, b % 2, :]
                        steps.add(nc.vector.reciprocal(k[:, 0:3], rsum[:, b % 2, 0:3]))
                        steps.settle()
                        steps.add(nc.vector.tensor_tensor(k[:, 4:7], k[:, 0:3], gates[:, i, bass.ds(6 * q + 3 * e, 3)],
                                                          ALU.mult))
                        steps.settle()
                        dve.wait_ge(pv_done, NC * q + LAST[2 * b + 1])
                        O = PS[:, 6 + b % 2, :]
                        steps.add(nc.vector.tensor_scalar(otmp[:, b % 2, :], O[:, 0:DH], k[:, 4:5], None, ALU.mult))
                        steps.settle()
                        steps.add(nc.vector.scalar_tensor_tensor(otmp[:, b % 2, :], O[:, DH:2 * DH], k[:, 5:6],
                                                                 otmp[:, b % 2, :], ALU.mult, ALU.add))
                        steps.settle()
                        dst = F1[:, bass.ds(Q0 + q, 1), i * P + e * DH:i * P + (e + 1) * DH]\
                            .rearrange("p o t -> p (o t)")
                        nc.vector.scalar_tensor_tensor(dst, O[:, 2 * DH:3 * DH], k[:, 6:7], otmp[:, b % 2, :],
                                                       ALU.mult, ALU.add).then_inc(o_used, 1)

                    dve.wait_ge(q_hi, 4 * q + 4)
                    maxes_a(0)
                    maxes_b(0)
                    for b in range(NB):
                        for u, maxes in ((0, maxes_a), (1, maxes_b)):
                            for c in range(NC):
                                if CHUNKS[c][0] == b and CHUNKS[c][1] == u:
                                    turned_low(c)
                            if b + 1 < NB:
                                maxes(b + 1)
                        combine(b)
                    steps.leave()
                steps.leave()
            dve.wait_ge(osq_ready, TT)
            nc.vector.tensor_scalar(small[:, 0:8], small[:, 56:64], 1.0 / (HEADS * DH), EPS, ALU.mult, ALU.add)\
                .then_inc(ss_read, 1)
            dve.wait_ge(rt_ready, 3)
            newton(steps)
            for t in range(TT):
                o = F1[:, 0:4, t * P:(t + 1) * P]
                nc.vector.tensor_scalar(o, o, small[:, 24 + t:25 + t], None, ALU.mult).then_inc(on_ready, 1)
            for k in range(4):
                dve.wait_ge(ma_hi, k + 1)
                nc.vector.scalar_tensor_tensor(m_lo(k), pair(k), par(P_GOUT + k), f32(m_hi(k)), ALU.mult, ALU.subtract)\
                    .then_inc(ma_lo, 1)
            dve.wait_ge(x1_in, 16 * KT)
            dve.wait_ge(acc_clear, 2)

            def residual(base, coef, i, k):
                split_lo(dve, base + 2, coef, i, k)
                _, _, n = at(base, coef, i, k)
                d = n - OUT0
                dve.wait_ge(unit_done, n + 1)
                x1 = F1[:, bass.ds(X1 + d, 1), :].rearrange("p o t -> p (o t)")
                nc.vector.tensor_tensor(x1, pair((base + k) % 3), x1, ALU.add).then_inc(x1_ready, 1)
                dve.wait_ge(x1sq_ready, d + 1)
                if not isinstance(d, int) or d:
                    dve.wait_ge(acc1_ready, d)
                nc.vector.tensor_tensor(ACC, ACC, SQ[0], ALU.add).then_inc(acc1_ready, 1)

            residual(OUT0, 0, 0, 0)
            residual(OUT0 + 1, 0, 0, 0)
            with dve.Fori(0, 2) as i:
                for k in range(3):
                    residual(OUT0 + 2, 3, i, k)
            norm_dve(dve, steps, 2, D)
            dve.wait_ge(rb_ready, 3)
            for k in range(KT):
                if k > 1:
                    dve.wait_ge(h_lo_ready, KT + k - 1)
                nc.vector.scalar_tensor_tensor(F1[:, k % 2, :], F1[:, X1 + k, :], par(P_GFFN + k), pair(3),
                                               ALU.mult, ALU.mult).then_inc(h_ready, 1)

            def gated(base, coef, i, k, e, f, par_pair):
                _, _, n = at(base, coef, i, k)
                split_lo(dve, base + 2, coef, i, k)
                dve.wait_ge(g_tap, f + 1)
                gate = pair(2 * e)
                steps.add(nc.vector.scalar_tensor_tensor(T1[e][:, 1:], gate[:, 0:T - 1], par(P_FCW + 3 * f + 1),
                                                         T1[e][:, 1:], ALU.mult, ALU.add))
                steps.settle()
                nc.vector.scalar_tensor_tensor(T1[e][:, 2:], gate[:, 0:T - 2], par(P_FCW + 3 * f), T1[e][:, 2:],
                                               ALU.mult, ALU.add).then_inc(taps_ready, 1)
                split_lo(dve, base + 2, coef, i, k + 1)
                dve.wait_ge(unit_done, n + 2)
                dve.wait_ge(silu_ready, f + 1)
                nc.vector.tensor_tensor(SA[e], SA[e], pair(2 * e + 1), ALU.mult).then_inc(a_ready, 1)
                dve.wait_ge(a_hi, f + 1)
                nc.vector.tensor_tensor(act_at(par_pair, e, 1), SA[e], f32(act_at(par_pair, e, 0)), ALU.subtract)\
                    .then_inc(a_lo, 1)

            def add_down(d, counted, n):
                if d < KT - 1:
                    dve.wait_ge(down_done, counted + d + 1)
                else:
                    dve.wait_ge(unit_done, n)
                x1 = F1[:, X1 + d, :]
                nc.vector.tensor_tensor(x1, pair(DOWN_PAIRS[d]), x1, ALU.add).then_inc(down_added, 1)

            for e in range(2):
                gated(FFN0, 0, 0, 2 * e, e, e, 0)
            with dve.Fori(0, 5) as i:
                steps.enter(i, 5, 4)
                for s in range(2):
                    base = FFN0 + 4 + 6 * s
                    for e in range(2):
                        gated(base, 12, i, 2 * e, e, 4 * i + 2 * s + 2 + e, (s + 1) % 2)
                    split_lo(dve, base + 2, 12, i, 4)
                    for d in range(KT):
                        add_down(d, (KT - 1) * (2 * i + s), base + 12 * i + 6)
                    split_lo(dve, base + 2, 12, i, 5)
                steps.leave()
            dve.wait_ge(acc_clear, 3)
            for d in range(KT + 1):
                if d < KT:
                    add_down(d, (KT - 1) * 10, N_UNITS)
                if d:
                    dve.wait_ge(x2sq_ready, d)
                    if d > 1:
                        dve.wait_ge(acc2_ready, d - 1)
                    nc.vector.tensor_tensor(ACC, ACC, SQ[(d - 1) % 2], ALU.add).then_inc(acc2_ready, 1)
            norm_dve(dve, steps, 3, D)
            dve.wait_ge(rb_ready, 4)
            for k in range(KT):
                nc.vector.scalar_tensor_tensor(F1[:, X1 + k, :], F1[:, X1 + k, :], par(P_GFIN + k), pair(3),
                                               ALU.mult, ALU.mult).then_inc(out_ready, 1)

        @block.tensor
        def _(pe):
            pe.wait_ge(consts_in, 32)
            pe.wait_ge(acc_ready, KT - 1)
            norm_sums(F1[:, 10, :])
            norm_spread(pe, 0)
            arrives = lambda kt: pe.wait_ge(h_lo_ready, kt + 1)
            with pe.Fori(0, CONV_T) as i:
                unit_matmuls(pe, 0, 3, i, 0, 0, h_hi, h_lo, arrives=arrives)
                unit_matmuls(pe, 1, 3, i, 0, 1, h_hi, h_lo)
                unit_matmuls(pe, 2, 3, i, 0, 2, h_hi, h_lo)
            pe.wait_ge(u_ready, CONV_T)
            unit_matmuls(pe, 12, 0, 0, 0, 0, h_hi, h_lo)
            pe.wait_ge(accy_ready, CONV_T)
            norm_sums(F1[:, ACCY, :])
            pe.wait_ge(cu_ready, CONV_T)
            unit_matmuls(pe, 13, 0, 0, 0, 1, h_hi, h_lo)
            norm_spread(pe, 1)
            pe.wait_ge(y_ready, CONV_T)
            with pe.Fori(0, 3) as i:
                for k in range(3):
                    unit_matmuls(pe, 14, 3, i, k, (14 + k) % 3, h_hi, h_lo)
            pe.wait_ge(qkv_ready, N_QKV)
            for t in range(TT):
                last = nc.tensor.transpose(PS[:, 4 + t // 4, (t % 4) * P:(t % 4 + 1) * P], F1[:, GATE, t * P:(t + 1) * P],
                                           ident)
            last.then_inc(gt_ready, 1)
            pe.wait_ge(w1_in, 16)
            pe.wait_ge(late_in, 16)
            pe.wait_ge(masks_in, 16)
            pe.wait_ge(mc_lo, CONV_T)
            for kv in range(2):
                for l in range(CMP_BLOCK // 2):
                    c = (P_POSK, P_POSV)[kv] + l
                    last = nc.tensor.matmul(PS[:, 6, kv:kv + 1], W1C[:, kv, l, :], params[:, c:c + 1], start=l == 0,
                                            stop=l == CMP_BLOCK // 2 - 1)
            last.then_inc(pos_ready, 1)
            pe.wait_ge(gexp_ready, 1)
            pe.wait_ge(posb_ready, 1)
            pe.wait_ge(ak_in, 16)
            with pe.Fori(0, KV) as g:
                pe.wait_ge(v_copied, g + 1)
                for t in range(TT):
                    last = nc.tensor.transpose(PS[:, 4 + t // 4, (t % 4) * P:(t % 4 + 1) * P], RB[:, t * P:(t + 1) * P],
                                               ident)
                last.then_inc(vt_ready, 1)
                for kv, src in ((0, CK), (1, CV)):
                    pe.wait_ge(ck_ready, 4 * g + 2 * kv + 2)
                    for l in range(CMP_BLOCK // 2):
                        last = nc.tensor.matmul(PS[:, 6 + kv, 0:NCMP], W1C[:, kv, l, :],
                                                src[:, 2 * l:2 * l + CMP_STRIDE * (NCMP - 1) + 1:CMP_STRIDE],
                                                start=l == 0, stop=l == CMP_BLOCK // 2 - 1)
                    last.then_inc(hid_ready, 1)
                pe.wait_ge(gelu_ready, 2 * g + 1)
                nc.tensor.matmul(PS[0:DH, 6, P:P + NCMP], w2c[:, 0, :], hidc[:, 0, 0:NCMP], start=True, stop=True)\
                    .then_inc(kvc_ready, 1)
                pe.wait_ge(gelu_ready, 2 * g + 2)
                nc.tensor.matmul(PS[0:NCMP, 7, P:P + DH], hidc[:, 1, 0:NCMP], w2c[:, 1, :], start=True, stop=True)\
                    .then_inc(kvc_ready, 1)
                with pe.Fori(0, 2) as jj:
                    q = 2 * g + jj
                    pe.wait_ge(k_lo, 2 * g + 2)
                    pe.wait_ge(kc_lo, 2 * g + 2)
                    pe.wait_ge(v_lo, g + 1)
                    pe.wait_ge(pad_ready, 2 * g + 2)
                    for e in range(2):
                        pe.wait_ge(q_lo, 2 * q + e + 1)
                        pe.wait_ge(aq_in[e], 16 * q + 16)
                    pe.wait_ge(q_hi, 4 * q + 4)

                    def scores(out, e, i, key, count, masked):
                        rows = slice(i * P, (i + 1) * P)
                        nc.tensor.matmul(out[:, 0:count], QA[e][:, rows], KA[:, key:key + count], start=True, stop=False)
                        last = nc.tensor.matmul(out[:, 0:count], QB[e][0:DH + AR, rows], KB[0:DH + AR, key:key + count],
                                                start=False, stop=not masked)
                        for n, (col, m, w) in enumerate(masked):
                            last = nc.tensor.matmul(out[:, col:col + w], masks[:, M_ID:M_ID + P], masks[:, m:m + w],
                                                    start=False, stop=n == len(masked) - 1)
                        return last

                    def scores_a(b):
                        e, i = BLOCKS[b]
                        if b:
                            pe.wait_ge(pa_ready, NB * q + b)
                        for c in range(0, i + 1, 4):
                            n = min(4, i + 1 - c)
                            last = scores(PS[:, c // 4, :], e, i, c * P, n * P,
                                          [((n - 1) * P, M_DIAG, P)] if c + n == i + 1 else [])
                        last.then_inc(sa_ready, 1)

                    def scores_b(b):
                        e, i = BLOCKS[b]
                        if b:
                            pe.wait_ge(pb_ready, NB * q + b)
                        j0 = max(0, i - WT)
                        for c in range(0, i + 1 - j0, 4):
                            n = min(4, i + 1 - j0 - c)
                            masked = [((n - 1) * P, M_DIAG, P)] if j0 + c + n == i + 1 else []
                            if i >= WT and c == 0:
                                masked = [(0, M_EDGE, P)] + masked
                            scores(PS[:, 2 + c // 4, :], e, i, T + (j0 + c) * P, n * P, masked)
                        scores(PS[:, 3, P:P + CW], e, i, 2 * T, CW, [(0, M_CMP + i * CW, CW)]).then_inc(sb_ready, 1)

                    def turn(c):
                        b, u, tiles = CHUNKS[c]
                        if c > 1:
                            pe.wait_ge(pt_lo, NC * q + c - 1)
                        pe.wait_ge((pa_ready, pb_ready)[u], NB * q + b + 1)
                        for m, (_, _, col) in enumerate(tiles):
                            last = nc.tensor.transpose(PS[:, 4 + c % 2, m * P:(m + 1) * P],
                                                       (PA, PB)[u][b % 2][:, col:col + P], ident)
                        last.then_inc(tp_ready, 1)

                    def values(c):
                        b, u, tiles = CHUNKS[c]
                        i = BLOCKS[b][1]
                        pe.wait_ge(pt_lo, NC * q + c + 1)
                        for m, (branch, j, _) in enumerate(tiles):
                            n = ("sel", "win", "cmp").index(branch)
                            first = j == (max(0, i - WT) if branch == "win" else 0)
                            end = branch == "cmp" or j == i
                            v_h, v_l = ((VHC, VLC) if branch == "cmp" else
                                        (x[:, j * P + n * DH:j * P + (n + 1) * DH] for x in (VH, VL)))
                            out = PS[:, 6 + b % 2, n * DH:(n + 1) * DH]
                            t_h, t_l = PTH[c % 2][:, m * P:(m + 1) * P], PTL[c % 2][:, m * P:(m + 1) * P]
                            nc.tensor.matmul(out, t_h, v_h, start=first, stop=False)
                            nc.tensor.matmul(out, t_h, v_l, start=False, stop=False)
                            last = nc.tensor.matmul(out, t_l, v_h, start=False, stop=end)
                        last.then_inc(pv_done, 1)

                    scores_a(0)
                    scores_b(0)
                    for c in range(NC):
                        b, u, _ = CHUNKS[c]
                        if (c == 0 or CHUNKS[c - 1][:2] != (b, u)) and b + 1 < NB:
                            (scores_a, scores_b)[u](b + 1)
                        turn(c)
                        if c:
                            values(c - 1)
                    values(NC - 1)
                    pe.wait_ge(o_used, NB * q + NB)
            pe.wait_ge(o_used, 4 * NB)
            for k in range(4):
                pe.wait_ge(on_ready, TT)
                for t in range(TT):
                    last = nc.tensor.transpose(PS[:, 2 * k + t // 4, (t % 4) * P:(t % 4 + 1) * P],
                                               F1[:, k, t * P:(t + 1) * P], ident)
                last.then_inc(ot_ready, 1)
            order = [4, 5, 6, 7, 0, 1, 2, 3]
            pe.wait_ge(ma_lo, 4)
            unit_matmuls(pe, OUT0, 0, 0, 0, OUT0 % 3, m_hi, m_lo, order)
            unit_matmuls(pe, OUT0 + 1, 0, 0, 0, (OUT0 + 1) % 3, m_hi, m_lo, order)
            with pe.Fori(0, 2) as i:
                for k in range(3):
                    unit_matmuls(pe, OUT0 + 2, 3, i, k, (OUT0 + 2 + k) % 3, m_hi, m_lo, order)
            pe.wait_ge(acc1_ready, N_OUT)
            norm_sums(ACC)
            norm_spread(pe, 2)
            arrives = lambda kt: pe.wait_ge(h_lo_ready, KT + kt + 1)
            pe.wait_ge(x1_ready, N_OUT)
            for k in range(4):
                unit_matmuls(pe, FFN0, 0, 0, k, k, h_hi, h_lo, arrives=arrives if k == 0 else None)

            def down(base, coef, i, k, par_pair, pairs_read, counted, before):
                units = [at(base, coef, i, k + a) for a in range(2)]
                pe.wait_ge(unit_lo, units[1][2] + 1)
                for d in range(KT):
                    p = DOWN_PAIRS[d]
                    if d in (0, 4):
                        pe.wait_ge(a_ready, pairs_read[d // 4])
                    if d in (2, 3, 6, 7):
                        pe.wait_ge(down_added, before + d - 1)
                    for a in range(2):
                        w_h, w_l = (w[:, units[a][0], d * P:(d + 1) * P] for w in (wh, wl))
                        for h in range(HALVES):
                            out, cols = PS[:, 2 * p + h, :], slice(h * BANK, (h + 1) * BANK)
                            nc.tensor.matmul(out, w_h, act_at(par_pair, a, 0)[:, cols], start=a == 0, stop=False)
                            nc.tensor.matmul(out, w_h, act_at(par_pair, a, 1)[:, cols], start=False, stop=False)
                        for h in range(HALVES):
                            out, cols = PS[:, 2 * p + h, :], slice(h * BANK, (h + 1) * BANK)
                            last = nc.tensor.matmul(out, w_l, act_at(par_pair, a, 0)[:, cols], start=False, stop=a == 1)
                        if d == KT - 1:
                            last.then_inc(unit_done, 1)
                    if d < KT - 1:
                        last.then_inc(down_done, 1)

            with pe.Fori(0, 5) as i:
                for s in range(2):
                    base = FFN0 + 4 + 6 * s
                    f = 4 * i + 2 * s + 2
                    for k in range(4):
                        if k % 2 == 0:
                            pe.wait_ge(a_ready, f - 2 + k // 2 + 1)
                        unit_matmuls(pe, base, 12, i, k, k, h_hi, h_lo)
                    pe.wait_ge(a_lo, f)
                    down(base, 12, i, 4, s % 2, (f + 1, f + 2), (KT - 1) * (2 * i + s), KT * (2 * i + s))
            pe.wait_ge(a_lo, FT)
            down(N_UNITS - 2, 0, 0, 0, 0, (FT, FT), (KT - 1) * 10, KT * 10)
            pe.wait_ge(acc2_ready, KT)
            norm_sums(ACC)
            norm_spread(pe, 3)


_W = [512] + [128] * 6 + [24] + [512] * 3
_OFF = [int(v) for v in np.cumsum([0] + _W)]


def _unit_columns():
    q, kc, vc, ks, vs, kw, vw, gl, bg, cg, u = _OFF[:-1]
    out = []
    for j in range(CONV_T):
        out += [range(o + j * P, o + (j + 1) * P) for o in (u, cg, bg)]
    out += [range(q + j * P, q + (j + 1) * P) for j in range(4)]
    out.append([gl + 3 * h + b for h in range(HEADS) for b in (1, 2, 0)] + [-1] * (P - 3 * HEADS))
    for g in range(KV):
        for a, b in ((ks, kw), (vs, vw), (kc, vc)):
            out.append([a + g * DH + d for d in range(DH)] + [b + g * DH + d for d in range(DH)])
    return [list(c) for c in out]


def _blocks(w):
    return w.reshape(KT, P, P).transpose(1, 0, 2).reshape(P, KT * P)


def _shape_constants():
    consts = np.zeros((P, NCON), np.float32)
    consts[:, C_ID:C_ID + P] = np.eye(P)
    consts[:, C_ONE:C_ONE + P] = 1.0
    t = np.arange(T).reshape(TT, P).T
    consts[:, C_VALID:C_VALID + TT] = t >= CMP_BLOCK - 1
    m = np.zeros((P, NMASK), np.float32)
    q, k = np.arange(P)[:, None], np.arange(P)[None, :]
    m[:, M_ID:M_ID + P] = np.eye(P)
    m[:, M_DIAG:M_DIAG + P] = np.where(k > q, NEG, 0.0)
    m[:, M_EDGE:M_EDGE + P] = np.where(k <= q, NEG, 0.0)
    n = np.arange(CW)[None, :]
    for i in range(TT):
        sees = (n < NCMP) & (CMP_STRIDE * n + CMP_BLOCK - 1 <= i * P + q)
        m[:, M_CMP + i * CW:M_CMP + (i + 1) * CW] = np.where(sees, 0.0, NEG)
    aq = np.zeros((HEADS, AR, T), np.float32)
    tok = np.arange(T)
    for h in range(HEADS):
        slope = 2.0 ** (-8.0 * (h + 1) / HEADS)
        aq[h, 0] = slope
        aq[h, 1] = -slope * (tok % P)
        for j in range(TT):
            aq[h, 2 + j] = P * slope * (j - tok // P)
    ak = np.zeros((AR, 2 * T + CW), np.float32)
    s = np.concatenate([tok, tok, CMP_STRIDE * np.arange(NCMP) + CMP_BLOCK - 1])
    ak[0, :len(s)] = s % P
    ak[1, :len(s)] = 1.0
    for j in range(TT):
        ak[2 + j, :len(s)] = s // P == j
    return consts, m, aq, ak


def kernel(x, norm_mix_g, w_in, pos_ck, w_ck1, w_ck2, pos_cv, w_cv1, w_cv2, conv_mix_w, norm_out_attn_g,
           norm_out_conv_g, w_out, norm_ffn_g, w_gate, w_up, ffn_conv_w, ffn_conv_b, w_down, norm_final_g):
    import concourse.bacc as bacc
    from concourse.bass_utils import run_bass_kernel_spmd

    A = np.ascontiguousarray
    w_in, w_out, w_gate, w_up, w_down = (np.asarray(a)[0] for a in (w_in, w_out, w_gate, w_up, w_down))
    padded = np.concatenate([w_in, np.zeros((D, 1), np.float32)], axis=1)
    units = [_blocks(padded[:, c]) for c in _unit_columns()]
    units += [_blocks(w_out[:, d * P:(d + 1) * P]) for d in range(N_OUT)]
    for pr in range(FT // 2 + 1):
        if pr < FT // 2:
            for f in (2 * pr, 2 * pr + 1):
                units += [_blocks(w_gate[:, f * P:(f + 1) * P]), _blocks(w_up[:, f * P:(f + 1) * P])]
        if pr:
            units += [w_down[f * P:(f + 1) * P] for f in (2 * pr - 2, 2 * pr - 1)]
    cols = lambda a, n: np.asarray(a).reshape(n, P).T
    taps = lambda a, n: np.asarray(a)[0].reshape(3, n, P).transpose(2, 1, 0).reshape(P, 3 * n)
    params = np.concatenate([cols(norm_mix_g, 8), cols(norm_out_attn_g, 4), cols(norm_out_conv_g, 4),
                             cols(norm_ffn_g, 8), cols(norm_final_g, 8), taps(conv_mix_w, CONV_T), taps(ffn_conv_w, FT),
                             cols(ffn_conv_b, FT), cols(pos_ck, 16), cols(pos_cv, 16)], axis=1)
    first = lambda a: np.asarray(a)[0].reshape(16, P, P).transpose(1, 0, 2).reshape(P, 2, 1024)
    consts, masks, aq, ak = _shape_constants()
    arrays = {
        "xT": A(np.asarray(x)[0].T.reshape(KT, P, T)),
        "w_units": A(np.stack(units)),
        "w_cmp1": A(np.concatenate([first(w_ck1), first(w_cv1)], axis=1)),
        "w_cmp2": A(np.stack([np.asarray(w_ck2)[0], np.asarray(w_cv2)[0]], axis=1)),
        "params": A(params), "consts": consts, "masks": masks, "alibi_q": aq, "alibi_k": ak,
    }
    nc = bacc.Bacc("TRN2", target_bir_lowering=False, num_devices=1)
    args = [nc.dram_tensor("in_" + n, a.shape, mybir.dt.from_np(a.dtype), kind="ExternalInput").ap() for n, a in arrays.items()]
    args.append(nc.dram_tensor("outT", (KT, P, T), F32, kind="ExternalOutput").ap())
    hybrid_layer(nc, *args)
    r = run_bass_kernel_spmd(nc, [{"in_" + n: a for n, a in arrays.items()}], core_ids=[0])
    return A(r.results[0]["outT"].reshape(D, T).T).reshape(1, T, D)
```

```python
import numpy as np
import concourse.bass as bass
from concourse import mybir
from contextlib import ExitStack

F32 = mybir.dt.float32
F32R = mybir.dt.float32r
BF16 = mybir.dt.bfloat16
ALU = mybir.AluOpType
ACT = mybir.ActivationFunctionType
AX = mybir.AxisListType

P = 128
D = 1024
T = 1024
KT = D // P
TT = T // P
BANK = 512
HALVES = T // BANK
HEADS, KV, DH = 8, 2, 64
GROUP = HEADS // KV
DFF = 2816
FT = DFF // P
CMP_BLOCK, CMP_STRIDE = 32, 16
NCMP = (T - CMP_BLOCK) // CMP_STRIDE + 1
CW = 64
WINDOW = 512
WT = WINDOW // P
SEL_BLOCK, SEL_TOPK = 64, 16
assert T // SEL_BLOCK <= SEL_TOPK
CONV_T = 4
EPS = 1e-6
NEG = -1e30
AR = 10
MR = 6

N_CONV = 3 * CONV_T
N_QKV = HEADS * DH // P + 3 * KV + 1
N_IN = N_CONV + N_QKV
N_OUT = D // P
OUT0 = N_IN
FFN0 = OUT0 + N_OUT
N_UNITS = FFN0 + 3 * FT
RING = 3

P_GMIX, P_GOUT, P_GFFN, P_GFIN = 0, 8, 16, 24
P_CONV = 32
P_FCW = P_CONV + 3 * CONV_T
P_FCB = P_FCW + 3 * FT
P_POSK = P_FCB + FT
P_POSV = P_POSK + CMP_BLOCK // 2
NPAR = P_POSV + CMP_BLOCK // 2
C_ID, C_ONE, C_VALID = 0, P, 2 * P
NCON = 2 * P + TT
M_ID, M_DIAG, M_EDGE, M_CMP = 0, GROUP * P, (GROUP + 1) * P, (GROUP + 2) * P
NMASK = M_CMP + TT * P


class Steps:

    def __init__(self, eng, sem):
        self.eng, self.sem, self.base, self.local, self.stack = eng, sem, 0, 0, []

    def add(self, ins):
        ins.then_inc(self.sem, 1)
        self.local += 1

    def settle(self):
        self.eng.wait_ge(self.sem, self.base + self.local)

    def enter(self, i, trips, per):
        start = self.base + self.local
        self.stack.append((start, trips, per))
        self.base, self.local = start + per * i, 0

    def leave(self):
        start, trips, per = self.stack.pop()
        assert self.local == per, (self.local, per)
        self.base, self.local = start, per * trips


def key_tiles(i):
    return [(0, j) for j in range(i + 1)] + [(1, j) for j in range(max(0, i - WT), i + 1)] + [(2, 0)]


STEPS = [(i, br, j) for i in range(TT) for br, j in key_tiles(i)]
NS = len(STEPS)


def hybrid_layer(nc, xT, w_units, w_cmp1, w_cmp2, params_d, consts_d, masks_d, alibi_q, alibi_k, outT):
    with ExitStack() as ctx:
        def sb(name, shape, dt=F32):
            return ctx.enter_context(nc.sbuf_tensor(name, shape, dt))

        def sem(name):
            return ctx.enter_context(nc.semaphore(name))

        params = sb("params", [P, NPAR])
        consts = sb("consts", [P, NCON])
        masks = sb("masks", [P, NMASK], BF16)
        w2c = sb("w2c", [P, 2, DH])
        raw = sb("raw", [P, RING, 1024])
        wh = sb("wh", [P, RING, 1024], F32R)
        wl = sb("wl", [P, RING, 1024], F32R)
        F1 = sb("F1", [P, 15, 1024])
        R1 = sb("R1", [P, 16, 1024], F32R)
        R2 = sb("R2", [P, 8, 1024], F32R)
        PBm = sb("PBm", [P, 2, 768])
        small = sb("small", [P, 64])
        gates = sb("gates", [P, TT, 3 * HEADS])
        nmax = sb("nmax", [P, 3, TT, GROUP])
        coef = sb("coef", [P, 2, 3 * GROUP])
        hidc = sb("hidc", [P, 2, CW])
        posb = sb("posb", [P, 2])
        PS = ctx.enter_context(nc.psum_tensor("PS", [P, 8, BANK], F32))

        def par(c, n=1):
            return params[:, c:c + n] if isinstance(c, int) else params[:, bass.ds(c, n)]

        ident = consts[:, C_ID:C_ID + P]
        ones = consts[:, C_ONE:C_ONE + P]

        def pair(p):
            return PS[:, 2 * p:2 * p + 2, :].rearrange("p a b -> p (a b)")

        Q0, GATE, KV0, Y0, X1 = 0, 4, 5, 11, 5
        U_S, CU_S, CT_S, SQ_S, ACCY = 5, 6, 7, 8, 9
        RF = R1[:, :, :].rearrange("p a b -> p (a b)")
        KCMP, KSEL, KWIN, KEYS = 64, P, P + T, P + 2 * T
        at_r = [0]

        def piece(n):
            at_r[0] += n
            return RF[:, at_r[0] - n:at_r[0]]

        QA = piece(GROUP * T).rearrange("p (i h q) -> p i h q", h=GROUP, q=P)
        QB = piece(GROUP * T).rearrange("p (i h q) -> p i h q", h=GROUP, q=P)
        KA, KB = piece(KEYS), piece(KEYS)
        NV, VW = 2 * TT + 1, DH + 2
        VH = piece(NV * VW).rearrange("p (j d) -> p j d", d=VW)
        VL = piece(NV * VW).rearrange("p (j d) -> p j d", d=VW)
        MH, ML = piece(P), piece(P)
        EB, PTH, PTL = ([buf[:, b // 2, 512 * (b % 2):512 * (b % 2 + 1)] for b in range(4)] for buf in (raw, wh, wl))
        OT = [PBm[:, :, :].rearrange("p a b -> p (a b)")[0:DH + 1, 512 * br:512 * (br + 1)] for br in range(3)]
        RB = PBm[:, :, :].rearrange("p a b -> p (a b)")[:, 0:1024]
        CK, CV = raw[:, 1, :], raw[:, 2, :]
        W1C = F1[:, Y0:Y0 + 4, :].rearrange("p a b -> p (a b)").rearrange("p (k l h) -> p k l h", k=2, l=16)
        OSUM = F1[:, GATE, 0:3 * GROUP * DH]

        def f32(ap):
            return ap.bitcast(F32)

        consts_in, late_in, w1_in, ak_in = sem("consts_in"), sem("late_in"), sem("w1_in"), sem("ak_in")
        masks_in = sem("masks_in")
        x_in, aq_in = [sem(f"x_in{k}") for k in range(KT)], sem("aq_in")
        x1_in, out_done = sem("x1_in"), sem("out_done")
        unit_in = [sem(f"unit_in{s}") for s in range(RING)]
        unit_hi, unit_lo, unit_done = sem("unit_hi"), sem("unit_lo"), sem("unit_done")
        dve_step = sem("dve_step")
        sq_ready, acc_ready = sem("sq_ready"), sem("acc_ready")
        ss_ready, ss_read, rt_ready, diag_ready, rb_ready = (sem("ss_ready"), sem("ss_read"), sem("rt_ready"),
                                                             sem("diag_ready"), sem("rb_ready"))
        h_ready, h_hi_ready, h_lo_ready = sem("h_ready"), sem("h_hi_ready"), sem("h_lo_ready")
        v_copied, clear_ready, acc_clear = sem("v_copied"), sem("clear_ready"), sem("acc_clear")
        u_ready, cu_ready, tap_ready, y_ready, ysq_ready, accy_ready = (
            sem("u_ready"), sem("cu_ready"), sem("tap_ready"), sem("y_ready"), sem("ysq_ready"), sem("accy_ready"))
        yn_ready, mc_hi, mc_lo = sem("yn_ready"), sem("mc_hi"), sem("mc_lo")
        qkv_ready = sem("qkv_ready")
        gt_ready, gexp_ready, gates_ready = sem("gt_ready"), sem("gexp_ready"), sem("gates_ready")
        pos_ready, posb_ready = sem("pos_ready"), sem("posb_ready")
        ck_ready, hid_ready, gelu_ready, kvc_ready = sem("ck_ready"), sem("hid_ready"), sem("gelu_ready"), sem("kvc_ready")
        vt_ready, v_hi, v_lo, k_hi, k_lo, kc_hi, kc_lo = (sem("vt_ready"), sem("v_hi"), sem("v_lo"), sem("k_hi"),
                                                        sem("k_lo"), sem("kc_hi"), sem("kc_lo"))
        q_hi, q_lo = sem("q_hi"), sem("q_lo")
        sa_ready, sb_ready, max_a, max_b = sem("sa_ready"), sem("sb_ready"), sem("max_a"), sem("max_b")
        mt_ready, mt_hi, mt_lo, m_in = sem("mt_ready"), sem("mt_hi"), sem("mt_lo"), sem("m_in")
        st_ready, e_ready, pt_hi, pt_lo, pv_done = (sem("st_ready"), sem("e_ready"), sem("pt_hi"), sem("pt_lo"),
                                                    sem("pv_done"))
        ot_copied, ot_turned, o_ready = sem("ot_copied"), sem("ot_turned"), sem("o_ready")
        osq_ready, on_ready, ot_ready, ma_hi, ma_lo = (sem("osq_ready"), sem("on_ready"), sem("ot_ready"),
                                                       sem("ma_hi"), sem("ma_lo"))
        x1_ready, x1sq_ready, acc1_ready = sem("x1_ready"), sem("x1sq_ready"), sem("acc1_ready")
        g_tap, taps_ready, silu_ready, a_ready, a_hi, a_lo = (sem("g_tap"), sem("taps_ready"), sem("silu_ready"),
                                                              sem("a_ready"), sem("a_hi"), sem("a_lo"))
        down_done, down_added = sem("down_done"), sem("down_added")
        x2sq_ready, acc2_ready, og_ready, out_ready = (sem("x2sq_ready"), sem("acc2_ready"), sem("og_ready"),
                                                       sem("out_ready"))

        def at(base, coef, i, k):
            return (base + k) % RING, (base + k) // RING + (coef // RING) * i + 1, base + k + coef * i

        def norm_sums(acc):
            for t in range(TT):
                last = nc.tensor.matmul(PS[:, 6, t:t + 1], acc[:, t * P:(t + 1) * P], ones[:, 0:1],
                                        start=True, stop=True)
            last.then_inc(ss_ready, 1)

        def norm_spread(pe, m):
            pe.wait_ge(diag_ready, m + 1)
            for h in range(HALVES):
                last = nc.tensor.matmul(PS[:, 6 + h, :], ones, RB[:, h * BANK:(h + 1) * BANK],
                                        start=True, stop=True)
            last.then_inc(rb_ready, 1)

        def norm_act(act, m):
            act.wait_ge(ss_read, m + 1 + (m > 1))
            nc.scalar.activation(small[:, 8:16], small[:, 0:8], ACT.Sqrt).then_inc(rt_ready, 1)

        def norm_dve(dve, steps, m, width):
            dve.wait_ge(ss_ready, m + 1)
            nc.vector.tensor_scalar(small[:, 0:8], PS[:, 6, 0:8], 1.0 / width, EPS, ALU.mult, ALU.add)\
                .then_inc(ss_read, 1)
            dve.wait_ge(rt_ready, m + 1 + (m > 1))
            newton(steps)
            nc.vector.tensor_tensor(RB.rearrange("p (t q) -> p t q", t=TT),
                                    ident.rearrange("p (o q) -> p o q", o=1).broadcast_to([P, TT, P]),
                                    small[:, 24:32].rearrange("p (t o) -> p t o", o=1).broadcast_to([P, TT, P]),
                                    ALU.mult).then_inc(diag_ready, 1)

        def newton(steps):
            v, root, r, rr, vrr, f, out = (small[:, c:c + 8] for c in (0, 8, 16, 32, 40, 48, 24))
            for ins in (lambda: nc.vector.reciprocal(r, root),
                        lambda: nc.vector.tensor_tensor(rr, r, r, ALU.mult),
                        lambda: nc.vector.tensor_tensor(vrr, rr, v, ALU.mult),
                        lambda: nc.vector.tensor_scalar(f, vrr, -0.5, 1.5, ALU.mult, ALU.add),
                        lambda: nc.vector.tensor_tensor(out, f, r, ALU.mult)):
                steps.add(ins())
                steps.settle()

        def load(sp, base, coef, i, k):
            slot, held, n = at(base, coef, i, k)
            sp.wait_ge(unit_lo, n - RING + 1)
            src = w_units[n] if isinstance(n, int) else w_units[bass.ds(n, 1), :, :].rearrange("o p n -> (o p) n")
            sp.dma_start(raw[:, slot, :], src).then_inc(unit_in[slot], 16)

        def split_hi(act, base, coef, i, k, free=False):
            slot, held, n = at(base, coef, i, k)
            act.wait_ge(unit_in[slot], 16 * held)
            if not free and (not isinstance(n, int) or n >= RING):
                act.wait_ge(unit_done, n - RING + 1)
            nc.scalar.activation(wh[:, slot, :], raw[:, slot, :], ACT.Copy).then_inc(unit_hi, 1)

        def split_lo(dve, base, coef, i, k, free=False):
            slot, held, n = at(base, coef, i, k)
            dve.wait_ge(unit_hi, n + 1)
            if not free and (not isinstance(n, int) or n >= RING):
                dve.wait_ge(unit_done, n - RING + 1)
            nc.vector.tensor_tensor(wl[:, slot, :], raw[:, slot, :], f32(wh[:, slot, :]), ALU.subtract)\
                .then_inc(unit_lo, 1)

        def unit_matmuls(pe, base, coef, i, k, p, hi, lo, order=range(KT), arrives=None):
            slot, held, n = at(base, coef, i, k)
            pe.wait_ge(unit_lo, n + 1)
            for kt in order:
                if arrives:
                    arrives(kt)
                w_h, w_l = wh[:, slot, kt * P:(kt + 1) * P], wl[:, slot, kt * P:(kt + 1) * P]
                first, end = kt == order[0], kt == order[-1]
                for h in range(HALVES):
                    out, cols = PS[:, 2 * p + h, :], slice(h * BANK, (h + 1) * BANK)
                    nc.tensor.matmul(out, w_h, hi(kt)[:, cols], start=first, stop=False)
                    nc.tensor.matmul(out, w_h, lo(kt)[:, cols], start=False, stop=False)
                for h in range(HALVES):
                    out, cols = PS[:, 2 * p + h, :], slice(h * BANK, (h + 1) * BANK)
                    last = nc.tensor.matmul(out, w_l, hi(kt)[:, cols], start=False, stop=end)
            last.then_inc(unit_done, 1)

        h_hi, h_lo = (lambda k: R1[:, k, :]), (lambda k: R1[:, 8 + k, :])
        m_hi = lambda k: R1[:, k, :] if k < 4 else R2[:, k - 4, :]
        m_lo = lambda k: R1[:, 4 + k, :] if k < 4 else R2[:, k, :]

        ROWS = [(h, i) for h in range(GROUP) for i in range(TT)]
        NR = len(ROWS)
        CMP_FIRST = [(i + 1) % 4 != 0 for i in range(TT)]
        CMP_IN_B = [BANK + (P if i >= WT else 0) for i in range(TT)]
        ENDS = [s + 1 for s in range(NS) if s + 1 == NS or STEPS[s + 1][:2] != STEPS[s][:2]]
        STEP_OF_TURN = [ENDS[3 * i + 2] + 1 for i in range(TT)]

        def act_at(par, e, part):
            return R2[:, 4 * par + 2 * e + part, :]

        T1 = [F1[:, 0, :], F1[:, 1, :]]
        SA = [F1[:, 2, :], F1[:, 3, :]]
        ACC = F1[:, 4, :]
        SQ = [F1[:, 13, :], F1[:, 14, :]]
        DOWN_PAIRS = [0, 1, 0, 1, 2, 3, 2, 3]

        block = ctx.enter_context(nc.Block())

        @block.sync
        def _(sp):
            sp.dma_start(F1[:, 0, :], xT[0]).then_inc(x_in[0], 16)
            sp.dma_start(consts[:, :], consts_d).then_inc(consts_in, 16)
            sp.dma_start(params[:, :], params_d).then_inc(consts_in, 16)
            for k in range(1, KT):
                sp.dma_start(F1[:, k, :], xT[k]).then_inc(x_in[k], 16)
            for n in range(RING):
                sp.dma_start(raw[:, n, :], w_units[n]).then_inc(unit_in[n], 16)
            sp.dma_start(w2c[:, :, :], w_cmp2).then_inc(late_in, 16)
            with sp.Fori(0, 4) as i:
                for k in range(3):
                    load(sp, 3, 3, i, k)
            with sp.Fori(0, 3) as i:
                for k in range(3):
                    load(sp, 15, 3, i, k)
            sp.wait_ge(mc_lo, CONV_T)
            sp.dma_start(F1[:, Y0:Y0 + 4, :], w_cmp1).then_inc(w1_in, 16)
            with sp.Fori(0, KV) as g:
                for part, src, done in ((0, MH, mt_hi), (1, ML, mt_lo)):
                    sp.wait_ge(done, g + 1)
                    for br in range(3):
                        row = DH + AR + 3 * part + br
                        sp.dma_start(f32(QB[row:row + 1, :, :, :]).rearrange("o i h q -> o (i h) q"),
                                     f32(src[32 * br:32 * br + 32, :])).then_inc(m_in, 16)
            sp.wait_ge(k_hi, 2 * KV)
            sp.wait_ge(k_lo, 4 * KV)
            sp.wait_ge(v_copied, KV)
            sp.wait_ge(ck_ready, 4 * KV)
            sp.wait_ge(hid_ready, 2 * KV)
            for k in range(KT):
                sp.dma_start(F1[:, X1 + k, :], xT[k]).then_inc(x1_in, 16)
            sp.wait_ge(pt_lo, KV * NS)
            load(sp, 24, 0, 0, 0)
            load(sp, 25, 0, 0, 0)
            load(sp, 26, 0, 0, 0)
            with sp.Fori(0, (N_UNITS - 28) // 3) as i:
                for k in range(3):
                    load(sp, 27, 3, i, k)
            load(sp, N_UNITS - 1, 0, 0, 0)
            for k in range(KT):
                sp.wait_ge(out_ready, k + 1)
                sp.dma_start(outT[k], F1[:, X1 + k, :]).then_inc(out_done, 16)
            sp.wait_ge(out_done, 16 * KT)

        @block.gpsimd
        def _(pool):
            pool.dma_start(masks[:, :], masks_d).then_inc(masks_in, 16)
            for k in range(KT):
                pool.wait_ge(h_hi_ready, k + 1)
                nc.gpsimd.tensor_tensor(h_lo(k), F1[:, k, :], f32(h_hi(k)), ALU.subtract).then_inc(h_lo_ready, 1)
            pool.wait_ge(ss_ready, 1)
            nc.gpsimd.memset(F1[:, ACCY, :], 0.0).then_inc(acc_clear, 1)
            pool.wait_ge(unit_done, N_IN)
            for pad, value in ((KA[:, 0:P], 0.0), (KB[0:DH, 0:P], 0.0), (VH, 0.0), (VL, 0.0)):
                nc.gpsimd.memset(f32(pad), value).then_inc(clear_ready, 1)
            pool.wait_ge(clear_ready, 4)
            nc.gpsimd.memset(f32(VH[:, :, DH:DH + 1]), 1.0).then_inc(clear_ready, 1)
            pool.dma_start(KB[DH:DH + AR + MR, :], alibi_k).then_inc(ak_in, 16)
            with pool.Fori(0, KV) as g:
                pool.dma_start(QB[DH:DH + AR, :, :, :].rearrange("r i h q -> r (i h q)"),
                               alibi_q[bass.ds(g, 1)].rearrange("o r n -> (o r) n")).then_inc(aq_in, 16)
                pool.wait_ge(st_ready, NS * g + NS)
            pool.wait_ge(o_ready, KV * TT)
            nc.gpsimd.memset(ACC, 0.0).then_inc(acc_clear, 1)
            for k in range(KT):
                pool.wait_ge(h_hi_ready, KT + k + 1)
                nc.gpsimd.tensor_tensor(h_lo(k), F1[:, k % 2, :], f32(h_hi(k)), ALU.subtract).then_inc(h_lo_ready, 1)
            nc.gpsimd.memset(ACC, 0.0).then_inc(acc_clear, 1)

        @block.scalar
        def _(act):
            for k in range(KT):
                act.wait_ge(x_in[k], 16)
                if k > 2:
                    act.wait_ge(acc_ready, k - 2)
                dst = F1[:, 10, :] if k == 0 else F1[:, 8 + k % 2, :]
                nc.scalar.activation(dst, F1[:, k, :], ACT.Square).then_inc(sq_ready, 1)
            norm_act(act, 0)
            split_hi(act, 0, 0, 0, 0)
            for k in range(KT):
                act.wait_ge(h_ready, k + 1)
                nc.scalar.activation(h_hi(k), F1[:, k, :], ACT.Copy).then_inc(h_hi_ready, 1)
            split_hi(act, 1, 0, 0, 0)
            act.wait_ge(h_lo_ready, KT)
            with act.Fori(0, CONV_T) as i:
                split_hi(act, 2, 3, i, 0, free=True)
                act.wait_ge(unit_done, 3 * i + 1)
                nc.scalar.activation(F1[:, U_S, :], pair(0), ACT.Copy).then_inc(u_ready, 1)
                split_hi(act, 3, 3, i, 0)
                act.wait_ge(cu_ready, i + 1)
                nc.scalar.activation(F1[:, CT_S, :], F1[:, CU_S, :], ACT.Copy, scale=par(P_CONV + 3 * i + 2))\
                    .then_inc(tap_ready, 1)
                split_hi(act, 4, 3, i, 0)
                act.wait_ge(y_ready, i + 1)
                nc.scalar.activation(F1[:, SQ_S, :], F1[:, bass.ds(Y0 + i, 1), :].rearrange("p o t -> p (o t)"),
                                     ACT.Square).then_inc(ysq_ready, 1)

            def evac(base, coef, i, k, slot):
                _, _, n = at(base, coef, i, k)
                act.wait_ge(unit_done, n + 1)
                nc.scalar.activation(slot, pair(n_pair(base + k)), ACT.Copy).then_inc(qkv_ready, 1)

            n_pair = lambda n: n % 3
            split_hi(act, 14, 0, 0, 0)
            evac(12, 0, 0, 0, F1[:, 0, :])
            norm_act(act, 1)
            split_hi(act, 15, 0, 0, 0)
            evac(13, 0, 0, 0, F1[:, 1, :])
            for k in range(CONV_T):
                act.wait_ge(yn_ready, k + 1)
                nc.scalar.activation(R2[:, k, :], F1[:, Y0 + k, :], ACT.Copy).then_inc(mc_hi, 1)
            with act.Fori(0, 2) as i:
                for k in range(3):
                    split_hi(act, 16, 3, i, k)
                    evac(14, 3, i, k, F1[:, bass.ds(3 * i + k + 2, 1), :].rearrange("p o t -> p (o t)"))
            for n in range(20, 23):
                if n + 2 < 24:
                    split_hi(act, n + 2, 0, 0, 0)
                evac(n, 0, 0, 0, F1[:, n - 12, :])
            act.wait_ge(gt_ready, 1)
            nc.scalar.activation(gates[:, :, :], PS[:, 4:6, :].rearrange("p a (b c) -> p (a b) c", c=P)[:, :, 0:3 * HEADS],
                                 ACT.Exp, scale=-1.0).then_inc(gexp_ready, 1)
            act.wait_ge(pos_ready, 1)
            nc.scalar.activation(posb[:, :], PS[:, 6, 0:2], ACT.Copy).then_inc(posb_ready, 1)
            act.wait_ge(clear_ready, 5)
            act.wait_ge(posb_ready, 1)
            act.wait_ge(unit_lo, N_IN + 1)
            with act.Fori(0, KV) as g:
                def kv_rows(what, half):
                    return F1[half * DH:(half + 1) * DH, bass.ds(KV0 + 3 * g + what, 1), :].rearrange("p o t -> p (o t)")

                def to_compress(dst, half):
                    nc.scalar.activation(dst[0:DH, :], kv_rows(2, half), ACT.Copy).then_inc(ck_ready, 1)
                    nc.scalar.activation(dst[DH:P, 0:T - 1], kv_rows(2, half)[:, 1:T], ACT.Copy).then_inc(ck_ready, 1)

                def hidden(kv):
                    act.wait_ge(hid_ready, 2 * g + kv + 1)
                    nc.scalar.activation(hidc[:, kv, 0:NCMP], PS[:, 6 + kv, 0:NCMP], ACT.Gelu_apprx_tanh,
                                         bias=posb[:, kv:kv + 1]).then_inc(gelu_ready, 1)

                def queries(h):
                    rows = slice((h % 2) * DH, (h % 2 + 1) * DH)
                    src = F1[rows, bass.ds(Q0 + 2 * g + h // 2, 1), :].rearrange("p o (i q) -> p (o i) q", q=P)
                    nc.scalar.activation(QA[rows, :, h, :], src, ACT.Copy, scale=DH ** -0.5).then_inc(q_hi, 1)

                to_compress(CK, 0)
                for half in range(2):
                    nc.scalar.activation(KA[half * DH:(half + 1) * DH, KSEL + half * T:KSEL + (half + 1) * T], kv_rows(0, half),
                                         ACT.Copy).then_inc(k_hi, 1)
                queries(0)
                hidden(0)
                act.wait_ge(kvc_ready, 2 * g + 1)
                for rows in (slice(0, DH), slice(DH, P)):
                    nc.scalar.activation(KA[rows, KCMP:KCMP + NCMP], PS[0:DH, 6, P:P + NCMP], ACT.Copy)\
                        .then_inc(kc_hi, 1)
                for h in range(1, GROUP):
                    queries(h)
                nc.scalar.activation(RB, F1[:, bass.ds(KV0 + 3 * g + 1, 1), :].rearrange("p o t -> p (o t)"), ACT.Copy)\
                    .then_inc(v_copied, 1)
                to_compress(CV, 1)
                act.wait_ge(mt_ready, g + 1)
                nc.scalar.activation(MH[0:96, :], PS[0:96, 0, 0:P], ACT.Copy).then_inc(mt_hi, 1)
                act.wait_ge(vt_ready, g + 1)
                nc.scalar.activation(VH[:, 0:2 * TT, 0:DH].rearrange("p (b j) d -> p b j d", b=2),
                                     pair(2).rearrange("p (j b d) -> p b j d", b=2, d=DH), ACT.Copy).then_inc(v_hi, 1)
                hidden(1)
                act.wait_ge(kvc_ready, 2 * g + 2)
                nc.scalar.activation(VH[KCMP:KCMP + NCMP, 2 * TT, 0:DH], PS[0:NCMP, 7, P:P + DH], ACT.Copy).then_inc(kc_hi, 1)

                for s in range(NS):
                    act.wait_ge(st_ready, NS * g + s + 1)
                    if s > 3:
                        act.wait_ge(pv_done, NS * g + s - 3)
                    nc.scalar.activation(PTH[s % 4], PS[:, s % 4, :], ACT.Exp).then_inc(pt_hi, 1)
                    nc.scalar.activation(EB[s % 4], PS[:, s % 4, :], ACT.Exp).then_inc(e_ready, 1)
                act.wait_ge(pv_done, NS * g + NS)
            act.wait_ge(o_ready, KV * TT)
            for t in range(TT):
                nc.scalar.activation(PS[:, t, :].rearrange("p (a b) -> p a b", a=4), F1[:, 0:4, t * P:(t + 1) * P],
                                     ACT.Square, accum_out=small[:, 56 + t:57 + t]).then_inc(osq_ready, 1)
            act.wait_ge(ss_read, 3)
            nc.scalar.activation(small[:, 8:16], small[:, 0:8], ACT.Sqrt).then_inc(rt_ready, 1)
            for k in range(4):
                act.wait_ge(ot_ready, k + 1)
                nc.scalar.activation(m_hi(k), pair(k), ACT.Copy, scale=par(P_GOUT + k)).then_inc(ma_hi, 1)

            def residual_square(base, coef, i, k):
                split_hi(act, base + 2, coef, i, k)
                _, _, n = at(base, coef, i, k)
                d = n - OUT0
                act.wait_ge(x1_ready, d + 1)
                if not isinstance(d, int) or d:
                    act.wait_ge(acc1_ready, d)
                nc.scalar.activation(SQ[0], F1[:, bass.ds(X1 + d, 1), :].rearrange("p o t -> p (o t)"), ACT.Square)\
                    .then_inc(x1sq_ready, 1)

            split_hi(act, 24, 0, 0, 0)
            residual_square(OUT0, 0, 0, 0)
            residual_square(OUT0 + 1, 0, 0, 0)
            with act.Fori(0, 2) as i:
                for k in range(3):
                    residual_square(OUT0 + 2, 3, i, k)
            norm_act(act, 2)
            for k in range(KT):
                act.wait_ge(h_ready, KT + k + 1)
                nc.scalar.activation(h_hi(k), F1[:, k % 2, :], ACT.Copy).then_inc(h_hi_ready, 1)

            def gated(base, coef, i, k, e, f, par_pair, down):
                _, _, n = at(base, coef, i, k)
                split_hi(act, base + 2, coef, i, k)
                act.wait_ge(unit_done, n + 1)
                nc.scalar.activation(T1[e], pair(2 * e), ACT.Identity, scale=par(P_FCW + 3 * f + 2), bias=par(P_FCB + f))\
                    .then_inc(g_tap, 1)
                split_hi(act, base + 2, coef, i, k + 1)
                act.wait_ge(taps_ready, f + 1)
                if not isinstance(f, int) or f > 1:
                    act.wait_ge(a_lo, f - 1)
                nc.scalar.activation(SA[e], T1[e], ACT.Silu).then_inc(silu_ready, 1)
                act.wait_ge(a_ready, f + 1)
                if down is not None:
                    act.wait_ge(unit_done, down)
                nc.scalar.activation(act_at(par_pair, e, 0), SA[e], ACT.Copy).then_inc(a_hi, 1)

            for e in range(2):
                gated(FFN0, 0, 0, 2 * e, e, e, 0, None)
            with act.Fori(0, 5) as i:
                for s in range(2):
                    base = FFN0 + 4 + 6 * s
                    for e in range(2):
                        gated(base, 12, i, 2 * e, e, 4 * i + 2 * s + 2 + e, (s + 1) % 2, base + 12 * i)
                    split_hi(act, base + 2, 12, i, 4)
                    split_hi(act, base + 2, 12, i, 5)
            for k in range(KT):
                act.wait_ge(down_added, 10 * KT + k + 1)
                if k > 1:
                    act.wait_ge(acc2_ready, k - 1)
                nc.scalar.activation(SQ[k % 2], F1[:, X1 + k, :], ACT.Square).then_inc(x2sq_ready, 1)
            norm_act(act, 3)

        @block.vector
        def _(dve):
            steps = Steps(dve, dve_step)
            for k in range(1, KT):
                dve.wait_ge(sq_ready, k + 1)
                if k > 1:
                    dve.wait_ge(acc_ready, k - 1)
                nc.vector.tensor_tensor(F1[:, 10, :], F1[:, 10, :], F1[:, 8 + k % 2, :], ALU.add).then_inc(acc_ready, 1)
            dve.wait_ge(consts_in, 32)
            norm_dve(dve, steps, 0, D)
            split_lo(dve, 0, 0, 0, 0)
            dve.wait_ge(rb_ready, 1)
            for k in range(KT):
                nc.vector.scalar_tensor_tensor(F1[:, k, :], F1[:, k, :], par(P_GMIX + k), pair(3), ALU.mult, ALU.mult)\
                    .then_inc(h_ready, 1)
            split_lo(dve, 1, 0, 0, 0)
            dve.wait_ge(acc_clear, 1)
            with dve.Fori(0, CONV_T) as i:
                steps.enter(i, CONV_T, 2)
                y = F1[:, bass.ds(Y0 + i, 1), :].rearrange("p o t -> p (o t)")
                cu, tap = F1[:, CU_S, :], F1[:, CT_S, :]
                split_lo(dve, 2, 3, i, 0, free=True)
                dve.wait_ge(u_ready, i + 1)
                dve.wait_ge(unit_done, 3 * i + 2)
                nc.vector.tensor_tensor(cu, pair(1), F1[:, U_S, :], ALU.mult).then_inc(cu_ready, 1)
                split_lo(dve, 3, 3, i, 0)
                dve.wait_ge(tap_ready, i + 1)
                dve.wait_ge(cu_ready, i + 1)
                for lag in (1, 2):
                    steps.add(nc.vector.scalar_tensor_tensor(tap[:, lag:], cu[:, 0:T - lag], par(P_CONV + 3 * i + 2 - lag),
                                                             tap[:, lag:], ALU.mult, ALU.add))
                    steps.settle()
                split_lo(dve, 4, 3, i, 0)
                dve.wait_ge(unit_done, 3 * i + 3)
                nc.vector.tensor_tensor(y, pair(2), tap, ALU.mult).then_inc(y_ready, 1)
                dve.wait_ge(ysq_ready, i + 1)
                nc.vector.tensor_tensor(F1[:, ACCY, :], F1[:, ACCY, :], F1[:, SQ_S, :], ALU.add).then_inc(accy_ready, 1)
                steps.leave()
            split_lo(dve, 14, 0, 0, 0)
            norm_dve(dve, steps, 1, CONV_T * P)
            split_lo(dve, 15, 0, 0, 0)
            dve.wait_ge(rb_ready, 2)
            for k in range(CONV_T):
                nc.vector.scalar_tensor_tensor(F1[:, Y0 + k, :], F1[:, Y0 + k, :], par(P_GOUT + 4 + k), pair(3),
                                               ALU.mult, ALU.mult).then_inc(yn_ready, 1)
            for k in range(CONV_T):
                dve.wait_ge(mc_hi, k + 1)
                nc.vector.tensor_tensor(R2[:, 4 + k, :], F1[:, Y0 + k, :], f32(R2[:, k, :]), ALU.subtract)\
                    .then_inc(mc_lo, 1)
            with dve.Fori(0, 2) as i:
                for k in range(3):
                    split_lo(dve, 16, 3, i, k)
            for n in range(22, 24):
                split_lo(dve, n, 0, 0, 0)
            dve.wait_ge(gexp_ready, 1)
            steps.add(nc.vector.tensor_scalar_add(gates[:, :, :], gates[:, :, :], 1.0))
            steps.settle()
            steps.add(nc.vector.reciprocal(gates[:, :, :], gates[:, :, :]))
            steps.settle()
            for g in range(KV):
                g3 = gates[:, :, (3 * g + 2) * GROUP:(3 * g + 3) * GROUP]
                steps.add(nc.vector.tensor_tensor(g3, g3, consts[:, C_VALID:C_VALID + TT]
                                                  .rearrange("p (t o) -> p t o", o=1).broadcast_to([P, TT, GROUP]),
                                                  ALU.mult))
            steps.settle()
            with dve.Fori(0, KV) as g:
                steps.enter(g, KV, 4 * TT)
                for half in range(2):
                    rows, other = slice(half * DH, (half + 1) * DH), slice((1 - half) * DH, (2 - half) * DH)
                    cols = slice(KSEL + half * T, KSEL + (half + 1) * T)
                    dve.wait_ge(k_hi, 2 * g + half + 1)
                    nc.vector.tensor_copy(KA[other, cols], f32(KA[rows, cols])).then_inc(k_lo, 1)
                    nc.vector.tensor_tensor(KB[0:DH, cols],
                                            F1[rows, bass.ds(KV0 + 3 * g, 1), :].rearrange("p o t -> p (o t)"),
                                            f32(KA[rows, cols]), ALU.subtract).then_inc(k_lo, 1)

                def queries(h):
                    e = h % 2
                    rows, other = slice(e * DH, (e + 1) * DH), slice((1 - e) * DH, (2 - e) * DH)
                    dve.wait_ge(q_hi, GROUP * g + h + 1)
                    nc.vector.tensor_copy(QB[0:DH, :, h, :], f32(QA[rows, :, h, :])).then_inc(q_lo, 1)
                    nc.vector.scalar_tensor_tensor(QA[other, :, h, :],
                                                   F1[rows, bass.ds(Q0 + 2 * g + h // 2, 1), :]
                                                   .rearrange("p o (i q) -> p (o i) q", q=P),
                                                   DH ** -0.5, f32(QA[rows, :, h, :]), ALU.mult, ALU.subtract)\
                        .then_inc(q_lo, 1)

                queries(0)
                dve.wait_ge(kc_hi, 3 * g + 2)
                nc.vector.tensor_tensor(KB[0:DH, KCMP:KCMP + NCMP], PS[0:DH, 6, P:P + NCMP],
                                        f32(KA[0:DH, KCMP:KCMP + NCMP]), ALU.subtract).then_inc(kc_lo, 1)

                def max_of(b, br, unit, col, count):
                    h, i = ROWS[b]
                    return nc.vector.tensor_reduce(nmax[:, br, i, h:h + 1],
                                                   pair(2 * (b % 2) + unit)[:, col:col + count], AX.X, ALU.max,
                                                   negate=True)

                for b in range(NR):
                    h, i = ROWS[b]
                    if i == 0 and h:
                        queries(h)
                    dve.wait_ge(sa_ready, NR * g + b + 1)
                    if CMP_FIRST[i]:
                        max_of(b, 2, 0, 0, CW)
                    max_of(b, 0, 0, CW * CMP_FIRST[i], P * (i + 1)).then_inc(max_a, 1)
                    dve.wait_ge(sb_ready, NR * g + b + 1)
                    if not CMP_FIRST[i]:
                        max_of(b, 2, 1, CMP_IN_B[i], CW)
                    max_of(b, 1, 1, 0, P * min(i + 1, WT + 1)).then_inc(max_b, 1)
                dve.wait_ge(mt_hi, g + 1)
                nc.vector.tensor_tensor(ML[0:96, :], PS[0:96, 0, 0:P], f32(MH[0:96, :]), ALU.subtract).then_inc(mt_lo, 1)
                dve.wait_ge(v_hi, g + 1)
                nc.vector.tensor_tensor(VL[:, 0:2 * TT, 0:DH].rearrange("p (b j) d -> p b j d", b=2),
                                        pair(2).rearrange("p (j b d) -> p b j d", b=2, d=DH),
                                        f32(VH[:, 0:2 * TT, 0:DH]).rearrange("p (b j) d -> p b j d", b=2),
                                        ALU.subtract).then_inc(v_lo, 1)
                dve.wait_ge(kc_hi, 3 * g + 3)
                nc.vector.tensor_tensor(VL[KCMP:KCMP + NCMP, 2 * TT, 0:DH], PS[0:NCMP, 7, P:P + DH],
                                        f32(VH[KCMP:KCMP + NCMP, 2 * TT, 0:DH]), ALU.subtract).then_inc(kc_lo, 1)

                def combine(i):
                    dve.wait_ge(ot_turned, TT * g + i + 1)
                    turned = PS[:, 6:8, 0:6 * VW].rearrange("p a (n d) -> p a n d", d=VW)
                    k = coef[:, :, :]
                    steps.add(nc.vector.reciprocal(k[:, 0, :].rearrange("p (a n) -> p a n", a=2), turned[:, :, :, DH]))
                    steps.settle()
                    steps.add(nc.vector.tensor_tensor(k[:, 1, :], k[:, 0, :], gates[:, i, bass.ds(3 * GROUP * g, 3 * GROUP)],
                                                      ALU.mult))
                    steps.settle()
                    steps.add(nc.vector.tensor_tensor(
                        OSUM.rearrange("p (a n d) -> p a n d", a=2, d=DH), turned[:, :, :, 0:DH],
                        k[:, 1, :].rearrange("p (a n o) -> p a n o", a=2, o=1).broadcast_to([P, 2, 6, DH]), ALU.mult))
                    steps.settle()
                    w = GROUP * DH
                    steps.add(nc.vector.tensor_tensor(OSUM[:, 0:w], OSUM[:, 0:w], OSUM[:, w:2 * w], ALU.add))
                    steps.settle()
                    nc.vector.tensor_tensor(F1[:, bass.ds(Q0 + 2 * g, 2), i * P:(i + 1) * P],
                                            OSUM[:, 0:w].rearrange("p (a b) -> p a b", a=2),
                                            OSUM[:, 2 * w:3 * w].rearrange("p (a b) -> p a b", a=2), ALU.add)\
                        .then_inc(o_ready, 1)

                for s in range(NS):
                    dve.wait_ge(e_ready, NS * g + s + 1)
                    nc.vector.tensor_tensor(PTL[s % 4], EB[s % 4], f32(PTH[s % 4]), ALU.subtract).then_inc(pt_lo, 1)
                    if s in ENDS:
                        n = ENDS.index(s)
                        dve.wait_ge(pv_done, NS * g + s)
                        if n and n % 3 == 0:
                            dve.wait_ge(ot_turned, TT * g + n // 3)
                        nc.vector.tensor_copy(OT[n % 3], PS[0:DH + 1, 4 + n % 2, :]).then_inc(ot_copied, 1)
                    if s - 1 in STEP_OF_TURN:
                        combine(STEP_OF_TURN.index(s - 1))
                dve.wait_ge(pv_done, NS * g + NS)
                nc.vector.tensor_copy(OT[2], PS[0:DH + 1, 4 + (3 * TT - 1) % 2, :]).then_inc(ot_copied, 1)
                combine(TT - 1)
                steps.leave()
            dve.wait_ge(osq_ready, TT)
            nc.vector.tensor_scalar(small[:, 0:8], small[:, 56:64], 1.0 / (HEADS * DH), EPS, ALU.mult, ALU.add)\
                .then_inc(ss_read, 1)
            dve.wait_ge(rt_ready, 3)
            newton(steps)
            for t in range(TT):
                o = F1[:, 0:4, t * P:(t + 1) * P]
                nc.vector.tensor_scalar(o, o, small[:, 24 + t:25 + t], None, ALU.mult).then_inc(on_ready, 1)
            for k in range(4):
                dve.wait_ge(ma_hi, k + 1)
                nc.vector.scalar_tensor_tensor(m_lo(k), pair(k), par(P_GOUT + k), f32(m_hi(k)), ALU.mult, ALU.subtract)\
                    .then_inc(ma_lo, 1)
            dve.wait_ge(x1_in, 16 * KT)
            dve.wait_ge(acc_clear, 2)

            def residual(base, coef, i, k):
                split_lo(dve, base + 2, coef, i, k)
                _, _, n = at(base, coef, i, k)
                d = n - OUT0
                dve.wait_ge(unit_done, n + 1)
                x1 = F1[:, bass.ds(X1 + d, 1), :].rearrange("p o t -> p (o t)")
                nc.vector.tensor_tensor(x1, pair((base + k) % 3), x1, ALU.add).then_inc(x1_ready, 1)
                dve.wait_ge(x1sq_ready, d + 1)
                if not isinstance(d, int) or d:
                    dve.wait_ge(acc1_ready, d)
                nc.vector.tensor_tensor(ACC, ACC, SQ[0], ALU.add).then_inc(acc1_ready, 1)

            split_lo(dve, 24, 0, 0, 0)
            residual(OUT0, 0, 0, 0)
            residual(OUT0 + 1, 0, 0, 0)
            with dve.Fori(0, 2) as i:
                for k in range(3):
                    residual(OUT0 + 2, 3, i, k)
            norm_dve(dve, steps, 2, D)
            dve.wait_ge(rb_ready, 3)
            for k in range(KT):
                if k > 1:
                    dve.wait_ge(h_lo_ready, KT + k - 1)
                nc.vector.scalar_tensor_tensor(F1[:, k % 2, :], F1[:, X1 + k, :], par(P_GFFN + k), pair(3),
                                               ALU.mult, ALU.mult).then_inc(h_ready, 1)

            def gated(base, coef, i, k, e, f, par_pair):
                _, _, n = at(base, coef, i, k)
                split_lo(dve, base + 2, coef, i, k)
                dve.wait_ge(g_tap, f + 1)
                gate = pair(2 * e)
                steps.add(nc.vector.scalar_tensor_tensor(T1[e][:, 1:], gate[:, 0:T - 1], par(P_FCW + 3 * f + 1),
                                                         T1[e][:, 1:], ALU.mult, ALU.add))
                steps.settle()
                nc.vector.scalar_tensor_tensor(T1[e][:, 2:], gate[:, 0:T - 2], par(P_FCW + 3 * f), T1[e][:, 2:],
                                               ALU.mult, ALU.add).then_inc(taps_ready, 1)
                split_lo(dve, base + 2, coef, i, k + 1)
                dve.wait_ge(unit_done, n + 2)
                dve.wait_ge(silu_ready, f + 1)
                nc.vector.tensor_tensor(SA[e], SA[e], pair(2 * e + 1), ALU.mult).then_inc(a_ready, 1)
                dve.wait_ge(a_hi, f + 1)
                nc.vector.tensor_tensor(act_at(par_pair, e, 1), SA[e], f32(act_at(par_pair, e, 0)), ALU.subtract)\
                    .then_inc(a_lo, 1)

            def add_down(d, counted, n):
                if d < KT - 1:
                    dve.wait_ge(down_done, counted + d + 1)
                else:
                    dve.wait_ge(unit_done, n)
                x1 = F1[:, X1 + d, :]
                nc.vector.tensor_tensor(x1, pair(DOWN_PAIRS[d]), x1, ALU.add).then_inc(down_added, 1)

            for e in range(2):
                gated(FFN0, 0, 0, 2 * e, e, e, 0)
            with dve.Fori(0, 5) as i:
                steps.enter(i, 5, 4)
                for s in range(2):
                    base = FFN0 + 4 + 6 * s
                    for e in range(2):
                        gated(base, 12, i, 2 * e, e, 4 * i + 2 * s + 2 + e, (s + 1) % 2)
                    split_lo(dve, base + 2, 12, i, 4)
                    for d in range(KT):
                        add_down(d, (KT - 1) * (2 * i + s), base + 12 * i + 6)
                    split_lo(dve, base + 2, 12, i, 5)
                steps.leave()
            dve.wait_ge(acc_clear, 3)
            for d in range(KT + 1):
                if d < KT:
                    add_down(d, (KT - 1) * 10, N_UNITS)
                if d:
                    dve.wait_ge(x2sq_ready, d)
                    if d > 1:
                        dve.wait_ge(acc2_ready, d - 1)
                    nc.vector.tensor_tensor(ACC, ACC, SQ[(d - 1) % 2], ALU.add).then_inc(acc2_ready, 1)
            norm_dve(dve, steps, 3, D)
            dve.wait_ge(rb_ready, 4)
            for k in range(KT):
                nc.vector.scalar_tensor_tensor(F1[:, X1 + k, :], F1[:, X1 + k, :], par(P_GFIN + k), pair(3),
                                               ALU.mult, ALU.mult).then_inc(out_ready, 1)

        @block.tensor
        def _(pe):
            pe.wait_ge(consts_in, 32)
            pe.wait_ge(acc_ready, KT - 1)
            norm_sums(F1[:, 10, :])
            norm_spread(pe, 0)
            arrives = lambda kt: pe.wait_ge(h_lo_ready, kt + 1)
            with pe.Fori(0, CONV_T) as i:
                unit_matmuls(pe, 0, 3, i, 0, 0, h_hi, h_lo, arrives=arrives)
                unit_matmuls(pe, 1, 3, i, 0, 1, h_hi, h_lo)
                unit_matmuls(pe, 2, 3, i, 0, 2, h_hi, h_lo)
            pe.wait_ge(u_ready, CONV_T)
            unit_matmuls(pe, 12, 0, 0, 0, 0, h_hi, h_lo)
            pe.wait_ge(accy_ready, CONV_T)
            norm_sums(F1[:, ACCY, :])
            pe.wait_ge(cu_ready, CONV_T)
            unit_matmuls(pe, 13, 0, 0, 0, 1, h_hi, h_lo)
            norm_spread(pe, 1)
            pe.wait_ge(y_ready, CONV_T)
            with pe.Fori(0, 3) as i:
                for k in range(3):
                    unit_matmuls(pe, 14, 3, i, k, (14 + k) % 3, h_hi, h_lo)
            pe.wait_ge(qkv_ready, N_QKV)
            for t in range(TT):
                last = nc.tensor.transpose(PS[:, 4 + t // 4, (t % 4) * P:(t % 4 + 1) * P], F1[:, GATE, t * P:(t + 1) * P],
                                           ident)
            last.then_inc(gt_ready, 1)
            pe.wait_ge(w1_in, 16)
            pe.wait_ge(late_in, 16)
            pe.wait_ge(masks_in, 16)
            pe.wait_ge(mc_lo, CONV_T)
            for kv in range(2):
                for l in range(CMP_BLOCK // 2):
                    c = (P_POSK, P_POSV)[kv] + l
                    last = nc.tensor.matmul(PS[:, 6, kv:kv + 1], W1C[:, kv, l, :], params[:, c:c + 1], start=l == 0,
                                            stop=l == CMP_BLOCK // 2 - 1)
            last.then_inc(pos_ready, 1)
            pe.wait_ge(gexp_ready, 1)
            pe.wait_ge(posb_ready, 1)
            pe.wait_ge(ak_in, 16)
            pe.wait_ge(clear_ready, 5)
            with pe.Fori(0, KV) as g:
                def compressed_hidden(kv, src):
                    pe.wait_ge(ck_ready, 4 * g + 2 * kv + 2)
                    for l in range(CMP_BLOCK // 2):
                        last = nc.tensor.matmul(PS[:, 6 + kv, 0:NCMP], W1C[:, kv, l, :],
                                                src[:, 2 * l:2 * l + CMP_STRIDE * (NCMP - 1) + 1:CMP_STRIDE],
                                                start=l == 0, stop=l == CMP_BLOCK // 2 - 1)
                    last.then_inc(hid_ready, 1)

                compressed_hidden(0, CK)
                pe.wait_ge(gelu_ready, 2 * g + 1)
                nc.tensor.matmul(PS[0:DH, 6, P:P + NCMP], w2c[:, 0, :], hidc[:, 0, 0:NCMP], start=True, stop=True)\
                    .then_inc(kvc_ready, 1)
                pe.wait_ge(aq_in, 16 * g + 16)
                pe.wait_ge(k_lo, 4 * g + 4)

                def scores(out, h, i, key, count, masked):
                    nc.tensor.matmul(out[:, 0:count], QA[:, i, h, :], KA[:, key:key + count], start=True, stop=False)
                    last = nc.tensor.matmul(out[:, 0:count], QB[0:DH + AR, i, h, :], KB[0:DH + AR, key:key + count],
                                            start=False, stop=not masked)
                    for n, (col, m, w) in enumerate(masked):
                        last = nc.tensor.matmul(out[:, col:col + w], masks[:, M_ID:M_ID + P], masks[:, m:m + w],
                                                start=False, stop=n == len(masked) - 1)
                    return last

                def unit_scores(bank, h, i, key, width, masked):
                    for c in range(0, width, BANK):
                        inside = [(col - c, m, w) for col, m, w in masked if c <= col < c + BANK]
                        last = scores(PS[:, bank + c // BANK, :], h, i, key + c, min(BANK, KEYS - key - c), inside)
                    return last

                for b in range(NR):
                    h, i = ROWS[b]
                    bank = 4 * (b % 2)
                    cmp_mask = M_CMP + i * P + P - CW
                    if i == 0:
                        pe.wait_ge(q_lo, 2 * GROUP * g + 2 * h + 2)
                    if b < 2:
                        pe.wait_ge(kc_lo, 2 * g + 1)
                    else:
                        pe.wait_ge(max_a, NR * g + b - 1)
                    lead = CW * CMP_FIRST[i]
                    unit_scores(bank, h, i, KSEL - lead, lead + P * (i + 1),
                                ([(0, cmp_mask, CW)] if lead else []) + [(lead + i * P, M_DIAG, P)]).then_inc(sa_ready, 1)
                    if b > 1:
                        pe.wait_ge(max_b, NR * g + b - 1)
                    j0 = max(0, i - WT)
                    last = unit_scores(bank + 2, h, i, KWIN + j0 * P, P * (i + 1 - j0),
                                       ([(0, M_EDGE, P)] if i >= WT else []) + [((i - j0) * P, M_DIAG, P)])
                    if not CMP_FIRST[i]:
                        col = CMP_IN_B[i] - BANK
                        last = scores(PS[:, bank + 3, col:col + CW], h, i, KCMP, CW, [(0, cmp_mask, CW)])
                    last.then_inc(sb_ready, 1)
                pe.wait_ge(max_a, NR * g + NR)
                pe.wait_ge(max_b, NR * g + NR)
                nc.tensor.transpose(PS[0:96, 0, 0:P], nmax[:, :, :, :].rearrange("p b i h -> p (b i h)"), ident)\
                    .then_inc(mt_ready, 1)

                pe.wait_ge(v_copied, g + 1)
                for t in range(TT):
                    last = nc.tensor.transpose(PS[:, 4 + t // 4, (t % 4) * P:(t % 4 + 1) * P], RB[:, t * P:(t + 1) * P],
                                               ident)
                last.then_inc(vt_ready, 1)
                compressed_hidden(1, CV)
                pe.wait_ge(gelu_ready, 2 * g + 2)
                nc.tensor.matmul(PS[0:NCMP, 7, P:P + DH], hidc[:, 1, 0:NCMP], w2c[:, 1, :], start=True, stop=True)\
                    .then_inc(kvc_ready, 1)
                pe.wait_ge(m_in, 96 * g + 96)

                def key_scores(s):
                    i, br, j = STEPS[s]
                    if s > 3:
                        pe.wait_ge(e_ready, NS * g + s - 3)
                    out, key = PS[:, s % 4, :], (KSEL, KWIN, 0)[br] + j * P
                    cols = slice(key, key + P)
                    flat = lambda q: q.rearrange("p h q -> p (h q)")
                    mask = {0: M_DIAG if j == i else None,
                            1: M_DIAG if j == i else M_EDGE if j == i - WT else None,
                            2: M_CMP + i * P}[br]
                    nc.tensor.matmul(out, KA[:, cols], flat(QA[:, i, :, :]), start=True, stop=False)
                    last = nc.tensor.matmul(out, KB[0:DH + AR + MR, cols], flat(QB[0:DH + AR + MR, i, :, :]),
                                            start=False, stop=mask is None)
                    if mask is not None:
                        last = nc.tensor.matmul(out, masks[:, mask:mask + P], masks[:, M_ID:M_ID + GROUP * P],
                                                start=False, stop=True)
                    last.then_inc(st_ready, 1)

                def values(s):
                    i, br, j = STEPS[s]
                    pe.wait_ge(pt_lo, NS * g + s + 1)
                    first, end = s == 0 or STEPS[s - 1][:2] != (i, br), s + 1 in ENDS
                    number = 3 * i + br
                    if first and number > 1:
                        pe.wait_ge(ot_copied, 3 * TT * g + number - 1)
                    n, out = (0, TT, 2 * TT)[br] + j, PS[0:DH + 1, 4 + number % 2, :]
                    nc.tensor.matmul(out, VH[:, n, 0:DH + 1], PTH[s % 4], start=first, stop=False)
                    nc.tensor.matmul(out, VL[:, n, 0:DH + 1], PTH[s % 4], start=False, stop=False)
                    nc.tensor.matmul(out, VH[:, n, 0:DH + 1], PTL[s % 4], start=False, stop=end).then_inc(pv_done, 1)

                def turn(i):
                    pe.wait_ge(ot_copied, 3 * (TT * g + i + 1))
                    if i:
                        pe.wait_ge(o_ready, TT * g + i)
                    for n in range(3 * GROUP):
                        last = nc.tensor.transpose(PS[:, 6 + n // 6, (n % 6) * VW:(n % 6) * VW + DH + 1],
                                                   OT[n // GROUP][:, (n % GROUP) * P:(n % GROUP + 1) * P],
                                                   ident[0:DH + 1, 0:DH + 1])
                    last.then_inc(ot_turned, 1)

                key_scores(0)
                key_scores(1)
                key_scores(2)
                pe.wait_ge(v_lo, g + 1)
                pe.wait_ge(kc_lo, 2 * g + 2)
                for s in range(NS):
                    if s + 3 < NS:
                        key_scores(s + 3)
                    values(s)
                    if s in STEP_OF_TURN:
                        turn(STEP_OF_TURN.index(s))
                turn(TT - 1)
                pe.wait_ge(o_ready, TT * g + TT)
            for k in range(4):
                pe.wait_ge(on_ready, TT)
                for t in range(TT):
                    last = nc.tensor.transpose(PS[:, 2 * k + t // 4, (t % 4) * P:(t % 4 + 1) * P],
                                               F1[:, k, t * P:(t + 1) * P], ident)
                last.then_inc(ot_ready, 1)
            order = [4, 5, 6, 7, 0, 1, 2, 3]
            pe.wait_ge(ma_lo, 4)
            unit_matmuls(pe, OUT0, 0, 0, 0, OUT0 % 3, m_hi, m_lo, order)
            unit_matmuls(pe, OUT0 + 1, 0, 0, 0, (OUT0 + 1) % 3, m_hi, m_lo, order)
            with pe.Fori(0, 2) as i:
                for k in range(3):
                    unit_matmuls(pe, OUT0 + 2, 3, i, k, (OUT0 + 2 + k) % 3, m_hi, m_lo, order)
            pe.wait_ge(acc1_ready, N_OUT)
            norm_sums(ACC)
            norm_spread(pe, 2)
            arrives = lambda kt: pe.wait_ge(h_lo_ready, KT + kt + 1)
            pe.wait_ge(x1_ready, N_OUT)
            for k in range(4):
                unit_matmuls(pe, FFN0, 0, 0, k, k, h_hi, h_lo, arrives=arrives if k == 0 else None)

            def down(base, coef, i, k, par_pair, pairs_read, counted, before):
                units = [at(base, coef, i, k + a) for a in range(2)]
                pe.wait_ge(unit_lo, units[1][2] + 1)
                for d in range(KT):
                    p = DOWN_PAIRS[d]
                    if d in (0, 4):
                        pe.wait_ge(a_ready, pairs_read[d // 4])
                    if d in (2, 3, 6, 7):
                        pe.wait_ge(down_added, before + d - 1)
                    for a in range(2):
                        w_h, w_l = (w[:, units[a][0], d * P:(d + 1) * P] for w in (wh, wl))
                        for h in range(HALVES):
                            out, cols = PS[:, 2 * p + h, :], slice(h * BANK, (h + 1) * BANK)
                            nc.tensor.matmul(out, w_h, act_at(par_pair, a, 0)[:, cols], start=a == 0, stop=False)
                            nc.tensor.matmul(out, w_h, act_at(par_pair, a, 1)[:, cols], start=False, stop=False)
                        for h in range(HALVES):
                            out, cols = PS[:, 2 * p + h, :], slice(h * BANK, (h + 1) * BANK)
                            last = nc.tensor.matmul(out, w_l, act_at(par_pair, a, 0)[:, cols], start=False, stop=a == 1)
                        if d == KT - 1:
                            last.then_inc(unit_done, 1)
                    if d < KT - 1:
                        last.then_inc(down_done, 1)

            with pe.Fori(0, 5) as i:
                for s in range(2):
                    base = FFN0 + 4 + 6 * s
                    f = 4 * i + 2 * s + 2
                    for k in range(4):
                        if k % 2 == 0:
                            pe.wait_ge(a_ready, f - 2 + k // 2 + 1)
                        unit_matmuls(pe, base, 12, i, k, k, h_hi, h_lo)
                    pe.wait_ge(a_lo, f)
                    down(base, 12, i, 4, s % 2, (f + 1, f + 2), (KT - 1) * (2 * i + s), KT * (2 * i + s))
            pe.wait_ge(a_lo, FT)
            down(N_UNITS - 2, 0, 0, 0, 0, (FT, FT), (KT - 1) * 10, KT * 10)
            pe.wait_ge(acc2_ready, KT)
            norm_sums(ACC)
            norm_spread(pe, 3)


_W = [512] + [128] * 6 + [24] + [512] * 3
_OFF = [int(v) for v in np.cumsum([0] + _W)]


def _unit_columns():
    q, kc, vc, ks, vs, kw, vw, gl, bg, cg, u = _OFF[:-1]
    out = []
    for j in range(CONV_T):
        out += [range(o + j * P, o + (j + 1) * P) for o in (u, cg, bg)]
    out += [range(q + j * P, q + (j + 1) * P) for j in range(4)]
    out.append([gl + 3 * (g * GROUP + h) + b for g in range(KV) for b in (1, 2, 0) for h in range(GROUP)]
               + [-1] * (P - 3 * HEADS))
    for g in range(KV):
        for a, b in ((ks, kw), (vs, vw), (kc, vc)):
            out.append([a + g * DH + d for d in range(DH)] + [b + g * DH + d for d in range(DH)])
    return [list(c) for c in out]


def _blocks(w):
    return w.reshape(KT, P, P).transpose(1, 0, 2).reshape(P, KT * P)


def _shape_constants():
    consts = np.zeros((P, NCON), np.float32)
    consts[:, C_ID:C_ID + P] = np.eye(P)
    consts[:, C_ONE:C_ONE + P] = 1.0
    t = np.arange(T).reshape(TT, P).T
    consts[:, C_VALID:C_VALID + TT] = t >= CMP_BLOCK - 1
    m = np.zeros((P, NMASK), np.float32)
    q, k = np.arange(P)[:, None], np.arange(P)[None, :]
    m[:, M_ID:M_ID + GROUP * P] = np.tile(np.eye(P), (1, GROUP))
    m[:, M_DIAG:M_DIAG + P] = np.where(k > q, NEG, 0.0)
    m[:, M_EDGE:M_EDGE + P] = np.where(k <= q, NEG, 0.0)
    n = np.arange(P)[None, :] - (P - CW)
    for i in range(TT):
        sees = (n >= 0) & (n < NCMP) & (CMP_STRIDE * n + CMP_BLOCK - 1 <= i * P + q)
        m[:, M_CMP + i * P:M_CMP + (i + 1) * P] = np.where(sees, 0.0, NEG)
    aq = np.zeros((HEADS, AR, T), np.float32)
    tok = np.arange(T)
    for h in range(HEADS):
        slope = 2.0 ** (-8.0 * (h + 1) / HEADS)
        aq[h, 0] = slope
        aq[h, 1] = -slope * (tok % P)
        for j in range(TT):
            aq[h, 2 + j] = P * slope * (j - tok // P)
    aq = aq.reshape(KV, GROUP, AR, TT, P).transpose(0, 2, 3, 1, 4).reshape(KV, AR, GROUP * T)
    ak = np.zeros((AR + MR, P + 2 * T), np.float32)
    pos = np.concatenate([CMP_STRIDE * np.arange(NCMP) + CMP_BLOCK - 1, [-1], tok, tok])
    seen, s = pos >= 0, np.maximum(pos, 0)
    ak[0, P - CW:] = seen * (s % P)
    ak[1, P - CW:] = seen
    for j in range(TT):
        ak[2 + j, P - CW:] = seen & (s // P == j)
    for br, cols in enumerate((slice(P, P + T), slice(P + T, P + 2 * T), slice(0, P))):
        ak[[AR + br, AR + 3 + br], cols] = 1.0
    return consts, m, aq, ak


def kernel(x, norm_mix_g, w_in, pos_ck, w_ck1, w_ck2, pos_cv, w_cv1, w_cv2, conv_mix_w, norm_out_attn_g,
           norm_out_conv_g, w_out, norm_ffn_g, w_gate, w_up, ffn_conv_w, ffn_conv_b, w_down, norm_final_g):
    import concourse.bacc as bacc
    from concourse.bass_utils import run_bass_kernel_spmd

    A = np.ascontiguousarray
    w_in, w_out, w_gate, w_up, w_down = (np.asarray(a)[0] for a in (w_in, w_out, w_gate, w_up, w_down))
    padded = np.concatenate([w_in, np.zeros((D, 1), np.float32)], axis=1)
    units = [_blocks(padded[:, c]) for c in _unit_columns()]
    units += [_blocks(w_out[:, d * P:(d + 1) * P]) for d in range(N_OUT)]
    for pr in range(FT // 2 + 1):
        if pr < FT // 2:
            for f in (2 * pr, 2 * pr + 1):
                units += [_blocks(w_gate[:, f * P:(f + 1) * P]), _blocks(w_up[:, f * P:(f + 1) * P])]
        if pr:
            units += [w_down[f * P:(f + 1) * P] for f in (2 * pr - 2, 2 * pr - 1)]
    cols = lambda a, n: np.asarray(a).reshape(n, P).T
    taps = lambda a, n: np.asarray(a)[0].reshape(3, n, P).transpose(2, 1, 0).reshape(P, 3 * n)
    params = np.concatenate([cols(norm_mix_g, 8), cols(norm_out_attn_g, 4), cols(norm_out_conv_g, 4),
                             cols(norm_ffn_g, 8), cols(norm_final_g, 8), taps(conv_mix_w, CONV_T), taps(ffn_conv_w, FT),
                             cols(ffn_conv_b, FT), cols(pos_ck, 16), cols(pos_cv, 16)], axis=1)
    first = lambda a: np.asarray(a)[0].reshape(16, P, P).transpose(1, 0, 2).reshape(P, 2, 1024)
    consts, masks, aq, ak = _shape_constants()
    arrays = {
        "xT": A(np.asarray(x)[0].T.reshape(KT, P, T)),
        "w_units": A(np.stack(units)),
        "w_cmp1": A(np.concatenate([first(w_ck1), first(w_cv1)], axis=1)),
        "w_cmp2": A(np.stack([np.asarray(w_ck2)[0], np.asarray(w_cv2)[0]], axis=1)),
        "params": A(params), "consts": consts, "masks": masks, "alibi_q": A(aq), "alibi_k": ak,
    }
    nc = bacc.Bacc("TRN2", target_bir_lowering=False, num_devices=1)
    args = [nc.dram_tensor("in_" + n, a.shape, mybir.dt.from_np(a.dtype), kind="ExternalInput").ap() for n, a in arrays.items()]
    args.append(nc.dram_tensor("outT", (KT, P, T), F32, kind="ExternalOutput").ap())
    hybrid_layer(nc, *args)
    r = run_bass_kernel_spmd(nc, [{"in_" + n: a for n, a in arrays.items()}], core_ids=[0])
    return A(r.results[0]["outT"].reshape(D, T).T).reshape(1, T, D)
```

```python
import numpy as np
import concourse.bass as bass
from concourse import mybir
from contextlib import ExitStack

F32 = mybir.dt.float32
F32R = mybir.dt.float32r
BF16 = mybir.dt.bfloat16
ALU = mybir.AluOpType
ACT = mybir.ActivationFunctionType
AX = mybir.AxisListType

P = 128
D = 1024
T = 1024
KT = D // P
TT = T // P
BANK = 512
HALVES = T // BANK
HEADS, KV, DH = 8, 2, 64
GROUP = HEADS // KV
DFF = 2816
FT = DFF // P
CMP_BLOCK, CMP_STRIDE = 32, 16
NCMP = (T - CMP_BLOCK) // CMP_STRIDE + 1
CW = 64
WINDOW = 512
WT = WINDOW // P
SEL_BLOCK, SEL_TOPK = 64, 16
assert T // SEL_BLOCK <= SEL_TOPK
CONV_T = 4
EPS = 1e-6
NEG = -1e30
AR = 10
MR = 6

N_CONV = 3 * CONV_T
N_QKV = HEADS * DH // P + 3 * KV + 1
N_IN = N_CONV + N_QKV
N_OUT = D // P
OUT0 = N_IN
FFN0 = OUT0 + N_OUT
N_UNITS = FFN0 + 3 * FT
RING = 3

P_GMIX, P_GOUT, P_GFFN, P_GFIN = 0, 8, 16, 24
P_CONV = 32
P_FCW = P_CONV + 3 * CONV_T
P_FCB = P_FCW + 3 * FT
P_POSK = P_FCB + FT
P_POSV = P_POSK + CMP_BLOCK // 2
NPAR = P_POSV + CMP_BLOCK // 2
C_ID, C_ONE, C_VALID = 0, P, 2 * P
NCON = 2 * P + TT
M_ID, M_DIAG, M_EDGE, M_CMP = 0, GROUP * P, (GROUP + 1) * P, (GROUP + 2) * P
NMASK = M_CMP + TT * P


class Steps:

    def __init__(self, eng, sem):
        self.eng, self.sem, self.base, self.local, self.stack = eng, sem, 0, 0, []

    def add(self, ins):
        ins.then_inc(self.sem, 1)
        self.local += 1

    def settle(self):
        self.eng.wait_ge(self.sem, self.base + self.local)

    def enter(self, i, trips, per):
        start = self.base + self.local
        self.stack.append((start, trips, per))
        self.base, self.local = start + per * i, 0

    def leave(self):
        start, trips, per = self.stack.pop()
        assert self.local == per, (self.local, per)
        self.base, self.local = start, per * trips


def key_tiles(i):
    return [(0, j) for j in range(i + 1)] + [(1, j) for j in range(max(0, i - WT), i + 1)] + [(2, 0)]


STEPS = [(i, br, j) for i in range(TT) for br, j in key_tiles(i)]
NS = len(STEPS)


def hybrid_layer(nc, xT, w_units, w_cmp1, w_cmp2, params_d, consts_d, masks_d, alibi_q, alibi_k, outT):
    with ExitStack() as ctx:
        def sb(name, shape, dt=F32):
            return ctx.enter_context(nc.sbuf_tensor(name, shape, dt))

        def sem(name):
            return ctx.enter_context(nc.semaphore(name))

        params = sb("params", [P, NPAR])
        consts = sb("consts", [P, NCON])
        masks = sb("masks", [P, NMASK], BF16)
        w2c = sb("w2c", [P, 2, DH])
        raw = sb("raw", [P, RING, 1024])
        wh = sb("wh", [P, RING, 1024], F32R)
        wl = sb("wl", [P, RING, 1024], F32R)
        F1 = sb("F1", [P, 15, 1024])
        R1 = sb("R1", [P, 16, 1024], F32R)
        R2 = sb("R2", [P, 8, 1024], F32R)
        PBm = sb("PBm", [P, 2, 768])
        small = sb("small", [P, 56])
        head_ss = sb("head_ss", [P, KV * TT])
        gates = sb("gates", [P, TT, 3 * HEADS])
        nmax = sb("nmax", [P, 3, TT, GROUP])
        coef = sb("coef", [P, 2, 3 * GROUP])
        hidc = sb("hidc", [P, 2, CW])
        posb = sb("posb", [P, 2])
        PS = ctx.enter_context(nc.psum_tensor("PS", [P, 8, BANK], F32))

        def par(c, n=1):
            return params[:, c:c + n] if isinstance(c, int) else params[:, bass.ds(c, n)]

        ident = consts[:, C_ID:C_ID + P]
        ones = consts[:, C_ONE:C_ONE + P]

        def pair(p):
            return PS[:, 2 * p:2 * p + 2, :].rearrange("p a b -> p (a b)")

        Q0, GATE, KV0, Y0, X1 = 0, 4, 5, 11, 5
        U_S, CU_S, CT_S, SQ_S, ACCY = 5, 6, 7, 8, 9
        RF = R1[:, :, :].rearrange("p a b -> p (a b)")
        KCMP, KSEL, KWIN, KEYS = 64, P, P + T, P + 2 * T
        at_r = [0]

        def piece(n):
            at_r[0] += n
            return RF[:, at_r[0] - n:at_r[0]]

        QA = piece(GROUP * T).rearrange("p (i h q) -> p i h q", h=GROUP, q=P)
        QB = piece(GROUP * T).rearrange("p (i h q) -> p i h q", h=GROUP, q=P)
        KA, KB = piece(KEYS), piece(KEYS)
        NV, VW = 2 * TT + 1, DH + 2
        VH = piece(NV * VW).rearrange("p (j d) -> p j d", d=VW)
        VL = piece(NV * VW).rearrange("p (j d) -> p j d", d=VW)
        MH, ML = piece(P), piece(P)
        EB, PTH, PTL = ([buf[:, b // 2, 512 * (b % 2):512 * (b % 2 + 1)] for b in range(4)] for buf in (raw, wh, wl))
        OT = [PBm[:, :, :].rearrange("p a b -> p (a b)")[0:DH + 1, 512 * br:512 * (br + 1)] for br in range(3)]
        RB = PBm[:, :, :].rearrange("p a b -> p (a b)")[:, 0:1024]
        CK, CV = raw[:, 1, :], raw[:, 2, :]
        W1C = F1[:, Y0:Y0 + 4, :].rearrange("p a b -> p (a b)").rearrange("p (k l h) -> p k l h", k=2, l=16)
        OSUM = F1[:, GATE, 0:3 * GROUP * DH]
        SQ_HEADS = F1[:, GATE, 3 * GROUP * DH:].rearrange("p (a b) -> p a b", a=2)

        def f32(ap):
            return ap.bitcast(F32)

        consts_in, late_in, w1_in, ak_in = sem("consts_in"), sem("late_in"), sem("w1_in"), sem("ak_in")
        masks_in = sem("masks_in")
        x_in, aq_in = [sem(f"x_in{k}") for k in range(KT)], sem("aq_in")
        x1_in, out_done = sem("x1_in"), sem("out_done")
        unit_in = [sem(f"unit_in{s}") for s in range(RING)]
        unit_hi, unit_lo, unit_done = sem("unit_hi"), sem("unit_lo"), sem("unit_done")
        dve_step = sem("dve_step")
        sq_ready, acc_ready = sem("sq_ready"), sem("acc_ready")
        ss_ready, ss_read, rt_ready, diag_ready, rb_ready = (sem("ss_ready"), sem("ss_read"), sem("rt_ready"),
                                                             sem("diag_ready"), sem("rb_ready"))
        h_ready, h_hi_ready, h_lo_ready = sem("h_ready"), sem("h_hi_ready"), sem("h_lo_ready")
        v_copied, clear_ready, acc_clear = sem("v_copied"), sem("clear_ready"), sem("acc_clear")
        u_ready, cu_ready, tap_ready, y_ready, ysq_ready, accy_ready = (
            sem("u_ready"), sem("cu_ready"), sem("tap_ready"), sem("y_ready"), sem("ysq_ready"), sem("accy_ready"))
        yn_ready, mc_hi, mc_lo = sem("yn_ready"), sem("mc_hi"), sem("mc_lo")
        qkv_ready = sem("qkv_ready")
        gt_ready, gexp_ready, gates_ready = sem("gt_ready"), sem("gexp_ready"), sem("gates_ready")
        pos_ready, posb_ready = sem("pos_ready"), sem("posb_ready")
        ck_ready, hid_ready, gelu_ready, kvc_ready = sem("ck_ready"), sem("hid_ready"), sem("gelu_ready"), sem("kvc_ready")
        vt_ready, v_hi, v_lo, k_hi, k_lo, kc_hi, kc_lo = (sem("vt_ready"), sem("v_hi"), sem("v_lo"), sem("k_hi"),
                                                        sem("k_lo"), sem("kc_hi"), sem("kc_lo"))
        q_hi, q_lo = sem("q_hi"), sem("q_lo")
        sa_ready, sb_ready, max_a, max_b = sem("sa_ready"), sem("sb_ready"), sem("max_a"), sem("max_b")
        mt_ready, mt_hi, mt_lo, m_in = sem("mt_ready"), sem("mt_hi"), sem("mt_lo"), sem("m_in")
        st_ready, e_ready, pt_hi, pt_lo, pv_done = (sem("st_ready"), sem("e_ready"), sem("pt_hi"), sem("pt_lo"),
                                                    sem("pv_done"))
        ot_copied, win_copied, ot_turned = sem("ot_copied"), sem("win_copied"), sem("ot_turned")
        o_scaled, o_pair, o_ready = sem("o_scaled"), sem("o_pair"), sem("o_ready")
        osq_ready, on_ready, ot_ready, ma_hi, ma_lo = (sem("osq_ready"), sem("on_ready"), sem("ot_ready"),
                                                       sem("ma_hi"), sem("ma_lo"))
        x1_ready, x1sq_ready, acc1_ready = sem("x1_ready"), sem("x1sq_ready"), sem("acc1_ready")
        g_tap, taps_ready, silu_ready, a_ready, a_hi, a_lo = (sem("g_tap"), sem("taps_ready"), sem("silu_ready"),
                                                              sem("a_ready"), sem("a_hi"), sem("a_lo"))
        down_done, down_added = sem("down_done"), sem("down_added")
        x2sq_ready, acc2_ready, og_ready, out_ready = (sem("x2sq_ready"), sem("acc2_ready"), sem("og_ready"),
                                                       sem("out_ready"))

        def at(base, coef, i, k):
            return (base + k) % RING, (base + k) // RING + (coef // RING) * i + 1, base + k + coef * i

        def norm_sums(acc, column=0, whole=True):
            for t in range(TT):
                last = nc.tensor.matmul(PS[:, 6, column + t:column + t + 1], acc[:, t * P:(t + 1) * P], ones[:, 0:1],
                                        start=True, stop=True)
            if whole:
                last.then_inc(ss_ready, 1)

        def norm_spread(pe, m):
            pe.wait_ge(diag_ready, m + 1)
            for h in range(HALVES):
                last = nc.tensor.matmul(PS[:, 6 + h, :], ones, RB[:, h * BANK:(h + 1) * BANK],
                                        start=True, stop=True)
            last.then_inc(rb_ready, 1)

        def norm_act(act, m):
            act.wait_ge(ss_read, m + 1 + (m > 1))
            nc.scalar.activation(small[:, 8:16], small[:, 0:8], ACT.Sqrt).then_inc(rt_ready, 1)

        def norm_dve(dve, steps, m, width, parts=1):
            dve.wait_ge(ss_ready, m + 1)
            sums = PS[:, 6, 0:8]
            if parts == 2:
                sums = small[:, 0:8]
                steps.add(nc.vector.tensor_reduce(sums, PS[:, 6, 0:16].rearrange("p (a t) -> p t a", a=2), AX.X, ALU.add))
                steps.settle()
            nc.vector.tensor_scalar(small[:, 0:8], sums, 1.0 / width, EPS, ALU.mult, ALU.add).then_inc(ss_read, 1)
            dve.wait_ge(rt_ready, m + 1 + (m > 1))
            newton(steps)
            nc.vector.tensor_tensor(RB.rearrange("p (t q) -> p t q", t=TT),
                                    ident.rearrange("p (o q) -> p o q", o=1).broadcast_to([P, TT, P]),
                                    small[:, 24:32].rearrange("p (t o) -> p t o", o=1).broadcast_to([P, TT, P]),
                                    ALU.mult).then_inc(diag_ready, 1)

        def newton(steps):
            v, root, r, rr, vrr, f, out = (small[:, c:c + 8] for c in (0, 8, 16, 32, 40, 48, 24))
            for ins in (lambda: nc.vector.reciprocal(r, root),
                        lambda: nc.vector.tensor_tensor(rr, r, r, ALU.mult),
                        lambda: nc.vector.tensor_tensor(vrr, rr, v, ALU.mult),
                        lambda: nc.vector.tensor_scalar(f, vrr, -0.5, 1.5, ALU.mult, ALU.add),
                        lambda: nc.vector.tensor_tensor(out, f, r, ALU.mult)):
                steps.add(ins())
                steps.settle()

        def load(sp, base, coef, i, k):
            slot, held, n = at(base, coef, i, k)
            sp.wait_ge(unit_lo, n - RING + 1)
            src = w_units[n] if isinstance(n, int) else w_units[bass.ds(n, 1), :, :].rearrange("o p n -> (o p) n")
            sp.dma_start(raw[:, slot, :], src).then_inc(unit_in[slot], 16)

        def split_hi(act, base, coef, i, k, free=False):
            slot, held, n = at(base, coef, i, k)
            act.wait_ge(unit_in[slot], 16 * held)
            if not free and (not isinstance(n, int) or n >= RING):
                act.wait_ge(unit_done, n - RING + 1)
            nc.scalar.activation(wh[:, slot, :], raw[:, slot, :], ACT.Copy).then_inc(unit_hi, 1)

        def split_lo(dve, base, coef, i, k, free=False):
            slot, held, n = at(base, coef, i, k)
            dve.wait_ge(unit_hi, n + 1)
            if not free and (not isinstance(n, int) or n >= RING):
                dve.wait_ge(unit_done, n - RING + 1)
            nc.vector.tensor_tensor(wl[:, slot, :], raw[:, slot, :], f32(wh[:, slot, :]), ALU.subtract)\
                .then_inc(unit_lo, 1)

        def unit_tile(slot, p, hi, lo, kt, first, end):
            w_h, w_l = wh[:, slot, kt * P:(kt + 1) * P], wl[:, slot, kt * P:(kt + 1) * P]
            for h in range(HALVES):
                out, cols = PS[:, 2 * p + h, :], slice(h * BANK, (h + 1) * BANK)
                nc.tensor.matmul(out, w_h, hi(kt)[:, cols], start=first, stop=False)
                nc.tensor.matmul(out, w_h, lo(kt)[:, cols], start=False, stop=False)
            for h in range(HALVES):
                out, cols = PS[:, 2 * p + h, :], slice(h * BANK, (h + 1) * BANK)
                last = nc.tensor.matmul(out, w_l, hi(kt)[:, cols], start=False, stop=end)
            return last

        def unit_matmuls(pe, base, coef, i, k, p, hi, lo, order=range(KT), part=None):
            slot, held, n = at(base, coef, i, k)
            pe.wait_ge(unit_lo, n + 1)
            for kt in part or order:
                last = unit_tile(slot, p, hi, lo, kt, kt == order[0], kt == order[-1])
            if kt == order[-1]:
                last.then_inc(unit_done, 1)

        def two_units(pe, n, h_count):
            pe.wait_ge(unit_lo, n + 2)
            for kt in range(KT):
                pe.wait_ge(h_lo_ready, h_count + kt + 1)
                for a in range(2):
                    last = unit_tile((n + a) % RING, a, h_hi, h_lo, kt, kt == 0, kt == KT - 1)
                    if kt == KT - 1:
                        last.then_inc(unit_done, 1)

        h_hi, h_lo = (lambda k: R1[:, k, :]), (lambda k: R1[:, 8 + k, :])
        m_hi = lambda k: R1[:, k, :] if k < 4 else R2[:, k - 4, :]
        m_lo = lambda k: R1[:, 4 + k, :] if k < 4 else R2[:, k, :]

        OT_PAIRS = [(OUT0 + 2) % 3, 3] * 2

        ROWS = [(h, i) for h in range(GROUP) for i in range(TT)]
        NR = len(ROWS)
        CMP_FIRST = [(i + 1) % 4 != 0 for i in range(TT)]
        CMP_IN_B = [BANK + (P if i >= WT else 0) for i in range(TT)]
        ENDS = [s + 1 for s in range(NS) if s + 1 == NS or STEPS[s + 1][:2] != STEPS[s][:2]]
        STEP_OF_TURN = [ENDS[3 * i + 2] + 2 for i in range(TT)]

        def act_at(par, e, part):
            return R2[:, 4 * par + 2 * e + part, :]

        T1 = [F1[:, 0, :], F1[:, 1, :]]
        SA = [F1[:, 2, :], F1[:, 3, :]]
        ACC = F1[:, 4, :]
        SQ = [F1[:, 13, :], F1[:, 14, :]]
        DOWN_PAIRS = [0, 1, 0, 1, 2, 3, 2, 3]

        block = ctx.enter_context(nc.Block())

        @block.sync
        def _(sp):
            sp.dma_start(F1[:, 0, :], xT[0]).then_inc(x_in[0], 16)
            for k in range(1, KT):
                sp.dma_start(F1[:, k, :], xT[k]).then_inc(x_in[k], 16)
            sp.dma_start(consts[:, :], consts_d).then_inc(consts_in, 16)
            sp.dma_start(params[:, :], params_d).then_inc(consts_in, 16)
            for n in range(RING):
                sp.dma_start(raw[:, n, :], w_units[n]).then_inc(unit_in[n], 16)
            sp.dma_start(w2c[:, :, :], w_cmp2).then_inc(late_in, 16)
            with sp.Fori(0, 4) as i:
                for k in range(3):
                    load(sp, 3, 3, i, k)
            with sp.Fori(0, 3) as i:
                for k in range(3):
                    load(sp, 15, 3, i, k)
            sp.wait_ge(mc_lo, CONV_T)
            sp.dma_start(F1[:, Y0:Y0 + 4, :], w_cmp1).then_inc(w1_in, 16)
            with sp.Fori(0, KV) as g:
                for part, src, done in ((0, MH, mt_hi), (1, ML, mt_lo)):
                    sp.wait_ge(done, g + 1)
                    for br in range(3):
                        row = DH + AR + 3 * part + br
                        sp.dma_start(f32(QB[row:row + 1, :, :, :]).rearrange("o i h q -> o (i h) q"),
                                     f32(src[32 * br:32 * br + 32, :])).then_inc(m_in, 16)
            sp.wait_ge(k_hi, 2 * KV)
            sp.wait_ge(k_lo, 4 * KV)
            sp.wait_ge(v_copied, KV)
            sp.wait_ge(ck_ready, 4 * KV)
            sp.wait_ge(hid_ready, 2 * KV)
            for k in range(KT):
                sp.dma_start(F1[:, X1 + k, :], xT[k]).then_inc(x1_in, 16)
            sp.wait_ge(pt_lo, KV * NS)
            load(sp, 24, 0, 0, 0)
            load(sp, 25, 0, 0, 0)
            load(sp, 26, 0, 0, 0)
            with sp.Fori(0, (N_UNITS - 28) // 3) as i:
                for k in range(3):
                    load(sp, 27, 3, i, k)
            load(sp, N_UNITS - 1, 0, 0, 0)
            for k in range(KT):
                sp.wait_ge(out_ready, k + 1)
                sp.dma_start(outT[k], F1[:, X1 + k, :]).then_inc(out_done, 16)
            sp.wait_ge(out_done, 16 * KT)

        @block.gpsimd
        def _(pool):
            pool.wait_ge(ss_ready, 1)
            nc.gpsimd.memset(F1[:, ACCY, :], 0.0).then_inc(acc_clear, 1)
            for k in range(KT):
                pool.wait_ge(h_hi_ready, k + 1)
                nc.gpsimd.tensor_tensor(h_lo(k), F1[:, k, :], f32(h_hi(k)), ALU.subtract).then_inc(h_lo_ready, 1)
            pool.dma_start(masks[:, :], masks_d).then_inc(masks_in, 16)
            pool.wait_ge(unit_done, N_IN)
            for pad, value in ((KA[:, 0:P], 0.0), (KB[0:DH, 0:P], 0.0), (VH, 0.0), (VL, 0.0)):
                nc.gpsimd.memset(f32(pad), value).then_inc(clear_ready, 1)
            pool.wait_ge(clear_ready, 4)
            nc.gpsimd.memset(f32(VH[:, :, DH:DH + 1]), 1.0).then_inc(clear_ready, 1)
            pool.dma_start(KB[DH:DH + AR + MR, :], alibi_k).then_inc(ak_in, 16)
            with pool.Fori(0, KV) as g:
                pool.dma_start(QB[DH:DH + AR, :, :, :].rearrange("r i h q -> r (i h q)"),
                               alibi_q[bass.ds(g, 1)].rearrange("o r n -> (o r) n")).then_inc(aq_in, 16)
                w = GROUP * DH
                for i in range(TT):
                    pool.wait_ge(o_scaled, TT * g + i + 1)
                    nc.gpsimd.tensor_tensor(OSUM[:, 0:w], OSUM[:, 0:w], OSUM[:, w:2 * w], ALU.add).then_inc(o_pair, 1)
                    pool.wait_ge(o_pair, TT * g + i + 1)
                    nc.gpsimd.tensor_tensor(F1[:, bass.ds(Q0 + 2 * g, 2), i * P:(i + 1) * P],
                                            OSUM[:, 0:w].rearrange("p (a b) -> p a b", a=2),
                                            OSUM[:, 2 * w:3 * w].rearrange("p (a b) -> p a b", a=2), ALU.add)\
                        .then_inc(o_ready, 1)
                pool.wait_ge(o_ready, TT * g + TT)
            pool.wait_ge(osq_ready, KV * TT)
            nc.gpsimd.memset(ACC, 0.0).then_inc(acc_clear, 1)
            for k in range(KT):
                pool.wait_ge(h_hi_ready, KT + k + 1)
                nc.gpsimd.tensor_tensor(h_lo(k), F1[:, k % 2, :], f32(h_hi(k)), ALU.subtract).then_inc(h_lo_ready, 1)
            nc.gpsimd.memset(ACC, 0.0).then_inc(acc_clear, 1)

        @block.scalar
        def _(act):
            for k in range(KT):
                act.wait_ge(x_in[k], 16)
                if k > 2:
                    act.wait_ge(acc_ready, k - 2)
                dst = F1[:, 10, :] if k == 0 else F1[:, 8 + k % 2, :]
                nc.scalar.activation(dst, F1[:, k, :], ACT.Square).then_inc(sq_ready, 1)
            norm_act(act, 0)
            split_hi(act, 0, 0, 0, 0)
            split_hi(act, 1, 0, 0, 0)
            for k in range(KT):
                act.wait_ge(h_ready, k + 1)
                nc.scalar.activation(h_hi(k), F1[:, k, :], ACT.Copy).then_inc(h_hi_ready, 1)
            with act.Fori(0, CONV_T) as i:
                split_hi(act, 2, 3, i, 0, free=True)
                act.wait_ge(unit_done, 3 * i + 1)
                nc.scalar.activation(F1[:, U_S, :], pair(0), ACT.Copy).then_inc(u_ready, 1)
                split_hi(act, 3, 3, i, 0)
                act.wait_ge(cu_ready, i + 1)
                nc.scalar.activation(F1[:, CT_S, :], F1[:, CU_S, :], ACT.Copy, scale=par(P_CONV + 3 * i + 2))\
                    .then_inc(tap_ready, 1)
                split_hi(act, 4, 3, i, 0)
                act.wait_ge(y_ready, i + 1)
                nc.scalar.activation(F1[:, SQ_S, :], F1[:, bass.ds(Y0 + i, 1), :].rearrange("p o t -> p (o t)"),
                                     ACT.Square).then_inc(ysq_ready, 1)

            def evac(base, coef, i, k, slot):
                _, _, n = at(base, coef, i, k)
                act.wait_ge(unit_done, n + 1)
                nc.scalar.activation(slot, pair(n_pair(base + k)), ACT.Copy).then_inc(qkv_ready, 1)

            n_pair = lambda n: n % 3
            split_hi(act, 14, 0, 0, 0)
            evac(12, 0, 0, 0, F1[:, 0, :])
            norm_act(act, 1)
            split_hi(act, 15, 0, 0, 0)
            evac(13, 0, 0, 0, F1[:, 1, :])
            for k in range(CONV_T):
                act.wait_ge(yn_ready, k + 1)
                nc.scalar.activation(R2[:, k, :], F1[:, Y0 + k, :], ACT.Copy).then_inc(mc_hi, 1)
            with act.Fori(0, 2) as i:
                for k in range(3):
                    split_hi(act, 16, 3, i, k)
                    evac(14, 3, i, k, F1[:, bass.ds(3 * i + k + 2, 1), :].rearrange("p o t -> p (o t)"))
            for n in range(20, 23):
                if n + 2 < 24:
                    split_hi(act, n + 2, 0, 0, 0)
                evac(n, 0, 0, 0, F1[:, n - 12, :])
            act.wait_ge(gt_ready, 1)
            nc.scalar.activation(gates[:, :, :], PS[:, 4:6, :].rearrange("p a (b c) -> p (a b) c", c=P)[:, :, 0:3 * HEADS],
                                 ACT.Exp, scale=-1.0).then_inc(gexp_ready, 1)
            act.wait_ge(clear_ready, 5)
            act.wait_ge(unit_lo, N_IN + 1)
            with act.Fori(0, KV) as g:
                def kv_rows(what, half):
                    return F1[half * DH:(half + 1) * DH, bass.ds(KV0 + 3 * g + what, 1), :].rearrange("p o t -> p (o t)")

                def to_compress(dst, half):
                    nc.scalar.activation(dst[0:DH, :], kv_rows(2, half), ACT.Copy).then_inc(ck_ready, 1)
                    nc.scalar.activation(dst[DH:P, 0:T - 1], kv_rows(2, half)[:, 1:T], ACT.Copy).then_inc(ck_ready, 1)

                def hidden(kv):
                    act.wait_ge(hid_ready, 2 * g + kv + 1)
                    act.wait_ge(posb_ready, 1)
                    nc.scalar.activation(hidc[:, kv, 0:NCMP], PS[:, 6 + kv, 0:NCMP], ACT.Gelu_apprx_tanh,
                                         bias=posb[:, kv:kv + 1]).then_inc(gelu_ready, 1)

                def queries(h):
                    rows = slice((h % 2) * DH, (h % 2 + 1) * DH)
                    src = F1[rows, bass.ds(Q0 + 2 * g + h // 2, 1), :].rearrange("p o (i q) -> p (o i) q", q=P)
                    for dst in (QA[rows, :, h, :], QB[0:DH, :, h, :]):
                        nc.scalar.activation(dst, src, ACT.Copy, scale=DH ** -0.5).then_inc(q_hi, 1)

                to_compress(CK, 0)
                for half in range(2):
                    nc.scalar.activation(KA[half * DH:(half + 1) * DH, KSEL + half * T:KSEL + (half + 1) * T], kv_rows(0, half),
                                         ACT.Copy).then_inc(k_hi, 1)
                queries(0)
                hidden(0)
                act.wait_ge(kvc_ready, 2 * g + 1)
                for rows in (slice(0, DH), slice(DH, P)):
                    nc.scalar.activation(KA[rows, KCMP:KCMP + NCMP], PS[0:DH, 6, P:P + NCMP], ACT.Copy)\
                        .then_inc(kc_hi, 1)
                for h in range(1, GROUP):
                    queries(h)
                nc.scalar.activation(RB, F1[:, bass.ds(KV0 + 3 * g + 1, 1), :].rearrange("p o t -> p (o t)"), ACT.Copy)\
                    .then_inc(v_copied, 1)
                to_compress(CV, 1)
                act.wait_ge(mt_ready, g + 1)
                nc.scalar.activation(MH[0:96, :], PS[0:96, 0, 0:P], ACT.Copy).then_inc(mt_hi, 1)
                act.wait_ge(vt_ready, g + 1)
                nc.scalar.activation(VH[:, 0:2 * TT, 0:DH].rearrange("p (b j) d -> p b j d", b=2),
                                     pair(2).rearrange("p (j b d) -> p b j d", b=2, d=DH), ACT.Copy).then_inc(v_hi, 1)
                hidden(1)
                act.wait_ge(kvc_ready, 2 * g + 2)
                nc.scalar.activation(VH[KCMP:KCMP + NCMP, 2 * TT, 0:DH], PS[0:NCMP, 7, P:P + DH], ACT.Copy).then_inc(kc_hi, 1)

                for s in range(NS + 3):
                    if s < NS:
                        act.wait_ge(st_ready, NS * g + s + 1)
                        if s > 3:
                            act.wait_ge(pv_done, NS * g + s - 3)
                        nc.scalar.activation(PTH[s % 4], PS[:, s % 4, :], ACT.Exp).then_inc(pt_hi, 1)
                        nc.scalar.activation(EB[s % 4], PS[:, s % 4, :], ACT.Exp).then_inc(e_ready, 1)
                    if s - 2 in ENDS and ENDS.index(s - 2) % 3 == 1:
                        n = ENDS.index(s - 2)
                        act.wait_ge(pv_done, NS * g + s - 2)
                        if n > 1:
                            act.wait_ge(ot_turned, TT * g + n // 3)
                        nc.scalar.activation(OT[1], PS[0:DH + 1, 4 + n % 2, :], ACT.Copy).then_inc(win_copied, 1)
                    if s - 5 in STEP_OF_TURN:
                        i = STEP_OF_TURN.index(s - 5)
                        act.wait_ge(o_ready, TT * g + i + 1)
                        nc.scalar.activation(SQ_HEADS, F1[:, bass.ds(Q0 + 2 * g, 2), i * P:(i + 1) * P], ACT.Square,
                                             accum_out=head_ss[:, bass.ds(TT * g + i, 1)]).then_inc(osq_ready, 1)
                act.wait_ge(pv_done, NS * g + NS)
            split_hi(act, 24, 0, 0, 0, free=True)
            for g in range(KV):
                act.wait_ge(o_ready, TT * g + TT)
                act.wait_ge(osq_ready, KV * (TT - 1) + g)
                nc.scalar.activation(SQ_HEADS, F1[:, Q0 + 2 * g:Q0 + 2 * g + 2, T - P:T], ACT.Square,
                                     accum_out=head_ss[:, TT * g + TT - 1:TT * g + TT]).then_inc(osq_ready, 1)
            act.wait_ge(ss_read, 3)
            nc.scalar.activation(small[:, 8:16], small[:, 0:8], ACT.Sqrt).then_inc(rt_ready, 1)
            for k in range(4):
                act.wait_ge(ot_ready, k + 1)
                nc.scalar.activation(m_hi(k), pair(OT_PAIRS[k]), ACT.Copy, scale=par(P_GOUT + k)).then_inc(ma_hi, 1)

            def residual_square(base, coef, i, k):
                split_hi(act, base + 2, coef, i, k)
                _, _, n = at(base, coef, i, k)
                d = n - OUT0
                act.wait_ge(x1_ready, d + 1)
                if not isinstance(d, int) or d:
                    act.wait_ge(acc1_ready, d)
                nc.scalar.activation(SQ[0], F1[:, bass.ds(X1 + d, 1), :].rearrange("p o t -> p (o t)"), ACT.Square)\
                    .then_inc(x1sq_ready, 1)

            residual_square(OUT0, 0, 0, 0)
            with act.Fori(0, 2) as i:
                for k in range(3):
                    residual_square(OUT0 + 1, 3, i, k)
            residual_square(OUT0 + 7, 0, 0, 0)
            norm_act(act, 2)
            for k in range(KT):
                act.wait_ge(h_ready, KT + k + 1)
                nc.scalar.activation(h_hi(k), F1[:, k % 2, :], ACT.Copy).then_inc(h_hi_ready, 1)

            def gated(base, coef, i, k, e, f, par_pair, down):
                _, _, n = at(base, coef, i, k)
                split_hi(act, base + 2, coef, i, k)
                act.wait_ge(unit_done, n + 1)
                nc.scalar.activation(T1[e], pair(2 * e), ACT.Identity, scale=par(P_FCW + 3 * f + 2), bias=par(P_FCB + f))\
                    .then_inc(g_tap, 1)
                split_hi(act, base + 2, coef, i, k + 1)
                act.wait_ge(taps_ready, f + 1)
                if not isinstance(f, int) or f > 1:
                    act.wait_ge(a_lo, f - 1)
                nc.scalar.activation(SA[e], T1[e], ACT.Silu).then_inc(silu_ready, 1)
                act.wait_ge(a_ready, f + 1)
                if down is not None:
                    act.wait_ge(unit_done, down)
                nc.scalar.activation(act_at(par_pair, e, 0), SA[e], ACT.Copy).then_inc(a_hi, 1)

            for e in range(2):
                gated(FFN0, 0, 0, 2 * e, e, e, 0, None)
            with act.Fori(0, 5) as i:
                for s in range(2):
                    base = FFN0 + 4 + 6 * s
                    for e in range(2):
                        gated(base, 12, i, 2 * e, e, 4 * i + 2 * s + 2 + e, (s + 1) % 2, base + 12 * i)
                    split_hi(act, base + 2, 12, i, 4)
                    split_hi(act, base + 2, 12, i, 5)
            for k in range(KT):
                act.wait_ge(down_added, 10 * KT + k + 1)
                if k > 1:
                    act.wait_ge(acc2_ready, k - 1)
                nc.scalar.activation(SQ[k % 2], F1[:, X1 + k, :], ACT.Square).then_inc(x2sq_ready, 1)
            norm_act(act, 3)

        @block.vector
        def _(dve):
            steps = Steps(dve, dve_step)
            for k in range(1, KT):
                dve.wait_ge(sq_ready, k + 1)
                if k > 1:
                    dve.wait_ge(acc_ready, k - 1)
                nc.vector.tensor_tensor(F1[:, 10, :], F1[:, 10, :], F1[:, 8 + k % 2, :], ALU.add).then_inc(acc_ready, 1)
            dve.wait_ge(consts_in, 32)
            norm_dve(dve, steps, 0, D)
            split_lo(dve, 0, 0, 0, 0)
            split_lo(dve, 1, 0, 0, 0)
            dve.wait_ge(rb_ready, 1)
            for k in range(KT):
                nc.vector.scalar_tensor_tensor(F1[:, k, :], F1[:, k, :], par(P_GMIX + k), pair(3), ALU.mult, ALU.mult)\
                    .then_inc(h_ready, 1)
            dve.wait_ge(acc_clear, 1)
            with dve.Fori(0, CONV_T) as i:
                steps.enter(i, CONV_T, 2)
                y = F1[:, bass.ds(Y0 + i, 1), :].rearrange("p o t -> p (o t)")
                cu, tap = F1[:, CU_S, :], F1[:, CT_S, :]
                split_lo(dve, 2, 3, i, 0, free=True)
                dve.wait_ge(u_ready, i + 1)
                dve.wait_ge(unit_done, 3 * i + 2)
                nc.vector.tensor_tensor(cu, pair(1), F1[:, U_S, :], ALU.mult).then_inc(cu_ready, 1)
                split_lo(dve, 3, 3, i, 0)
                dve.wait_ge(tap_ready, i + 1)
                dve.wait_ge(cu_ready, i + 1)
                for lag in (1, 2):
                    steps.add(nc.vector.scalar_tensor_tensor(tap[:, lag:], cu[:, 0:T - lag], par(P_CONV + 3 * i + 2 - lag),
                                                             tap[:, lag:], ALU.mult, ALU.add))
                    steps.settle()
                split_lo(dve, 4, 3, i, 0)
                dve.wait_ge(unit_done, 3 * i + 3)
                nc.vector.tensor_tensor(y, pair(2), tap, ALU.mult).then_inc(y_ready, 1)
                dve.wait_ge(ysq_ready, i + 1)
                nc.vector.tensor_tensor(F1[:, ACCY, :], F1[:, ACCY, :], F1[:, SQ_S, :], ALU.add).then_inc(accy_ready, 1)
                steps.leave()
            split_lo(dve, 14, 0, 0, 0)
            norm_dve(dve, steps, 1, CONV_T * P)
            split_lo(dve, 15, 0, 0, 0)
            dve.wait_ge(rb_ready, 2)
            for k in range(CONV_T):
                nc.vector.scalar_tensor_tensor(F1[:, Y0 + k, :], F1[:, Y0 + k, :], par(P_GOUT + 4 + k), pair(3),
                                               ALU.mult, ALU.mult).then_inc(yn_ready, 1)
            for k in range(CONV_T):
                dve.wait_ge(mc_hi, k + 1)
                nc.vector.tensor_tensor(R2[:, 4 + k, :], F1[:, Y0 + k, :], f32(R2[:, k, :]), ALU.subtract)\
                    .then_inc(mc_lo, 1)
            with dve.Fori(0, 2) as i:
                for k in range(3):
                    split_lo(dve, 16, 3, i, k)
            for n in range(22, 24):
                split_lo(dve, n, 0, 0, 0)
            dve.wait_ge(gexp_ready, 1)
            steps.add(nc.vector.tensor_scalar_add(gates[:, :, :], gates[:, :, :], 1.0))
            steps.settle()
            steps.add(nc.vector.reciprocal(gates[:, :, :], gates[:, :, :]))
            steps.settle()
            for g in range(KV):
                g3 = gates[:, :, (3 * g + 2) * GROUP:(3 * g + 3) * GROUP]
                steps.add(nc.vector.tensor_tensor(g3, g3, consts[:, C_VALID:C_VALID + TT]
                                                  .rearrange("p (t o) -> p t o", o=1).broadcast_to([P, TT, GROUP]),
                                                  ALU.mult))
            steps.settle()
            dve.wait_ge(pos_ready, 1)
            nc.vector.tensor_copy(posb[:, :], PS[:, 7, BANK // 2:BANK // 2 + 2]).then_inc(posb_ready, 1)
            with dve.Fori(0, KV) as g:
                steps.enter(g, KV, 2 * TT)
                for half in range(2):
                    rows, other = slice(half * DH, (half + 1) * DH), slice((1 - half) * DH, (2 - half) * DH)
                    cols = slice(KSEL + half * T, KSEL + (half + 1) * T)
                    dve.wait_ge(k_hi, 2 * g + half + 1)
                    nc.vector.tensor_copy(KA[other, cols], f32(KA[rows, cols])).then_inc(k_lo, 1)
                    nc.vector.tensor_tensor(KB[0:DH, cols],
                                            F1[rows, bass.ds(KV0 + 3 * g, 1), :].rearrange("p o t -> p (o t)"),
                                            f32(KA[rows, cols]), ALU.subtract).then_inc(k_lo, 1)

                def queries(h, tiles):
                    e = h % 2
                    rows, other = slice(e * DH, (e + 1) * DH), slice((1 - e) * DH, (2 - e) * DH)
                    dve.wait_ge(q_hi, 2 * GROUP * g + 2 * h + 1)
                    nc.vector.scalar_tensor_tensor(QA[other, tiles, h, :],
                                                   F1[rows, bass.ds(Q0 + 2 * g + h // 2, 1), :]
                                                   .rearrange("p o (i q) -> p (o i) q", q=P)[:, tiles, :],
                                                   DH ** -0.5, f32(QA[rows, tiles, h, :]), ALU.mult, ALU.subtract)\
                        .then_inc(q_lo, 1)

                early, late = slice(0, TT // 2), slice(TT // 2, TT)
                queries(0, early)
                queries(0, late)
                dve.wait_ge(kc_hi, 3 * g + 2)
                nc.vector.tensor_tensor(KB[0:DH, KCMP:KCMP + NCMP], PS[0:DH, 6, P:P + NCMP],
                                        f32(KA[0:DH, KCMP:KCMP + NCMP]), ALU.subtract).then_inc(kc_lo, 1)

                def max_of(b, br, unit, col, count):
                    h, i = ROWS[b]
                    return nc.vector.tensor_reduce(nmax[:, br, i, h:h + 1],
                                                   pair(2 * (b % 2) + unit)[:, col:col + count], AX.X, ALU.max,
                                                   negate=True)

                for b in range(NR):
                    h, i = ROWS[b]
                    if i in (2, 3) and h + 1 < GROUP:
                        queries(h + 1, early if i == 2 else late)
                    dve.wait_ge(sa_ready, NR * g + b + 1)
                    if CMP_FIRST[i]:
                        max_of(b, 2, 0, 0, CW)
                    max_of(b, 0, 0, CW * CMP_FIRST[i], P * (i + 1)).then_inc(max_a, 1)
                    dve.wait_ge(sb_ready, NR * g + b + 1)
                    if not CMP_FIRST[i]:
                        max_of(b, 2, 1, CMP_IN_B[i], CW)
                    max_of(b, 1, 1, 0, P * min(i + 1, WT + 1)).then_inc(max_b, 1)
                dve.wait_ge(mt_hi, g + 1)
                nc.vector.tensor_tensor(ML[0:96, :], PS[0:96, 0, 0:P], f32(MH[0:96, :]), ALU.subtract).then_inc(mt_lo, 1)
                dve.wait_ge(v_hi, g + 1)
                nc.vector.tensor_tensor(VL[:, 0:2 * TT, 0:DH].rearrange("p (b j) d -> p b j d", b=2),
                                        pair(2).rearrange("p (j b d) -> p b j d", b=2, d=DH),
                                        f32(VH[:, 0:2 * TT, 0:DH]).rearrange("p (b j) d -> p b j d", b=2),
                                        ALU.subtract).then_inc(v_lo, 1)
                dve.wait_ge(kc_hi, 3 * g + 3)
                nc.vector.tensor_tensor(VL[KCMP:KCMP + NCMP, 2 * TT, 0:DH], PS[0:NCMP, 7, P:P + DH],
                                        f32(VH[KCMP:KCMP + NCMP, 2 * TT, 0:DH]), ALU.subtract).then_inc(kc_lo, 1)

                turned = PS[:, 6:8, 0:6 * VW].rearrange("p a (n d) -> p a n d", d=VW)
                inverse, factor = coef[:, 0, :], coef[:, 1, :]

                def invert(i):
                    dve.wait_ge(ot_turned, TT * g + i + 1)
                    steps.add(nc.vector.reciprocal(inverse.rearrange("p (a n) -> p a n", a=2), turned[:, :, :, DH]))

                def weigh(i):
                    steps.settle()
                    steps.add(nc.vector.tensor_tensor(factor, inverse, gates[:, i, bass.ds(3 * GROUP * g, 3 * GROUP)],
                                                      ALU.mult))

                def scale(i):
                    steps.settle()
                    if i:
                        dve.wait_ge(o_ready, TT * g + i)
                    nc.vector.tensor_tensor(
                        OSUM.rearrange("p (a n d) -> p a n d", a=2, d=DH), turned[:, :, :, 0:DH],
                        factor.rearrange("p (a n o) -> p a n o", a=2, o=1).broadcast_to([P, 2, 6, DH]), ALU.mult)\
                        .then_inc(o_scaled, 1)

                for s in range(NS + 6):
                    if s < NS:
                        dve.wait_ge(e_ready, NS * g + s + 1)
                        nc.vector.tensor_tensor(PTL[s % 4], EB[s % 4], f32(PTH[s % 4]), ALU.subtract).then_inc(pt_lo, 1)
                    if s - 1 in ENDS and ENDS.index(s - 1) % 3 != 1:
                        n = ENDS.index(s - 1)
                        dve.wait_ge(pv_done, NS * g + s - 1)
                        if n and n % 3 == 0:
                            dve.wait_ge(ot_turned, TT * g + n // 3)
                        nc.vector.tensor_copy(OT[n % 3], PS[0:DH + 1, 4 + n % 2, :]).then_inc(ot_copied, 1)
                    for later, part in ((1, invert), (2, weigh), (3, scale)):
                        if s - later in STEP_OF_TURN:
                            part(STEP_OF_TURN.index(s - later))
                steps.leave()
            dve.wait_ge(osq_ready, KV * TT)
            steps.add(nc.vector.tensor_tensor(small[:, 0:8], head_ss[:, 0:TT], head_ss[:, TT:2 * TT], ALU.add))
            steps.settle()
            nc.vector.tensor_scalar(small[:, 0:8], small[:, 0:8], 1.0 / (HEADS * DH), EPS, ALU.mult, ALU.add)\
                .then_inc(ss_read, 1)
            split_lo(dve, 24, 0, 0, 0, free=True)
            dve.wait_ge(rt_ready, 3)
            newton(steps)
            for t in range(TT):
                o = F1[:, 0:4, t * P:(t + 1) * P]
                nc.vector.tensor_scalar(o, o, small[:, 24 + t:25 + t], None, ALU.mult).then_inc(on_ready, 1)
            for k in range(4):
                dve.wait_ge(ma_hi, k + 1)
                nc.vector.scalar_tensor_tensor(m_lo(k), pair(OT_PAIRS[k]), par(P_GOUT + k), f32(m_hi(k)), ALU.mult, ALU.subtract)\
                    .then_inc(ma_lo, 1)
            dve.wait_ge(x1_in, 16 * KT)
            dve.wait_ge(acc_clear, 2)

            def residual(base, coef, i, k, summed=True):
                split_lo(dve, base + 2, coef, i, k)
                _, _, n = at(base, coef, i, k)
                d = n - OUT0
                dve.wait_ge(unit_done, n + 1)
                x1 = F1[:, bass.ds(X1 + d, 1), :].rearrange("p o t -> p (o t)")
                nc.vector.tensor_tensor(x1, pair((base + k) % 3), x1, ALU.add).then_inc(x1_ready, 1)
                if not summed:
                    return
                dve.wait_ge(x1sq_ready, d + 1)
                if not isinstance(d, int) or d:
                    dve.wait_ge(acc1_ready, d)
                nc.vector.tensor_tensor(ACC, ACC, SQ[0], ALU.add).then_inc(acc1_ready, 1)

            residual(OUT0, 0, 0, 0)
            with dve.Fori(0, 2) as i:
                for k in range(3):
                    residual(OUT0 + 1, 3, i, k)
            residual(OUT0 + 7, 0, 0, 0, summed=False)
            norm_dve(dve, steps, 2, D, 2)
            dve.wait_ge(rb_ready, 3)
            for k in range(KT):
                if k > 1:
                    dve.wait_ge(h_lo_ready, KT + k - 1)
                nc.vector.scalar_tensor_tensor(F1[:, k % 2, :], F1[:, X1 + k, :], par(P_GFFN + k), pair(3),
                                               ALU.mult, ALU.mult).then_inc(h_ready, 1)

            def gated(base, coef, i, k, e, f, par_pair):
                _, _, n = at(base, coef, i, k)
                split_lo(dve, base + 2, coef, i, k)
                dve.wait_ge(g_tap, f + 1)
                gate = pair(2 * e)
                steps.add(nc.vector.scalar_tensor_tensor(T1[e][:, 1:], gate[:, 0:T - 1], par(P_FCW + 3 * f + 1),
                                                         T1[e][:, 1:], ALU.mult, ALU.add))
                steps.settle()
                nc.vector.scalar_tensor_tensor(T1[e][:, 2:], gate[:, 0:T - 2], par(P_FCW + 3 * f), T1[e][:, 2:],
                                               ALU.mult, ALU.add).then_inc(taps_ready, 1)
                split_lo(dve, base + 2, coef, i, k + 1)
                dve.wait_ge(unit_done, n + 2)
                dve.wait_ge(silu_ready, f + 1)
                nc.vector.tensor_tensor(SA[e], SA[e], pair(2 * e + 1), ALU.mult).then_inc(a_ready, 1)
                dve.wait_ge(a_hi, f + 1)
                nc.vector.tensor_tensor(act_at(par_pair, e, 1), SA[e], f32(act_at(par_pair, e, 0)), ALU.subtract)\
                    .then_inc(a_lo, 1)

            def add_down(d, counted, n):
                if d < KT - 1:
                    dve.wait_ge(down_done, counted + d + 1)
                else:
                    dve.wait_ge(unit_done, n)
                x1 = F1[:, X1 + d, :]
                nc.vector.tensor_tensor(x1, pair(DOWN_PAIRS[d]), x1, ALU.add).then_inc(down_added, 1)

            for e in range(2):
                gated(FFN0, 0, 0, 2 * e, e, e, 0)
            with dve.Fori(0, 5) as i:
                steps.enter(i, 5, 4)
                for s in range(2):
                    base = FFN0 + 4 + 6 * s
                    for e in range(2):
                        gated(base, 12, i, 2 * e, e, 4 * i + 2 * s + 2 + e, (s + 1) % 2)
                    split_lo(dve, base + 2, 12, i, 4)
                    for d in range(KT):
                        add_down(d, (KT - 1) * (2 * i + s), base + 12 * i + 6)
                    split_lo(dve, base + 2, 12, i, 5)
                steps.leave()
            dve.wait_ge(acc_clear, 3)
            for d in range(KT):
                add_down(d, (KT - 1) * 10, N_UNITS)
                if d:
                    dve.wait_ge(x2sq_ready, d)
                    if d > 1:
                        dve.wait_ge(acc2_ready, d - 1)
                    nc.vector.tensor_tensor(ACC, ACC, SQ[(d - 1) % 2], ALU.add).then_inc(acc2_ready, 1)
            norm_dve(dve, steps, 3, D, 2)
            dve.wait_ge(rb_ready, 4)
            for k in range(KT):
                nc.vector.scalar_tensor_tensor(F1[:, X1 + k, :], F1[:, X1 + k, :], par(P_GFIN + k), pair(3),
                                               ALU.mult, ALU.mult).then_inc(out_ready, 1)

        @block.tensor
        def _(pe):
            pe.wait_ge(consts_in, 32)
            pe.wait_ge(acc_ready, KT - 1)
            norm_sums(F1[:, 10, :])
            norm_spread(pe, 0)
            two_units(pe, 0, 0)
            unit_matmuls(pe, 2, 0, 0, 0, 2, h_hi, h_lo)
            with pe.Fori(1, CONV_T) as i:
                unit_matmuls(pe, 0, 3, i, 0, 0, h_hi, h_lo)
                unit_matmuls(pe, 1, 3, i, 0, 1, h_hi, h_lo)
                unit_matmuls(pe, 2, 3, i, 0, 2, h_hi, h_lo)
            pe.wait_ge(u_ready, CONV_T)
            unit_matmuls(pe, 12, 0, 0, 0, 0, h_hi, h_lo)
            pe.wait_ge(accy_ready, CONV_T)
            norm_sums(F1[:, ACCY, :])
            pe.wait_ge(cu_ready, CONV_T)
            unit_matmuls(pe, 13, 0, 0, 0, 1, h_hi, h_lo)
            norm_spread(pe, 1)
            pe.wait_ge(y_ready, CONV_T)
            with pe.Fori(0, 3) as i:
                for k in range(3):
                    unit_matmuls(pe, 14, 3, i, k, (14 + k) % 3, h_hi, h_lo)
            pe.wait_ge(qkv_ready, N_QKV - 2)
            for t in range(TT):
                last = nc.tensor.transpose(PS[:, 4 + t // 4, (t % 4) * P:(t % 4 + 1) * P], F1[:, GATE, t * P:(t + 1) * P],
                                           ident)
            last.then_inc(gt_ready, 1)
            pe.wait_ge(w1_in, 16)
            pe.wait_ge(late_in, 16)
            pe.wait_ge(masks_in, 16)
            pe.wait_ge(mc_lo, CONV_T)
            for kv in range(2):
                for l in range(CMP_BLOCK // 2):
                    c = (P_POSK, P_POSV)[kv] + l
                    last = nc.tensor.matmul(PS[:, 7, BANK // 2 + kv:BANK // 2 + kv + 1], W1C[:, kv, l, :], params[:, c:c + 1], start=l == 0,
                                            stop=l == CMP_BLOCK // 2 - 1)
            last.then_inc(pos_ready, 1)
            pe.wait_ge(gexp_ready, 1)
            pe.wait_ge(ak_in, 16)
            pe.wait_ge(clear_ready, 5)
            with pe.Fori(0, KV) as g:
                def compressed_hidden(kv, src):
                    pe.wait_ge(ck_ready, 4 * g + 2 * kv + 2)
                    for l in range(CMP_BLOCK // 2):
                        last = nc.tensor.matmul(PS[:, 6 + kv, 0:NCMP], W1C[:, kv, l, :],
                                                src[:, 2 * l:2 * l + CMP_STRIDE * (NCMP - 1) + 1:CMP_STRIDE],
                                                start=l == 0, stop=l == CMP_BLOCK // 2 - 1)
                    last.then_inc(hid_ready, 1)

                compressed_hidden(0, CK)
                pe.wait_ge(gelu_ready, 2 * g + 1)
                nc.tensor.matmul(PS[0:DH, 6, P:P + NCMP], w2c[:, 0, :], hidc[:, 0, 0:NCMP], start=True, stop=True)\
                    .then_inc(kvc_ready, 1)
                pe.wait_ge(aq_in, 16 * g + 16)
                pe.wait_ge(k_lo, 4 * g + 4)

                def scores(bank, col, h, i, key, count, masked):
                    out = PS[:, bank, col:col + count]
                    nc.tensor.matmul(out, QA[:, i, h, :], KA[:, key:key + count], start=True, stop=False)
                    nc.tensor.matmul(out, QB[0:DH + AR, i, h, :], KB[0:DH + AR, key:key + count], start=False,
                                     stop=not masked)

                def unit_scores(bank, h, i, key, width, masked_cols):
                    for c in range(0, width, BANK):
                        scores(bank + c // BANK, 0, h, i, key + c, min(BANK, KEYS - key - c),
                               any(c <= col < c + BANK for col in masked_cols))

                def mask(bank, col, m, w, last=True):
                    out = PS[:, bank + col // BANK, col % BANK:col % BANK + w]
                    return nc.tensor.matmul(out, masks[:, M_ID:M_ID + P], masks[:, m:m + w], start=False, stop=last)

                for b in range(NR):
                    h, i = ROWS[b]
                    bank = 4 * (b % 2)
                    cmp_mask = M_CMP + i * P + P - CW
                    if i == 0:
                        pe.wait_ge(q_hi, 2 * GROUP * g + 2 * h + 2)
                        pe.wait_ge(q_lo, 2 * GROUP * g + 2 * h + 2)
                    if b < 2:
                        pe.wait_ge(kc_lo, 2 * g + 1)
                    else:
                        pe.wait_ge(max_a, NR * g + b - 1)
                    lead = CW * CMP_FIRST[i]
                    a_diag = lead + i * P
                    unit_scores(bank, h, i, KSEL - lead, lead + P * (i + 1), [0, a_diag] if lead else [a_diag])
                    if b > 1:
                        pe.wait_ge(max_b, NR * g + b - 1)
                    j0 = max(0, i - WT)
                    b_diag = (i - j0) * P
                    unit_scores(bank + 2, h, i, KWIN + j0 * P, b_diag + P, [0, b_diag] if i >= WT else [b_diag])
                    if lead:
                        mask(bank, 0, cmp_mask, CW, last=a_diag >= BANK)
                    mask(bank, a_diag, M_DIAG, P).then_inc(sa_ready, 1)
                    if i >= WT:
                        mask(bank + 2, 0, M_EDGE, P)
                    last = mask(bank + 2, b_diag, M_DIAG, P)
                    if not lead:
                        scores(bank + 3, CMP_IN_B[i] - BANK, h, i, KCMP, CW, True)
                        last = mask(bank + 2, CMP_IN_B[i], cmp_mask, CW)
                    last.then_inc(sb_ready, 1)
                pe.wait_ge(max_a, NR * g + NR)
                pe.wait_ge(max_b, NR * g + NR)
                nc.tensor.transpose(PS[0:96, 0, 0:P], nmax[:, :, :, :].rearrange("p b i h -> p (b i h)"), ident)\
                    .then_inc(mt_ready, 1)

                pe.wait_ge(v_copied, g + 1)
                for t in range(TT):
                    last = nc.tensor.transpose(PS[:, 4 + t // 4, (t % 4) * P:(t % 4 + 1) * P], RB[:, t * P:(t + 1) * P],
                                               ident)
                last.then_inc(vt_ready, 1)
                compressed_hidden(1, CV)
                pe.wait_ge(gelu_ready, 2 * g + 2)
                nc.tensor.matmul(PS[0:NCMP, 7, P:P + DH], hidc[:, 1, 0:NCMP], w2c[:, 1, :], start=True, stop=True)\
                    .then_inc(kvc_ready, 1)
                pe.wait_ge(m_in, 96 * g + 96)

                def key_scores(s):
                    i, br, j = STEPS[s]
                    if s > 3:
                        pe.wait_ge(e_ready, NS * g + s - 3)
                    out, key = PS[:, s % 4, :], (KSEL, KWIN, 0)[br] + j * P
                    cols = slice(key, key + P)
                    flat = lambda q: q.rearrange("p h q -> p (h q)")
                    mask = {0: M_DIAG if j == i else None,
                            1: M_DIAG if j == i else M_EDGE if j == i - WT else None,
                            2: M_CMP + i * P}[br]
                    nc.tensor.matmul(out, KA[:, cols], flat(QA[:, i, :, :]), start=True, stop=False)
                    last = nc.tensor.matmul(out, KB[0:DH + AR + MR, cols], flat(QB[0:DH + AR + MR, i, :, :]),
                                            start=False, stop=mask is None)
                    if mask is not None:
                        last = nc.tensor.matmul(out, masks[:, mask:mask + P], masks[:, M_ID:M_ID + GROUP * P],
                                                start=False, stop=True)
                    last.then_inc(st_ready, 1)

                def values(s):
                    i, br, j = STEPS[s]
                    pe.wait_ge(pt_lo, NS * g + s + 1)
                    first, end = s == 0 or STEPS[s - 1][:2] != (i, br), s + 1 in ENDS
                    number = 3 * i + br
                    if first and number > 1:
                        if number % 3 == 0:
                            pe.wait_ge(win_copied, TT * g + i)
                        else:
                            pe.wait_ge(ot_copied, 2 * (TT * g + i) + (number % 3 == 2))
                    n, out = (0, TT, 2 * TT)[br] + j, PS[0:DH + 1, 4 + number % 2, :]
                    nc.tensor.matmul(out, VH[:, n, 0:DH + 1], PTH[s % 4], start=first, stop=False)
                    nc.tensor.matmul(out, VL[:, n, 0:DH + 1], PTH[s % 4], start=False, stop=False)
                    nc.tensor.matmul(out, VH[:, n, 0:DH + 1], PTL[s % 4], start=False, stop=end).then_inc(pv_done, 1)

                def turn(i):
                    pe.wait_ge(ot_copied, 2 * (TT * g + i + 1))
                    pe.wait_ge(win_copied, TT * g + i + 1)
                    if i:
                        pe.wait_ge(o_scaled, TT * g + i)
                    for n in range(3 * GROUP):
                        last = nc.tensor.transpose(PS[:, 6 + n // 6, (n % 6) * VW:(n % 6) * VW + DH + 1],
                                                   OT[n // GROUP][:, (n % GROUP) * P:(n % GROUP + 1) * P],
                                                   ident[0:DH + 1, 0:DH + 1])
                    last.then_inc(ot_turned, 1)

                key_scores(0)
                key_scores(1)
                key_scores(2)
                pe.wait_ge(v_lo, g + 1)
                pe.wait_ge(kc_lo, 2 * g + 2)
                for s in range(NS + 3):
                    if s + 3 < NS:
                        key_scores(s + 3)
                    if s < NS:
                        values(s)
                    if s in STEP_OF_TURN:
                        turn(STEP_OF_TURN.index(s))
                pe.wait_ge(o_scaled, TT * g + TT)
            order = [4, 5, 6, 7, 0, 1, 2, 3]
            for n in (OUT0, OUT0 + 1):
                unit_matmuls(pe, n, 0, 0, 0, n % 3, m_hi, m_lo, order, order[:4])
            pe.wait_ge(on_ready, TT)
            for k in range(4):
                if k > 1:
                    pe.wait_ge(ma_lo, k - 1)
                for t in range(TT):
                    last = nc.tensor.transpose(PS[:, 2 * OT_PAIRS[k] + t // 4, (t % 4) * P:(t % 4 + 1) * P],
                                               F1[:, k, t * P:(t + 1) * P], ident)
                last.then_inc(ot_ready, 1)
            for kt in order[4:]:
                pe.wait_ge(ma_lo, kt + 1)
                for n in (OUT0, OUT0 + 1):
                    unit_matmuls(pe, n, 0, 0, 0, n % 3, m_hi, m_lo, order, [kt])
            with pe.Fori(0, 2) as i:
                for k in range(3):
                    unit_matmuls(pe, OUT0 + 2, 3, i, k, (OUT0 + 2 + k) % 3, m_hi, m_lo, order)
            pe.wait_ge(acc1_ready, N_OUT - 1)
            norm_sums(ACC, 8, whole=False)
            pe.wait_ge(x1sq_ready, N_OUT)
            norm_sums(SQ[0])
            norm_spread(pe, 2)
            pe.wait_ge(x1_ready, N_OUT)
            two_units(pe, FFN0, KT)
            for k in (2, 3):
                unit_matmuls(pe, FFN0, 0, 0, k, k, h_hi, h_lo)

            def down(base, coef, i, k, par_pair, pairs_read, counted, before):
                units = [at(base, coef, i, k + a) for a in range(2)]
                pe.wait_ge(unit_lo, units[1][2] + 1)
                for d in range(KT):
                    p = DOWN_PAIRS[d]
                    if d in (0, 4):
                        pe.wait_ge(a_ready, pairs_read[d // 4])
                    if d in (2, 3, 6, 7):
                        pe.wait_ge(down_added, before + d - 1)
                    for a in range(2):
                        w_h, w_l = (w[:, units[a][0], d * P:(d + 1) * P] for w in (wh, wl))
                        for h in range(HALVES):
                            out, cols = PS[:, 2 * p + h, :], slice(h * BANK, (h + 1) * BANK)
                            nc.tensor.matmul(out, w_h, act_at(par_pair, a, 0)[:, cols], start=a == 0, stop=False)
                            nc.tensor.matmul(out, w_h, act_at(par_pair, a, 1)[:, cols], start=False, stop=False)
                        for h in range(HALVES):
                            out, cols = PS[:, 2 * p + h, :], slice(h * BANK, (h + 1) * BANK)
                            last = nc.tensor.matmul(out, w_l, act_at(par_pair, a, 0)[:, cols], start=False, stop=a == 1)
                        if d == KT - 1:
                            last.then_inc(unit_done, 1)
                    if d < KT - 1:
                        last.then_inc(down_done, 1)

            with pe.Fori(0, 5) as i:
                for s in range(2):
                    base = FFN0 + 4 + 6 * s
                    f = 4 * i + 2 * s + 2
                    for k in range(4):
                        if k % 2 == 0:
                            pe.wait_ge(a_ready, f - 2 + k // 2 + 1)
                        unit_matmuls(pe, base, 12, i, k, k, h_hi, h_lo)
                    pe.wait_ge(a_lo, f)
                    down(base, 12, i, 4, s % 2, (f + 1, f + 2), (KT - 1) * (2 * i + s), KT * (2 * i + s))
            pe.wait_ge(a_lo, FT)
            down(N_UNITS - 2, 0, 0, 0, 0, (FT, FT), (KT - 1) * 10, KT * 10)
            pe.wait_ge(acc2_ready, KT - 1)
            norm_sums(ACC, 8, whole=False)
            pe.wait_ge(x2sq_ready, KT)
            norm_sums(SQ[(KT - 1) % 2])
            norm_spread(pe, 3)


_W = [512] + [128] * 6 + [24] + [512] * 3
_OFF = [int(v) for v in np.cumsum([0] + _W)]


def _unit_columns():
    q, kc, vc, ks, vs, kw, vw, gl, bg, cg, u = _OFF[:-1]
    out = []
    for j in range(CONV_T):
        out += [range(o + j * P, o + (j + 1) * P) for o in (u, cg, bg)]
    out += [range(q + j * P, q + (j + 1) * P) for j in range(4)]
    out.append([gl + 3 * (g * GROUP + h) + b for g in range(KV) for b in (1, 2, 0) for h in range(GROUP)]
               + [-1] * (P - 3 * HEADS))
    for g in range(KV):
        for a, b in ((ks, kw), (vs, vw), (kc, vc)):
            out.append([a + g * DH + d for d in range(DH)] + [b + g * DH + d for d in range(DH)])
    return [list(c) for c in out]


def _blocks(w):
    return w.reshape(KT, P, P).transpose(1, 0, 2).reshape(P, KT * P)


def _shape_constants():
    consts = np.zeros((P, NCON), np.float32)
    consts[:, C_ID:C_ID + P] = np.eye(P)
    consts[:, C_ONE:C_ONE + P] = 1.0
    t = np.arange(T).reshape(TT, P).T
    consts[:, C_VALID:C_VALID + TT] = t >= CMP_BLOCK - 1
    m = np.zeros((P, NMASK), np.float32)
    q, k = np.arange(P)[:, None], np.arange(P)[None, :]
    m[:, M_ID:M_ID + GROUP * P] = np.tile(np.eye(P), (1, GROUP))
    m[:, M_DIAG:M_DIAG + P] = np.where(k > q, NEG, 0.0)
    m[:, M_EDGE:M_EDGE + P] = np.where(k <= q, NEG, 0.0)
    n = np.arange(P)[None, :] - (P - CW)
    for i in range(TT):
        sees = (n >= 0) & (n < NCMP) & (CMP_STRIDE * n + CMP_BLOCK - 1 <= i * P + q)
        m[:, M_CMP + i * P:M_CMP + (i + 1) * P] = np.where(sees, 0.0, NEG)
    aq = np.zeros((HEADS, AR, T), np.float32)
    tok = np.arange(T)
    for h in range(HEADS):
        slope = 2.0 ** (-8.0 * (h + 1) / HEADS)
        aq[h, 0] = slope
        aq[h, 1] = -slope * (tok % P)
        for j in range(TT):
            aq[h, 2 + j] = P * slope * (j - tok // P)
    aq = aq.reshape(KV, GROUP, AR, TT, P).transpose(0, 2, 3, 1, 4).reshape(KV, AR, GROUP * T)
    ak = np.zeros((AR + MR, P + 2 * T), np.float32)
    pos = np.concatenate([CMP_STRIDE * np.arange(NCMP) + CMP_BLOCK - 1, [-1], tok, tok])
    seen, s = pos >= 0, np.maximum(pos, 0)
    ak[0, P - CW:] = seen * (s % P)
    ak[1, P - CW:] = seen
    for j in range(TT):
        ak[2 + j, P - CW:] = seen & (s // P == j)
    for br, cols in enumerate((slice(P, P + T), slice(P + T, P + 2 * T), slice(0, P))):
        ak[[AR + br, AR + 3 + br], cols] = 1.0
    return consts, m, aq, ak


def kernel(x, norm_mix_g, w_in, pos_ck, w_ck1, w_ck2, pos_cv, w_cv1, w_cv2, conv_mix_w, norm_out_attn_g,
           norm_out_conv_g, w_out, norm_ffn_g, w_gate, w_up, ffn_conv_w, ffn_conv_b, w_down, norm_final_g):
    import concourse.bacc as bacc
    from concourse.bass_utils import run_bass_kernel_spmd

    A = np.ascontiguousarray
    w_in, w_out, w_gate, w_up, w_down = (np.asarray(a)[0] for a in (w_in, w_out, w_gate, w_up, w_down))
    padded = np.concatenate([w_in, np.zeros((D, 1), np.float32)], axis=1)
    units = [_blocks(padded[:, c]) for c in _unit_columns()]
    units += [_blocks(w_out[:, d * P:(d + 1) * P]) for d in range(N_OUT)]
    for pr in range(FT // 2 + 1):
        if pr < FT // 2:
            for f in (2 * pr, 2 * pr + 1):
                units += [_blocks(w_gate[:, f * P:(f + 1) * P]), _blocks(w_up[:, f * P:(f + 1) * P])]
        if pr:
            units += [w_down[f * P:(f + 1) * P] for f in (2 * pr - 2, 2 * pr - 1)]
    cols = lambda a, n: np.asarray(a).reshape(n, P).T
    taps = lambda a, n: np.asarray(a)[0].reshape(3, n, P).transpose(2, 1, 0).reshape(P, 3 * n)
    params = np.concatenate([cols(norm_mix_g, 8), cols(norm_out_attn_g, 4), cols(norm_out_conv_g, 4),
                             cols(norm_ffn_g, 8), cols(norm_final_g, 8), taps(conv_mix_w, CONV_T), taps(ffn_conv_w, FT),
                             cols(ffn_conv_b, FT), cols(pos_ck, 16), cols(pos_cv, 16)], axis=1)
    first = lambda a: np.asarray(a)[0].reshape(16, P, P).transpose(1, 0, 2).reshape(P, 2, 1024)
    consts, masks, aq, ak = _shape_constants()
    arrays = {
        "xT": A(np.asarray(x)[0].T.reshape(KT, P, T)),
        "w_units": A(np.stack(units)),
        "w_cmp1": A(np.concatenate([first(w_ck1), first(w_cv1)], axis=1)),
        "w_cmp2": A(np.stack([np.asarray(w_ck2)[0], np.asarray(w_cv2)[0]], axis=1)),
        "params": A(params), "consts": consts, "masks": masks, "alibi_q": A(aq), "alibi_k": ak,
    }
    nc = bacc.Bacc("TRN2", target_bir_lowering=False, num_devices=1)
    args = [nc.dram_tensor("in_" + n, a.shape, mybir.dt.from_np(a.dtype), kind="ExternalInput").ap() for n, a in arrays.items()]
    args.append(nc.dram_tensor("outT", (KT, P, T), F32, kind="ExternalOutput").ap())
    hybrid_layer(nc, *args)
    r = run_bass_kernel_spmd(nc, [{"in_" + n: a for n, a in arrays.items()}], core_ids=[0])
    return A(r.results[0]["outT"].reshape(D, T).T).reshape(1, T, D)
```
